# Optimizing a Trainium2 kernel written in Bass

```python
import jax, jax.numpy as jnp
from jax import lax
import numpy as np
import math

D_MODEL = 1024
BATCH = 1
SEQ = 256
DEPTH = 1

CHUNK = 64
D_MIX = D_MODEL
CONV_WIDTH = D_MIX // 2
CONV_GROUPS = 8
CONV_K = 3
HGRN_WIDTH = D_MIX - CONV_WIDTH
HGRN_HEADS = 4
HGRN_DK = HGRN_WIDTH // HGRN_HEADS
HGRN_DV = HGRN_WIDTH // HGRN_HEADS
N_PROJ_SLOTS = 7
PROJ_WIDTH = 3 * CONV_WIDTH + 4 * HGRN_WIDTH
MEM_LEN = 256
XATTN_HEADS = 4
XATTN_HEAD_DIM = D_MODEL // XATTN_HEADS
N_GROUPS = 4
EXPERTS_PER_GROUP = 4
N_EXPERTS = N_GROUPS * EXPERTS_PER_GROUP
TOPK_IN_GROUP = 2
D_EXPERT = D_MODEL // 2
EPS = 1e-6


def rms_norm(x, g):
    xf = x.astype(jnp.float32)
    y = xf * lax.rsqrt(jnp.mean(xf * xf, axis=-1, keepdims=True) + EPS)
    return (y * g.astype(jnp.float32)).astype(x.dtype)

def hgrn2_chunkwise(q, k, v, log_f):
    bsz, seq, heads, dk = q.shape
    dv = v.shape[-1]
    n_chunks = seq // CHUNK

    def to_chunks(t):
        return t.reshape(bsz, n_chunks, CHUNK, heads, t.shape[-1]).transpose(1, 0, 3, 2, 4)

    tri = jnp.tril(jnp.ones((CHUNK, CHUNK), dtype=bool))

    def step(state, inp):
        qc, kc, vc, ac = inp
        b = jnp.cumsum(ac, axis=2)
        diff = b[:, :, :, None, :] - b[:, :, None, :, :]
        decay = jnp.exp(jnp.where(tri[None, None, :, :, None], diff, -jnp.inf))
        scores = jnp.einsum('bhtsk,bhsk->bhts', qc[:, :, :, None, :] * decay, kc)
        o = (jnp.einsum('bhts,bhsv->bhtv', scores, vc)
             + jnp.einsum('bhtk,bhkv->bhtv', qc * jnp.exp(b), state))
        b_last = b[:, :, -1:, :]
        state = (jnp.exp(b_last[:, :, 0, :])[..., None] * state
                 + jnp.einsum('bhsk,bhsv->bhkv', kc * jnp.exp(b_last - b), vc))
        return state, o

    s0 = jnp.zeros((bsz, heads, dk, dv), jnp.float32)
    _, o = lax.scan(step, s0, (to_chunks(q), to_chunks(k), to_chunks(v), to_chunks(log_f)))
    return o.transpose(1, 0, 3, 2, 4).reshape(bsz, seq, heads, dv)

def parallel_mixer(h, w_in, conv_w, lb, hgrn_norm, w_out):
    bsz, seq, _ = h.shape
    proj = jnp.einsum('bsd,dp->bsp', h, w_in)
    cb, cc, cx, hq, hf, hi, hg = jnp.split(proj, N_PROJ_SLOTS, axis=-1)
    u = jnp.pad(cc * cx, ((0, 0), (CONV_K - 1, 0), (0, 0)))
    conv = sum(u[:, j:j + seq] * conv_w[j] for j in range(CONV_K))
    y_a = cb * conv
    z = hf.astype(jnp.float32).reshape(bsz, seq, HGRN_HEADS, HGRN_DK)
    lbh = lb.astype(jnp.float32).reshape(HGRN_HEADS, HGRN_DK)
    log_f = jnp.log(lbh + (1.0 - lbh) * jax.nn.sigmoid(z))
    k = (1.0 - lbh) * jax.nn.sigmoid(-z)
    q = hq.astype(jnp.float32).reshape(bsz, seq, HGRN_HEADS, HGRN_DK)
    v = hi.astype(jnp.float32).reshape(bsz, seq, HGRN_HEADS, HGRN_DV)
    o = hgrn2_chunkwise(q, k, v, log_f)
    o = o * lax.rsqrt(jnp.mean(o * o, axis=-1, keepdims=True) + EPS)
    o = o * hgrn_norm.astype(jnp.float32).reshape(HGRN_HEADS, HGRN_DV)
    g = hg.astype(jnp.float32).reshape(bsz, seq, HGRN_HEADS, HGRN_DV)
    y_b = (o * jax.nn.silu(g)).reshape(bsz, seq, HGRN_WIDTH).astype(h.dtype)
    y = jnp.concatenate([y_a, y_b], axis=-1)
    return jnp.einsum('bsm,md->bsd', y, w_out)

def memory_cross_attention(h, m, w_q, w_kv, w_o):
    bsz, seq, _ = h.shape
    q = jnp.einsum('bsd,de->bse', h, w_q).reshape(bsz, seq, XATTN_HEADS, XATTN_HEAD_DIM)
    kv = jnp.einsum('bmd,de->bme', m, w_kv)
    k, v = jnp.split(kv, 2, axis=-1)
    k = k.reshape(bsz, m.shape[1], XATTN_HEADS, XATTN_HEAD_DIM)
    v = v.reshape(bsz, m.shape[1], XATTN_HEADS, XATTN_HEAD_DIM)
    s = jnp.einsum('bshd,bmhd->bhsm', q, k).astype(jnp.float32) * (XATTN_HEAD_DIM ** -0.5)
    p = jax.nn.softmax(s, axis=-1).astype(v.dtype)
    o = jnp.einsum('bhsm,bmhd->bshd', p, v).reshape(bsz, seq, D_MODEL)
    return jnp.einsum('bse,ed->bsd', o, w_o)

def hierarchical_moe(h, w_group, b_group, w_expert, b_expert, w_gate, w_up, w_down):
    bsz, seq, d = h.shape
    t = h.reshape(-1, d)
    g_prob = jax.nn.softmax((t @ w_group + b_group).astype(jnp.float32), axis=-1)
    g_p, g_idx = lax.top_k(g_prob, 1)
    e_logits = (t @ w_expert + b_expert).astype(jnp.float32).reshape(-1, N_GROUPS, EXPERTS_PER_GROUP)
    e_logits = jnp.take_along_axis(e_logits, g_idx[:, :, None], axis=1)[:, 0]
    e_prob = jax.nn.softmax(e_logits, axis=-1)
    e_p, e_idx = lax.top_k(e_prob, TOPK_IN_GROUP)
    weights = g_p * e_p / jnp.sum(e_p, axis=-1, keepdims=True)
    expert_id = g_idx * EXPERTS_PER_GROUP + e_idx
    combine = jnp.sum(jax.nn.one_hot(expert_id, N_EXPERTS, dtype=jnp.float32) * weights[..., None], axis=1)
    out = jnp.zeros(t.shape, jnp.float32)
    for e in range(N_EXPERTS):
        hid = jax.nn.silu(t @ w_gate[e]) * (t @ w_up[e])
        out = out + combine[:, e:e + 1] * (hid @ w_down[e])
    return out.astype(h.dtype).reshape(bsz, seq, d)

def first_inputs(seed: int = 0) -> dict:
    key = jax.random.key(seed)
    ks = jax.random.split(key, 24)
    f32 = jnp.float32

    def nrm(k, shape, scale):
        return jax.random.normal(k, shape, f32) * scale

    def gain(k, shape):
        return 1.0 + 0.02 * jax.random.normal(k, shape, f32)

    return {
        "x": jax.random.normal(ks[0], (BATCH, SEQ, D_MODEL), f32),
        "mem": jax.random.normal(ks[1], (BATCH, MEM_LEN, D_MODEL), f32),
        "mix_norm": gain(ks[2], (DEPTH, D_MODEL)),
        "w_in": nrm(ks[3], (DEPTH, D_MODEL, PROJ_WIDTH), D_MODEL ** -0.5),
        "conv_w": nrm(ks[4], (DEPTH, CONV_K, CONV_WIDTH), CONV_K ** -0.5),
        "hgrn_lb": jax.random.normal(ks[5], (DEPTH + 1, HGRN_WIDTH), f32),
        "hgrn_norm": gain(ks[6], (DEPTH, HGRN_WIDTH)),
        "w_out": nrm(ks[7], (DEPTH, D_MIX, D_MODEL), D_MIX ** -0.5),
        "xattn_norm": gain(ks[8], (DEPTH, D_MODEL)),
        "mem_norm": gain(ks[9], (DEPTH, D_MODEL)),
        "w_q": nrm(ks[10], (DEPTH, D_MODEL, D_MODEL), D_MODEL ** -0.5),
        "w_kv": nrm(ks[11], (DEPTH, D_MODEL, 2 * D_MODEL), D_MODEL ** -0.5),
        "w_o": nrm(ks[12], (DEPTH, D_MODEL, D_MODEL), D_MODEL ** -0.5),
        "ffn_norm": gain(ks[13], (DEPTH, D_MODEL)),
        "w_group": nrm(ks[14], (DEPTH, D_MODEL, N_GROUPS), D_MODEL ** -0.5),
        "b_group": nrm(ks[15], (DEPTH, N_GROUPS), 0.01),
        "w_expert": nrm(ks[16], (DEPTH, D_MODEL, N_EXPERTS), D_MODEL ** -0.5),
        "b_expert": nrm(ks[17], (DEPTH, N_EXPERTS), 0.01),
        "w_gate": nrm(ks[18], (DEPTH, N_EXPERTS, D_MODEL, D_EXPERT), D_MODEL ** -0.5),
        "w_up": nrm(ks[19], (DEPTH, N_EXPERTS, D_MODEL, D_EXPERT), D_MODEL ** -0.5),
        "w_down": nrm(ks[20], (DEPTH, N_EXPERTS, D_EXPERT, D_MODEL), D_EXPERT ** -0.5),
        "final_norm": gain(ks[21], (D_MODEL,)),
    }

def first_block(x, mem, mix_norm, w_in, conv_w, hgrn_lb, hgrn_norm, w_out,
              xattn_norm, mem_norm, w_q, w_kv, w_o,
              ffn_norm, w_group, b_group, w_expert, b_expert, w_gate, w_up, w_down,
              final_norm):
    lb_all = jnp.cumsum(jax.nn.softmax(hgrn_lb.astype(jnp.float32), axis=0), axis=0)
    for l in range(DEPTH):
        x = x + parallel_mixer(rms_norm(x, mix_norm[l]), w_in[l], conv_w[l], lb_all[l],
                               hgrn_norm[l], w_out[l])
        x = x + memory_cross_attention(rms_norm(x, xattn_norm[l]), rms_norm(mem, mem_norm[l]),
                                       w_q[l], w_kv[l], w_o[l])
        x = x + hierarchical_moe(rms_norm(x, ffn_norm[l]), w_group[l], b_group[l], w_expert[l],
                                 b_expert[l], w_gate[l], w_up[l], w_down[l])
    return rms_norm(x, final_norm)


DEPTH_2 = 2

GRID_W = 64
CTX_LEN = 256
HEAD_DIM = 64
ROPE_BASE = 10000.0
NEG_INF = -1e30
Q_BLOCK = 128

NA_HEADS = 8
NA_WIN_R = 8
NA_WIN_C = 16
NA_QCB = 16
NA_KCB = 32
NA_WIDTH = NA_HEADS * HEAD_DIM
NA_SCALE = HEAD_DIM ** -0.5

MLA_HEADS = 8
MLA_Q_LORA = 384
MLA_KV_LORA = 256
MLA_NOPE = 64
MLA_ROPE = 32
MLA_V = 64
MLA_QK = MLA_NOPE + MLA_ROPE
MLA_WIDTH = MLA_HEADS * MLA_V
MLA_SCALE = MLA_QK ** -0.5

DIFF_HEADS = 4
DIFF_D = 64
DIFF_V = 2 * DIFF_D
DIFF_QK_WIDTH = DIFF_HEADS * 2 * DIFF_D
DIFF_WIDTH = DIFF_HEADS * DIFF_V
DIFF_SCALE = DIFF_D ** -0.5

N_BRANCH = 3
BRANCH_WIDTH = 512

IN_SPLITS = (NA_WIDTH, NA_WIDTH, NA_WIDTH,
             MLA_Q_LORA, MLA_KV_LORA, MLA_ROPE,
             DIFF_QK_WIDTH, DIFF_QK_WIDTH, DIFF_WIDTH,
             N_BRANCH * BRANCH_WIDTH, N_BRANCH * D_MODEL)
D_IN = sum(IN_SPLITS)


def rms_norm_2(x, g):
    xf = x.astype(jnp.float32)
    y = xf * lax.rsqrt(jnp.mean(xf * xf, axis=-1, keepdims=True) + EPS)
    return (y * g.astype(jnp.float32)).astype(x.dtype)

def axial_rope_tables(n_tokens, rot_dim):
    t = jnp.arange(n_tokens, dtype=jnp.int32)
    row = (t // GRID_W).astype(jnp.float32)
    col = (t % GRID_W).astype(jnp.float32)
    n_freq = rot_dim // 4
    inv = ROPE_BASE ** (-jnp.arange(n_freq, dtype=jnp.float32) / n_freq)
    ang = jnp.concatenate([row[:, None] * inv, col[:, None] * inv], axis=-1)
    return jnp.cos(ang), jnp.sin(ang)

def apply_rope(x, cos, sin):
    half = x.shape[-1] // 2
    shape = (cos.shape[0],) + (1,) * (x.ndim - 3) + (half,)
    cs = cos.reshape(shape).astype(x.dtype)
    sn = sin.reshape(shape).astype(x.dtype)
    x1, x2 = x[..., :half], x[..., half:]
    return jnp.concatenate([x1 * cs - x2 * sn, x2 * cs + x1 * sn], axis=-1)

def rope_tail(x, cos, sin, n_rot):
    return jnp.concatenate([x[..., :-n_rot], apply_rope(x[..., -n_rot:], cos, sin)], axis=-1)

def softmax_attend(q, k, v, scale):
    s = jnp.einsum('bqhd,bkhd->bhqk', q, k).astype(jnp.float32) * scale
    p = jax.nn.softmax(s, axis=-1).astype(v.dtype)
    return jnp.einsum('bhqk,bkhv->bqhv', p, v)

def diff_attend(q, k, v, lam, scale):
    s = jnp.einsum('bqhmd,bkhmd->bhmqk', q, k).astype(jnp.float32) * scale
    p = jax.nn.softmax(s, axis=-1)
    a = (p[:, :, 0] - lam * p[:, :, 1]).astype(v.dtype)
    return jnp.einsum('bhqk,bkhv->bqhv', a, v)

def blocked_queries(fn, q):
    B, T = q.shape[0], q.shape[1]
    nb = T // Q_BLOCK
    qb = jnp.moveaxis(q.reshape((B, nb, Q_BLOCK) + q.shape[2:]), 1, 0)
    out = lax.map(fn, qb)
    out = jnp.moveaxis(out, 0, 1)
    return out.reshape((B, T) + out.shape[3:])

def neighbourhood_attend(q, k, v, k_ctx, v_ctx, rpb):
    B, T, H, d = q.shape
    L = k_ctx.shape[1]
    rows = T // GRID_W
    kr = min(NA_WIN_R, rows)
    ncb = GRID_W // NA_QCB
    qcol = np.arange(GRID_W).reshape(ncb, NA_QCB)
    cstart = np.clip(qcol - NA_WIN_C // 2, 0, GRID_W - NA_WIN_C)
    band0 = np.clip(np.arange(ncb) * NA_QCB - NA_WIN_C // 2, 0, GRID_W - NA_KCB)
    kcol = band0[:, None] + np.arange(NA_KCB)
    kcol_f = np.tile(kcol, (1, kr))
    krow = np.repeat(np.arange(kr), NA_KCB)
    col_in = jnp.asarray((kcol_f[:, None, :] >= cstart[:, :, None])
                         & (kcol_f[:, None, :] < cstart[:, :, None] + NA_WIN_C))
    dc_idx = np.clip(kcol_f[:, None, :] - qcol[:, :, None], -(NA_WIN_C - 1), NA_WIN_C - 1) + (NA_WIN_C - 1)
    nk = kr * NA_KCB
    qg = q.reshape(B, rows, ncb, NA_QCB, H, d)
    kg = k.reshape(B, rows, GRID_W, H, d)
    vg = v.reshape(B, rows, GRID_W, H, d)

    def row_fn(r):
        rs = jnp.clip(r - kr // 2, 0, rows - kr)
        kb = lax.dynamic_slice_in_dim(kg, rs, kr, axis=1)[:, :, kcol]
        vb = lax.dynamic_slice_in_dim(vg, rs, kr, axis=1)[:, :, kcol]
        kb = kb.transpose(0, 2, 1, 3, 4, 5).reshape(B, ncb, nk, H, d)
        vb = vb.transpose(0, 2, 1, 3, 4, 5).reshape(B, ncb, nk, H, d)
        qr = lax.dynamic_index_in_dim(qg, r, axis=1, keepdims=False)
        dr = rs + krow - r + (NA_WIN_R - 1)
        bias = rpb[:, dr[None, None, :], dc_idx].astype(jnp.float32)
        s_lat = jnp.einsum('bnqhd,bnkhd->bhnqk', qr, kb).astype(jnp.float32) * NA_SCALE + bias
        s_lat = jnp.where(col_in, s_lat, NEG_INF)
        s_ctx = jnp.einsum('bnqhd,bkhd->bhnqk', qr, k_ctx).astype(jnp.float32) * NA_SCALE
        p = jax.nn.softmax(jnp.concatenate([s_ctx, s_lat], axis=-1), axis=-1).astype(v.dtype)
        return (jnp.einsum('bhnqk,bkhd->bnqhd', p[..., :L], v_ctx)
                + jnp.einsum('bhnqk,bnkhd->bnqhd', p[..., L:], vb))

    out = lax.map(row_fn, jnp.arange(rows))
    return out.transpose(1, 0, 2, 3, 4, 5).reshape(B, T, H * d)

def mixer_inputs(h, w_in_l, na_q_g, na_k_g, mla_cq_g, mla_ckv_g, w_uq_l, w_ukv_l,
                 mla_q_g, mla_k_g, diff_q_g, diff_k_g):
    lead = h.shape[:-1]
    split_points = [int(s) for s in np.cumsum(IN_SPLITS)[:-1]]
    (na_q, na_k, na_v, cq, ckv, k_rope, dq, dk, dv, z, gm) = jnp.split(h @ w_in_l, split_points, axis=-1)
    na_q = rms_norm_2(na_q.reshape(lead + (NA_HEADS, HEAD_DIM)), na_q_g)
    na_k = rms_norm_2(na_k.reshape(lead + (NA_HEADS, HEAD_DIM)), na_k_g)
    na_v = na_v.reshape(lead + (NA_HEADS, HEAD_DIM))
    mq = (rms_norm_2(cq, mla_cq_g) @ w_uq_l).reshape(lead + (MLA_HEADS, MLA_QK))
    kv = (rms_norm_2(ckv, mla_ckv_g) @ w_ukv_l).reshape(lead + (MLA_HEADS, MLA_NOPE + MLA_V))
    k_nope, mv = kv[..., :MLA_NOPE], kv[..., MLA_NOPE:]
    k_r = jnp.broadcast_to(k_rope[..., None, :], lead + (MLA_HEADS, MLA_ROPE))
    mk = rms_norm_2(jnp.concatenate([k_nope, k_r], axis=-1), mla_k_g)
    mq = rms_norm_2(mq, mla_q_g)
    dq = rms_norm_2(dq.reshape(lead + (DIFF_HEADS, 2, DIFF_D)), diff_q_g)
    dk = rms_norm_2(dk.reshape(lead + (DIFF_HEADS, 2, DIFF_D)), diff_k_g)
    dv = dv.reshape(lead + (DIFF_HEADS, DIFF_V))
    return (na_q, na_k, na_v, mq, mk, mv, dq, dk, dv, z, gm)

def diff_finish(o, subln_g, lam_init):
    o = rms_norm_2(o, subln_g) * (1.0 - lam_init)
    return o.reshape(o.shape[:-2] + (DIFF_WIDTH,))

def merge_branches(o_na, o_mla, o_diff, z, gm, w_br_l, w_out_l):
    z_na, z_mla, z_diff = jnp.split(z, N_BRANCH, axis=-1)
    g_na, g_mla, g_diff = jnp.split(gm, N_BRANCH, axis=-1)
    y = (jax.nn.sigmoid(g_na) * ((o_na * jax.nn.silu(z_na)) @ w_br_l[0])
         + jax.nn.sigmoid(g_mla) * ((o_mla * jax.nn.silu(z_mla)) @ w_br_l[1])
         + jax.nn.sigmoid(g_diff) * ((o_diff * jax.nn.silu(z_diff)) @ w_br_l[2]))
    return y @ w_out_l

def second_inputs(seed: int = 0) -> dict:
    key = jax.random.key(seed)
    ks = jax.random.split(key, 26)
    f32 = jnp.float32

    def nrm(k, shape, s):
        return jax.random.normal(k, shape, f32) * s

    def gain(k, shape):
        return 1.0 + 0.05 * jax.random.normal(k, shape, f32)

    D = D_MODEL
    return {
        'x': nrm(ks[0], (BATCH, SEQ, D), 1.0),
        'c': nrm(ks[1], (BATCH, D), 1.0),
        'ctx': nrm(ks[2], (BATCH, CTX_LEN, D), 1.0),
        'c_ctx': nrm(ks[3], (D,), 1.0),
        'norm_g': gain(ks[4], (DEPTH_2, D)),
        'w_ada': nrm(ks[5], (DEPTH_2, D, 3 * D), D ** -0.5),
        'b_ada': nrm(ks[6], (DEPTH_2, 3 * D), 0.02),
        'w_in': nrm(ks[7], (DEPTH_2, D, D_IN), D ** -0.5),
        'na_rpb': nrm(ks[8], (DEPTH_2, NA_HEADS, 2 * NA_WIN_R - 1, 2 * NA_WIN_C - 1), 0.1),
        'na_q_g': gain(ks[9], (DEPTH_2, HEAD_DIM)),
        'na_k_g': gain(ks[10], (DEPTH_2, HEAD_DIM)),
        'mla_cq_g': gain(ks[11], (DEPTH_2, MLA_Q_LORA)),
        'mla_ckv_g': gain(ks[12], (DEPTH_2, MLA_KV_LORA)),
        'w_uq': nrm(ks[13], (DEPTH_2, MLA_Q_LORA, MLA_HEADS * MLA_QK), MLA_Q_LORA ** -0.5),
        'w_ukv': nrm(ks[14], (DEPTH_2, MLA_KV_LORA, MLA_HEADS * (MLA_NOPE + MLA_V)), MLA_KV_LORA ** -0.5),
        'mla_q_g': gain(ks[15], (DEPTH_2, MLA_QK)),
        'mla_k_g': gain(ks[16], (DEPTH_2, MLA_QK)),
        'diff_q_g': gain(ks[17], (DEPTH_2, DIFF_D)),
        'diff_k_g': gain(ks[18], (DEPTH_2, DIFF_D)),
        'diff_lq1': nrm(ks[19], (DEPTH_2, DIFF_D), 0.1),
        'diff_lk1': nrm(ks[20], (DEPTH_2, DIFF_D), 0.1),
        'diff_lq2': nrm(ks[21], (DEPTH_2, DIFF_D), 0.1),
        'diff_lk2': nrm(ks[22], (DEPTH_2, DIFF_D), 0.1),
        'diff_subln_g': gain(ks[23], (DEPTH_2, DIFF_V)),
        'w_br': nrm(ks[24], (DEPTH_2, N_BRANCH, BRANCH_WIDTH, D), BRANCH_WIDTH ** -0.5),
        'w_out': nrm(ks[25], (DEPTH_2, D, D), D ** -0.5),
    }

def second_block(x, c, ctx, c_ctx, norm_g, w_ada, b_ada, w_in, na_rpb, na_q_g, na_k_g,
              mla_cq_g, mla_ckv_g, w_uq, w_ukv, mla_q_g, mla_k_g, diff_q_g, diff_k_g,
              diff_lq1, diff_lk1, diff_lq2, diff_lk2, diff_subln_g, w_br, w_out):
    B, T, _ = x.shape
    f32 = jnp.float32
    cos_m, sin_m = axial_rope_tables(T, MLA_ROPE)
    cos_d, sin_d = axial_rope_tables(T, DIFF_D)
    for l in range(DEPTH_2):
        last = l == DEPTH_2 - 1
        lam_init = 0.8 - 0.6 * math.exp(-0.3 * l)
        lam = (jnp.exp(jnp.sum(diff_lq1[l].astype(f32) * diff_lk1[l].astype(f32)))
               - jnp.exp(jnp.sum(diff_lq2[l].astype(f32) * diff_lk2[l].astype(f32))) + lam_init)
        shift, scale, gate = jnp.split(jax.nn.silu(c) @ w_ada[l] + b_ada[l], 3, axis=-1)
        shift_c, scale_c, gate_c = jnp.split(jax.nn.silu(c_ctx) @ w_ada[l] + b_ada[l], 3, axis=-1)
        h = rms_norm_2(x, norm_g[l]) * (1.0 + scale[:, None]) + shift[:, None]
        hc = rms_norm_2(ctx, norm_g[l]) * (1.0 + scale_c) + shift_c
        params = (w_in[l], na_q_g[l], na_k_g[l], mla_cq_g[l], mla_ckv_g[l], w_uq[l], w_ukv[l],
                  mla_q_g[l], mla_k_g[l], diff_q_g[l], diff_k_g[l])
        (na_q, na_k, na_v, m_q, m_k, m_v, d_q, d_k, d_v, z, gm) = mixer_inputs(h, *params)
        (cna_q, cna_k, cna_v, cm_q, cm_k, cm_v, cd_q, cd_k, cd_v, cz, cgm) = mixer_inputs(hc, *params)
        m_q = rope_tail(m_q, cos_m, sin_m, MLA_ROPE)
        m_k = rope_tail(m_k, cos_m, sin_m, MLA_ROPE)
        d_q = apply_rope(d_q, cos_d, sin_d)
        d_k = apply_rope(d_k, cos_d, sin_d)
        m_k_all = jnp.concatenate([cm_k, m_k], axis=1)
        m_v_all = jnp.concatenate([cm_v, m_v], axis=1)
        d_k_all = jnp.concatenate([cd_k, d_k], axis=1)
        d_v_all = jnp.concatenate([cd_v, d_v], axis=1)
        o_na = neighbourhood_attend(na_q, na_k, na_v, cna_k, cna_v, na_rpb[l])
        o_mla = blocked_queries(lambda qb: softmax_attend(qb, m_k_all, m_v_all, MLA_SCALE), m_q)
        o_mla = o_mla.reshape(B, T, MLA_WIDTH)
        o_diff = blocked_queries(lambda qb: diff_attend(qb, d_k_all, d_v_all, lam, DIFF_SCALE), d_q)
        o_diff = diff_finish(o_diff, diff_subln_g[l], lam_init)
        x_new = x + gate[:, None] * merge_branches(o_na, o_mla, o_diff, z, gm, w_br[l], w_out[l])
        if not last:
            co_na = softmax_attend(cna_q, cna_k, cna_v, NA_SCALE).reshape(B, -1, NA_WIDTH)
            co_mla = softmax_attend(cm_q, cm_k, cm_v, MLA_SCALE).reshape(B, -1, MLA_WIDTH)
            co_diff = diff_finish(diff_attend(cd_q, cd_k, cd_v, lam, DIFF_SCALE), diff_subln_g[l], lam_init)
            ctx = ctx + gate_c * merge_branches(co_na, co_mla, co_diff, cz, cgm, w_br[l], w_out[l])
        x = x_new
    return x


def setup_inputs(seed=0):
    out = dict(first_inputs(seed))
    for name, value in second_inputs(seed + 1).items():
        if name != "x":
            out[name + "_2"] = value
    return out


def reference(
    x, mem, mix_norm, w_in, conv_w, hgrn_lb, hgrn_norm, w_out, xattn_norm, mem_norm, w_q, w_kv,
    w_o, ffn_norm, w_group, b_group, w_expert, b_expert, w_gate, w_up, w_down, final_norm, c_2,
    ctx_2, c_ctx_2, norm_g_2, w_ada_2, b_ada_2, w_in_2, na_rpb_2, na_q_g_2, na_k_g_2,
    mla_cq_g_2, mla_ckv_g_2, w_uq_2, w_ukv_2, mla_q_g_2, mla_k_g_2, diff_q_g_2, diff_k_g_2,
    diff_lq1_2, diff_lk1_2, diff_lq2_2, diff_lk2_2, diff_subln_g_2, w_br_2, w_out_2,
):
    x = first_block(
        x, mem, mix_norm, w_in, conv_w, hgrn_lb, hgrn_norm, w_out, xattn_norm, mem_norm, w_q,
        w_kv, w_o, ffn_norm, w_group, b_group, w_expert, b_expert, w_gate, w_up, w_down,
        final_norm,
    )
    return second_block(
        x, c_2, ctx_2, c_ctx_2, norm_g_2, w_ada_2, b_ada_2, w_in_2, na_rpb_2, na_q_g_2,
        na_k_g_2, mla_cq_g_2, mla_ckv_g_2, w_uq_2, w_ukv_2, mla_q_g_2, mla_k_g_2, diff_q_g_2,
        diff_k_g_2, diff_lq1_2, diff_lk1_2, diff_lq2_2, diff_lk2_2, diff_subln_g_2, w_br_2,
        w_out_2,
    )


_drawn_inputs = setup_inputs


def setup_inputs(seed=0):
    import zlib

    import numpy as np

    out = dict(_drawn_inputs(seed))
    spreads = {}
    factors = {'hgrn_norm': 3.447,
     'xattn_norm': 8.0,
     'mem_norm': 8.0,
     'b_group': 8.0,
     'b_expert': 8.0,
     'final_norm': 2.722,
     'norm_g_2': 2.725,
     'na_rpb_2': 8.0,
     'na_q_g_2': 8.0,
     'na_k_g_2': 8.0,
     'mla_cq_g_2': 8.0,
     'mla_ckv_g_2': 7.041,
     'mla_q_g_2': 8.0,
     'mla_k_g_2': 8.0,
     'diff_q_g_2': 8.0,
     'diff_k_g_2': 8.0,
     'diff_lk1_2': 5.16,
     'diff_lq2_2': 8.0,
     'diff_lk2_2': 3.119,
     'diff_subln_g_2': 3.832}
    for name, (base, spread) in spreads.items():
        noise = np.random.default_rng([zlib.crc32(name.encode()), seed]).standard_normal(out[name].shape)
        drawn = base * np.exp(spread * noise) if base else spread * noise
        out[name] = __import__('jax').numpy.asarray(drawn.astype(out[name].dtype))
    for name, factor in factors.items():
        out[name] = (out[name] * factor).astype(out[name].dtype)
    return out
```

```python
from contextlib import ExitStack
import math

import concourse.bass as bass
from concourse import mybir

F32 = mybir.dt.float32
U32 = mybir.dt.uint32
ALU = mybir.AluOpType
ACT = mybir.ActivationFunctionType
X_AXIS = mybir.AxisListType.X

P = 128
D = 1024
KT_D = D // P
TOK = 256
TT = TOK // P
EPS = 1e-6
N_EXPERTS = 16
SLOT = KT_D * 512
RING = 4
CAP = 64
MOE_RING = 6
HEADS1 = 4
LEVELS = [128, 64, 32, 16, 8, 4, 2, 1]
LAYERS = 2
UNITS = 8
C_NAQ, C_NAK, C_NAV, C_CQ, C_CKV = 0, 512, 1024, 1536, 1920
C_DQ, C_DK, C_DV, C_Z, C_GM = 2208, 2720, 3232, 3744, 5280
QK_DIM = {"na": 64, "mla": 96, "diff": 64}
V_DIM = {"na": 64, "mla": 64, "diff": 128}
BRANCHES = ["na", "mla", "diff"]
ROPE = {"mla": 32, "diff": 64}

COLS = {}
_at = 0
for _name, _n in [("mix_norm", 8), ("xattn_norm", 8), ("mem_norm", 8), ("ffn_norm", 8), ("conv_w", 12),
                  ("hgrn_lb", 8), ("hgrn_norm", 4), ("norm_g_2", 16), ("mla_cq_g_2", 6), ("mla_ckv_g_2", 4),
                  ("b_ada_2", 48), ("c_2", 8), ("c_ctx_2", 8)]:
    COLS[_name] = _at
    _at += _n
N_COLS = _at
ROWV = {}
_at = 0
for _name, _n in [("na_q_g_2", 64), ("na_k_g_2", 64), ("mla_q_g_2", 96), ("mla_k_g_2", 96), ("diff_q_g_2", 64),
                  ("diff_k_g_2", 64), ("diff_subln_g_2", 128), ("diff_lq1_2", 64), ("diff_lk1_2", 64),
                  ("diff_lq2_2", 64), ("diff_lk2_2", 64)]:
    ROWV[_name] = (_at, _n)
    _at += _n
N_ROWV = _at
CONST = {}
_at = 0
for _name, _n in [("ident", 128), ("reverse", 128), ("colmask", 64), ("cos_diff", 64), ("sin_diff", 64), ("cos_mla", 32),
                  ("sin_mla", 32), ("rank", 4), ("before", 128), ("iota", 64)]:
    CONST[_name] = (_at, _n)
    _at += _n
N_CONST = _at


class Program:
    pass


class Signal:

    def __init__(self, sem, name, book):
        self.sem, self.name, self.count, self.book = sem, name, 0, book

    def step(self, *key):
        self.count += 1
        self.book["now"][(self.name, key)] = self.count
        return 1

    def at(self, *key):
        return self.book["before"].get((self.name, key), 1) if self.book["before"] is not None else 1


def read_crowded(engine, k):
    engine.wait_ge(k.crowded_ready.sem, k.crowded_ready.at())
    return engine.value_load(k.crowded[0:1, 0:1], min_val=0, max_val=1)


def weight_chunks(w):
    def cols(ap, c0, n):
        return ap[:, c0:c0 + n].rearrange("(k p) n -> p k n", p=P)

    before, after = [], []
    for part in [4, 3, 5, 6, 1, 2, 0]:
        before.append((("mix", part), cols(w["w_in"][0], 512 * part, 512), ("mix", part, 1)))
    for half in range(2):
        before.append((("mixout", half), cols(w["w_out"][0], 512 * half, 512), ("mixout", half, TT - 1)))
    for n in range(2):
        before.append((("xk", n), cols(w["w_kv"][0], 512 * n, 512), ("xk", n, 1)))
    for n in range(2):
        before.append((("xv", n), cols(w["w_kv"][0], D + 512 * n, 512), ("xv", n, TT - 1)))
    for n in range(2):
        before.append((("xq", n), cols(w["w_q"][0], 512 * n, 512), ("xq", n, 1)))
    for n in range(2):
        before.append((("xo", n), cols(w["w_o"][0], 512 * n, 512), ("xo", n, TT - 1)))
    for l in range(LAYERS):
        win = w["w_in_2"][l]

        def add(key, src, *last):
            after.append((key, src, last))
        for n in range(4):
            add(("ada", l, n), cols(w["w_ada_2"][l], 512 * n, 512), "ada", l, n)
        for b, branch in enumerate(BRANCHES):
            if branch == "mla":
                add(("mla", l, "ckv"), cols(win, C_CKV, 288), "mla", l, "ckv", 3)
                add(("mla", l, "cq"), cols(win, C_CQ, 384), "mla", l, "cq", 3)
                add(("mla", l, "ukv"), cols(w["w_ukv_2"][l], 0, 1024), "mla", l, "ukv", 3, 1)
                add(("mla", l, "uq"), cols(w["w_uq_2"][l], 0, 768), "mla", l, "uq", 3, 1)
            else:
                for part, c0 in zip("kvq", (C_NAK, C_NAV, C_NAQ) if branch == "na" else (C_DK, C_DV, C_DQ)):
                    add((branch, l, part), cols(win, c0, 512), branch, l, part, 3)
            add(("z", l, b), cols(win, C_Z + 512 * b, 512), "z", l, b, 3)
            add(("br", l, b), cols(w["w_br_2"][l, b], 0, 1024), "br", l, b, 1, 3)
            for half in range(2):
                add(("gm", l, b, half), cols(win, C_GM + 1024 * b + 512 * half, 512), "gm", l, b, half, 3)
        for n in range(4, 6):
            add(("ada", l, n), cols(w["w_ada_2"][l], 512 * n, 512), "gate", l, n, "x")
        for half in range(2):
            add(("out", l, half), cols(w["w_out_2"][l], 512 * half, 512), "out", l, half, 3)
    return before, after


def tiles_of(l, what):
    return [0, 1, 2, 3] if l < LAYERS - 1 or what == "kv" else [2, 3]


def attention_units(l):
    return [(t, u) for t in tiles_of(l, "q") for u in range(UNITS)]



def load_program(sp, k):
    w = k.w
    before, after = weight_chunks(w)

    def load(n, chunks, first_waits=None):
        key, src, _ = chunks[n]
        slot = n % RING
        if n >= RING:
            sp.wait_ge(k.gemm_done.sem, k.gemm_done.at(*chunks[n - RING][2]))
        dst = k.pool6[:, slot * SLOT:slot * SLOT + src.shape[1] * src.shape[2]]
        k.loads[slot] += 1
        k.landed[key] = (slot, 16 * k.loads[slot])
        sp.dma_start(dst.rearrange("p (k n) -> p k n", k=src.shape[1]), src).then_inc(k.slot_loaded[slot], 16)

    sp.dma_start(k.x_rows, w["x"][0].rearrange("(t p) d -> p t d", p=P)).then_inc(k.x_loaded, 16)
    sp.dma_start(k.const, w["const"]).then_inc(k.small_loaded, 16)
    sp.dma_start(k.col_rows, w["col_vecs"].rearrange("(t p) d -> p t d", p=P)).then_inc(k.small_loaded, 16)
    load(0, before)
    sp.dma_start(k.masks, w["masks"]).then_inc(k.masks_loaded, 16)
    load(1, before)
    sp.dma_start(k.ctx_rows, w["mem"][0].rearrange("(t p) d -> p t d", p=P)).then_inc(k.mem_loaded, 16)
    sp.dma_start(k.router_w[:, :, 0:4], w["w_group"][0].rearrange("(k p) n -> p k n", p=P)).then_inc(k.router_loaded, 16)
    sp.dma_start(k.router_w[:, :, 4:20], w["w_expert"][0].rearrange("(k p) n -> p k n", p=P)).then_inc(k.router_loaded, 16)
    sp.dma_start(k.router_b[:, 0:4], w["b_group"].partition_broadcast(P)[:, 0, :]).then_inc(k.router_loaded, 16)
    sp.dma_start(k.router_b[:, 4:20], w["b_expert"].partition_broadcast(P)[:, 0, :]).then_inc(k.router_loaded, 16)
    for n in range(2, len(before)):
        load(n, before)

    def expert_src(e, part):
        if part == 2:
            return w["w_down_flat"][bass.ds(e * 512, 512), :].rearrange("(k p) n -> p k n", p=P)
        return [w["w_gate_flat"], w["w_up_flat"]][part][bass.ds(e * D, D), :].rearrange("(k p) n -> p k n", p=P)

    def load_expert(e, j, part):
        slot = 3 * j + part
        kt = 4 if part == 2 else KT_D
        dst = k.pool6[:, slot * SLOT:(slot + 1) * SLOT].rearrange("p (k n) -> p k n", k=kt)
        sp.dma_start(dst, expert_src(e, part)).then_inc(k.slot_loaded[slot], 16)

    for slot in range(MOE_RING):
        if slot < RING:
            held = [n for n in range(len(before)) if n % RING == slot][-1]
            sp.wait_ge(k.gemm_done.sem, k.gemm_done.at(*before[held][2]))
        else:
            sp.wait_ge(k.scores_done.sem, k.scores_done.at("x", TT - 1, HEADS1 - 1))
        load_expert(slot // 3, slot // 3, slot % 3)
    crowded = read_crowded(sp, k)
    with sp.If(crowded == 0):
        with sp.Fori(1, N_EXPERTS // 2) as p:
            for j in range(2):
                sp.wait_ge(k.pair_gate, 2 * p + j - 1)
                load_expert(2 * p + j, j, 0)
                sp.wait_ge(k.pair_up, 2 * p + j - 1)
                load_expert(2 * p + j, j, 1)
            for j in range(2):
                sp.wait_ge(k.pair_down, 2 * p + j - 1)
                load_expert(2 * p + j, j, 2)
        sp.wait_ge(k.pair_down, N_EXPERTS)
    with sp.Else():
        with sp.Fori(1, N_EXPERTS // 2) as i:
            for j in range(2):
                sp.wait_ge(k.moe_gate, 4 * i + 2 * j - 2)
                load_expert(2 * i + j, j, 0)
                sp.wait_ge(k.moe_up, 4 * i + 2 * j - 2)
                load_expert(2 * i + j, j, 1)
                sp.wait_ge(k.moe_down, 8 * i + 4 * j - 4)
                load_expert(2 * i + j, j, 2)
        sp.wait_ge(k.moe_down, 4 * N_EXPERTS)
    k.moe_base = list(k.loads)
    for slot in range(MOE_RING):
        k.loads[slot] += N_EXPERTS // 2

    sp.wait_ge(k.norm_rows.sem, k.norm_rows.at("mem", 1))
    sp.dma_start(k.ctx_rows, w["ctx_2"][0].rearrange("(t p) d -> p t d", p=P)).then_inc(k.ctx_loaded, 16)

    def load_layer_vectors(l):
        sp.dma_start(k.rowv, w["row_vecs"][l].partition_broadcast(P)).then_inc(k.rowv_loaded, 16)

    def load_gate_bias(l):
        for who in range(2 if l == 0 else 1):
            sp.dma_start(k.gates[:, who, :], w["b_ada_2"][l, 2 * D:].partition_broadcast(P)).then_inc(k.gate_bias_loaded, 16)

    def load_bias(l):
        for t in range(TT):
            for r in range(2):
                for h in range(8):
                    at = w["rpb"][l, h, 7 - 2 * t - r, 0:1]
                    src = bass.AP(tensor=at.tensor, offset=at.offset, ap=[[1, 64], [127, 4], [1, 64]])
                    dst = k.bias[64 * r:64 * r + 64, t, h, :].rearrange("p (a b) -> p a b", a=4)
                    sp.dma_start(dst, src).then_inc(k.bias_loaded, 16)

    sp.dma_start(k.v_flat[:, 0:D], w["final_norm"].partition_broadcast(P)).then_inc(k.final_norm_loaded, 16)
    load_layer_vectors(0)
    load_bias(0)
    for n in range(len(after)):
        key = after[n][0]
        if key == ("ada", 1, 0):
            sp.wait_ge(k.merged.sem, k.merged.at(0, 2, 1, 3))
            load_layer_vectors(1)
            load_bias(1)
        if key[0] == "ada" and key[2] == 4:
            sp.wait_ge(k.pv_done.sem, k.pv_done.at("diff", key[1], 3, UNITS - 1))
            load_gate_bias(key[1])
        load(n, after)

    sp.wait_ge(k.layer_done.sem, k.layer_done.at("x", LAYERS - 1, 3, 1))
    sp.dma_start(w["out"][0].rearrange("(t p) d -> p t d", p=P), k.x_rows).then_inc(k.stored, 16)
    sp.wait_ge(k.stored, 16)



def tensor_program(pe, k):
    readers = {}

    def wait(signal, *key):
        pe.wait_ge(signal.sem, signal.at(*key))

    def use(bank, signal, *key):
        if bank in readers:
            wait(readers[bank][0], *readers[bank][1])
        readers[bank] = (signal, key)
        return k.banks[bank]

    def weights(key, kt, cols):
        slot, value = k.landed[key]
        pe.wait_ge(k.slot_loaded[slot], value)
        return k.pool6[:, slot * SLOT:slot * SLOT + kt * cols].rearrange("p (k n) -> p k n", k=kt)

    turn = [0]

    def gemm_bank(signal, *key):
        turn[0] += 1
        return use("G%d" % (turn[0] % 2), signal, *key)

    def gemm_rows(key, kt, cols, lhs, groups, out_cols=None):
        wt = weights(key, kt, cols)
        for step, tile, c0, n, reader in groups:
            bank = gemm_bank(*reader)
            for c in range(kt):
                mm = nc.tensor.matmul(bank[:, 0:n], lhs(c, tile), wt[:, c, c0:c0 + n], start=(c == 0), stop=(c == kt - 1))
            k.bank_of[step] = bank
            mm.then_inc(k.gemm_done.sem, k.gemm_done.step(*step))

    def gemm_t(key, rhs, reader):
        wt = weights(key, KT_D, 512)
        for pair in range(2):
            bank = k.bank_of[(*key, pair)] = gemm_bank(*reader, pair)
            for g in range(2):
                f = 2 * pair + g
                for c in range(KT_D):
                    mm = nc.tensor.matmul(bank[:, 256 * g:256 * g + 256], wt[:, c, P * f:P * f + P], rhs(c),
                                          start=(c == 0), stop=(c == KT_D - 1))
            mm.then_inc(k.gemm_done.sem, k.gemm_done.step(*key, pair))

    flip = [0]

    def transposes(step, blocks, reader, width=P):
        flip[0] += 1
        bank = k.bank_of[step] = use("T%d" % (flip[0] % 2), *reader)
        for n, block in enumerate(blocks):
            mm = nc.tensor.transpose(bank[0:width, P * n:P * n + P], block, k.ident)
        mm.then_inc(k.turned.sem, k.turned.step(*step))

    def turn_normed(what, tile):
        wait(k.norm_rows, what, tile)
        for half in range(2):
            transposes((what, tile, half), [k.xn[:, tile % 2, P * c:P * c + P] for c in range(4 * half, 4 * half + 4)],
                       (k.ht_ready, what, tile, half))

    nc = k.nc
    xh = lambda c: k.ht[:, c, TOK:2 * TOK]
    mh = lambda c: k.ht[:, c, 0:TOK]
    tile_of_h = lambda c, t: k.ht[:, c, P * t:P * t + P]

    pe.wait_ge(k.small_loaded, 32)
    bank = use("T0", k.cols_ready)
    for n in range(2):
        mm = nc.tensor.transpose(bank[:, P * n:P * n + P], k.col_rows[:, n, :], k.ident)
    mm.then_inc(k.turned.sem, k.turned.step("cols"))

    for t in range(TT):
        turn_normed("mixer", t)
    wait(k.ht_ready, "mixer", 1, 1)

    def level_scores(n):
        size = (LEVELS + [0])[n]
        if size:
            wait(k.level_ready, n)
        else:
            wait(k.kk_ready)
        if size == 128:
            bank = use("S0", k.scores_taken, n, 0)
            for h in range(HEADS1):
                lv = k.level[:, n % 2, :].rearrange("p (h t) -> p h t", h=HEADS1)
                mm = nc.tensor.matmul(bank[:, P * h:P * h + P], lv[:, h, 0:P], lv[:, h, P:2 * P], start=True, stop=True)
            mm.then_inc(k.scores_done.sem, k.scores_done.step("level", n, 0))
            return
        for half in range(2):
            bank = use("S%d" % half, k.scores_taken, n, half)
            for b in range(4):
                at = slice(P * (4 * half + b), P * (4 * half + b) + P)
                left, right = (k.kk[:, at], k.qq[:, at]) if size == 0 else (k.level[:, n % 2, at],) * 2
                mm = nc.tensor.matmul(bank[:, P * b:P * b + P], left, right, start=True, stop=True)
            mm.then_inc(k.scores_done.sem, k.scores_done.step("level", n, half))

    gemm_t(("mix", 4), xh, (k.mix_read, 4))
    gemm_t(("mix", 3), xh, (k.mix_read, 3))
    gemm_rows(("mix", 5), KT_D, 512, lambda c, t: tile_of_h(c, 2 + t),
              [(("mix", 5, t), t, 0, 512, (k.mix_read, 5, t)) for t in range(TT)])
    for n, part in enumerate([6, 1, 2, 0]):
        level_scores(2 * n)
        level_scores(2 * n + 1)
        gemm_t(("mix", part), xh, (k.mix_read, part) if part not in (2, 0) else (k.conv_read, part))
    level_scores(len(LEVELS))
    wait(k.scores_taken, len(LEVELS), 1)
    wait(k.mix_read, 5, 1)
    for t in range(TT):
        bank = use("O%d" % t, k.hgrn_out, t)
        for h in range(HEADS1):
            out = bank[:, P * h:P * h + P]
            if t == 1:
                nc.tensor.matmul(out, k.far_scores[:, P * h:P * h + P], k.v[:, 0, P * h:P * h + P], start=True, stop=False)
            at = P * (2 * h + t)
            mm = nc.tensor.matmul(out, k.near_scores[:, at:at + P], k.v[:, t, P * h:P * h + P], start=(t == 0), stop=True)
        mm.then_inc(k.pv_done.sem, k.pv_done.step("hgrn", t))
    for t in range(TT):
        wait(k.hgrn_normed, t)
        transposes(("hgrn", t), [k.o[:, t, P * h:P * h + P] for h in range(HEADS1)], (k.yt_ready, t))
    wait(k.yt_ready, 1)
    wait(k.conv_read, 0, 1)
    for half in range(2):
        gemm_rows(("mixout", half), KT_D, 512, lambda c, t: k.t_out[:, c, P * t:P * t + P],
                  [(("mixout", half, t), t, 0, 512, (k.x_added, "mixout", half, t)) for t in range(TT)])

    for t in range(TT):
        turn_normed("mem", t)
    wait(k.ht_ready, "mem", 1, 1)
    for n in range(2):
        gemm_t(("xk", n), mh, (k.cross_read, "xk", n))
    for n in range(2):
        gemm_rows(("xv", n), KT_D, 512, tile_of_h,
                  [(("xv", n, t), t, 0, 512, (k.cross_read, "xv", n, t)) for t in range(TT)])
    for t in range(TT):
        turn_normed("cross", t)
    wait(k.ht_ready, "cross", 1, 1)
    for n in range(2):
        gemm_t(("xq", n), xh, (k.cross_read, "xq", n))
    wait(k.cross_read, "xq", 1, 1)
    units = [(t, h) for t in range(TT) for h in range(HEADS1)]

    def cross_scores(n):
        t, h = units[n]
        bank = k.bank_of["x", t, h] = use("S%d" % (n % 2), k.probs_ready, "x", t, h)
        for c in range(2):
            mm = nc.tensor.matmul(bank[:, 0:TOK], k.cross_q[:, 2 * h + c, P * t:P * t + P], k.cross_k[:, 2 * h + c, :],
                                  start=(c == 0), stop=(c == 1))
        mm.then_inc(k.scores_done.sem, k.scores_done.step("x", t, h))

    def cross_values(n):
        t, h = units[n]
        wait(k.probs_scaled, "x", t, h)
        transposes(("xp", t, h), [k.probs[:, n % 2, P * c:P * c + P] for c in range(TT)], (k.probs_turned, "x", t, h))
        wait(k.probs_turned, "x", t, h)
        bank = k.bank_of["xo_bank", t, h] = use("O%d" % (n % 2), k.cross_out, t, h)
        for f in range(2):
            for c in range(TT):
                at = 256 * h + P * f
                mm = nc.tensor.matmul(bank[:, P * f:P * f + P], k.cross_v[:, c, at:at + P],
                                      k.probs_t[:, n % 2, P * c:P * c + P], start=(c == 0), stop=(c == TT - 1))
        mm.then_inc(k.pv_done.sem, k.pv_done.step("x", t, h))

    cross_scores(0)
    for n in range(len(units)):
        if n + 1 < len(units):
            cross_scores(n + 1)
        cross_values(n)
    wait(k.cross_out, TT - 1, HEADS1 - 1)
    for n in range(2):
        gemm_rows(("xo", n), KT_D, 512, lambda c, t: k.t_out[:, c, P * t:P * t + P],
                  [(("xo", n, t), t, 0, 512, (k.x_added, "xo", n, t)) for t in range(TT)])

    for t in range(TT):
        turn_normed("moe", t)
    wait(k.ht_ready, "moe", 1, 1)
    pe.wait_ge(k.router_loaded, 64)
    bank = k.bank_of["router",] = gemm_bank(k.routed)
    for t in range(TT):
        for c in range(KT_D):
            mm = nc.tensor.matmul(bank[:, 20 * t:20 * t + 20], tile_of_h(c, 2 + t), k.router_w[:, c, :],
                                  start=(c == 0), stop=(c == KT_D - 1))
    mm.then_inc(k.gemm_done.sem, k.gemm_done.step("router"))
    wait(k.picked)
    bank = k.bank_of["places",] = gemm_bank(k.places_read)
    nc.tensor.matmul(bank[:, 0:16], k.before, k.selected[:, 0, :], start=True, stop=True)
    nc.tensor.matmul(bank[:, 16:32], k.before, k.selected[:, 1, :], start=True, stop=False)
    nc.tensor.matmul(bank[:, 16:32], k.ones, k.selected[:, 0, :], start=False, stop=True)
    nc.tensor.matmul(bank[:, 32:48], k.ones, k.selected[:, 0, :], start=True, stop=False)
    nc.tensor.matmul(bank[:, 32:48], k.ones, k.selected[:, 1, :], start=False, stop=True)\
        .then_inc(k.gemm_done.sem, k.gemm_done.step("places"))
    for bank in sorted(readers):
        wait(readers[bank][0], *readers[bank][1])
    readers.clear()
    gate_bank, up_bank, down_banks, list_banks, sum_banks = (k.all_banks[0], k.all_banks[1], k.all_banks[2:4],
                                                             k.all_banks[4:6], k.all_banks[6:8])

    def gather():
        for j in range(2):
            for f in range(KT_D):
                for t in range(TT):
                    mm = nc.tensor.matmul(list_banks[j][:, CAP * f:CAP * f + CAP], k.xn[:, t, P * f:P * f + P],
                                          k.lists[:, t, j, :], start=(t == 0), stop=(t == TT - 1))
            mm.then_inc(k.pair_gathered, 1)

    def turn_lists(p):
        pe.wait_ge(k.pair_tokens, 2 * p + 1)
        for t in range(TT):
            mm = nc.tensor.transpose(list_banks[0][:, P * t:P * t + P], k.weighted[:, t, :, :].rearrange("p j n -> p (j n)"),
                                     k.ident)
        mm.then_inc(k.pair_turned, 1)

    def expert_pair(p, first, last):
        def w_slot(j, part, kt):
            pe.wait_ge(k.slot_loaded[3 * j + part], 16 * (p + 1 + k.moe_base[3 * j + part]))
            return k.pool6[:, (3 * j + part) * SLOT:(3 * j + part + 1) * SLOT].rearrange("p (k n) -> p k n", k=kt)

        for j in range(2):
            for part, bank, sem, freed in ((0, gate_bank, k.pair_gate, k.pair_silu), (1, up_bank, k.pair_up, k.pair_hidden)):
                wt = w_slot(j, part, KT_D)
                if part == 0:
                    pe.wait_ge(k.pair_tokens, 2 * p + j + 1)
                if not (first and j == 0):
                    pe.wait_ge(freed, 2 * p + j)
                for f in range(4):
                    for c in range(KT_D):
                        mm = nc.tensor.matmul(bank[:, CAP * f:CAP * f + CAP], wt[:, c, P * f:P * f + P],
                                              k.tokens[:, j, c, :], start=(c == 0), stop=(c == KT_D - 1))
                mm.then_inc(sem, 1)
        for j in range(2):
            wt = w_slot(j, 2, 4)
            pe.wait_ge(k.pair_hidden, 2 * p + j + 1)
            if not first and j == 0:
                pe.wait_ge(k.pair_rows, 2 * p)
            for half in range(2):
                for c in range(4):
                    mm = nc.tensor.matmul(down_banks[half][CAP * j:CAP * j + CAP, :], k.pair_h[:, j, c, :],
                                          wt[:, c, 512 * half:512 * half + 512], start=(c == 0), stop=(c == 3))
            mm.then_inc(k.pair_down, 1)
        if not last:
            pe.wait_ge(k.pair_lists, p + 2)
            pe.wait_ge(k.pair_weights, p + 1)
            gather()
        pe.wait_ge(k.pair_rows, 2 * p + 2)
        pe.wait_ge(k.pair_weights, p + 1)
        for g in range(4):
            t, half = g // 2, g % 2
            if not (first and g < 2):
                pe.wait_ge(k.pair_summed, 4 * p + g - 1)
            nc.tensor.matmul(sum_banks[g % 2], k.weighted_t[:, P * t:P * t + P], k.down_rows[:, 512 * half:512 * half + 512],
                             start=True, stop=True).then_inc(k.pair_spread, 1)
        if not last:
            turn_lists(p + 1)

    def expert(e, i, j, first):
        def w_slot(part, kt):
            pe.wait_ge(k.slot_loaded[3 * j + part], 16 * (i + 1 + k.moe_base[3 * j + part]))
            return k.pool6[:, (3 * j + part) * SLOT:(3 * j + part + 1) * SLOT].rearrange("p (k n) -> p k n", k=kt)

        for part, (sem, freed) in enumerate([(k.moe_gate, k.moe_silu), (k.moe_up, k.moe_hidden)]):
            wt = w_slot(part, KT_D)
            for pair in range(2):
                if not first:
                    pe.wait_ge(freed, 2 * e + pair - 1)
                bank = k.all_banks[2 * part + pair]
                for g in range(2):
                    f = 2 * pair + g
                    for c in range(KT_D):
                        mm = nc.tensor.matmul(bank[:, TOK * g:TOK * g + TOK], wt[:, c, P * f:P * f + P], xh(c),
                                              start=(c == 0), stop=(c == KT_D - 1))
                mm.then_inc(sem, 1)
        wt = w_slot(2, 4)
        for t in range(TT):
            for half in range(2):
                g = 2 * t + half
                if not first:
                    pe.wait_ge(k.moe_added, 4 * e + g - 3)
                for c in range(4):
                    if g == 0 and c % 2 == 0:
                        pe.wait_ge(k.moe_hidden, 2 * e + c // 2 + 1)
                    mm = nc.tensor.matmul(k.all_banks[4 + g], k.hidden[:, c, P * t:P * t + P],
                                          wt[:, c, 512 * half:512 * half + 512], start=(c == 0), stop=(c == 3))
                mm.then_inc(k.moe_down, 1)

    crowded = read_crowded(pe, k)
    with pe.If(crowded == 0):
        pe.wait_ge(k.pair_lists, 1)
        gather()
        turn_lists(0)
        expert_pair(0, True, False)
        with pe.Fori(1, N_EXPERTS // 2 - 1) as p:
            expert_pair(p, False, False)
        expert_pair(N_EXPERTS // 2 - 1, False, True)
        pe.wait_ge(k.pair_summed, 2 * N_EXPERTS)
    with pe.Else():
        expert(0, 0, 0, True)
        expert(1, 0, 1, False)
        with pe.Fori(1, N_EXPERTS // 2) as i:
            for j in range(2):
                expert(2 * i + j, i, j, False)
        pe.wait_ge(k.moe_added, 4 * N_EXPERTS)

    wait(k.silu_c)
    for l in range(LAYERS):
        bank = k.bank_of["ada", l] = gemm_bank(k.ada_ready, l)
        for n in range(4):
            wt = weights(("ada", l, n), KT_D, 512)
            for f in range(4):
                at = 2 * (4 * n + f)
                for c in range(KT_D):
                    mm = nc.tensor.matmul(bank[:, at:at + 2], wt[:, c, P * f:P * f + P], k.sc[:, c, :],
                                          start=(c == 0), stop=(c == KT_D - 1))
            mm.then_inc(k.gemm_done.sem, k.gemm_done.step("ada", l, n))
        for t in range(4):
            turn_normed(("h", l), t)
        wait(k.ht_ready, ("h", l), 3, 1)

        def project(branch, part, kind, kt=KT_D, cols=512):
            gemm_rows((branch, l, part), kt, cols, tile_of_h,
                      [((branch, l, part, t), t, 0, cols, (k.proj_read, branch, l, part, t)) for t in tiles_of(l, kind)])

        def turn_heads(branch, part, t):
            wait(k.heads_ready, branch, l, part, t)
            dim = QK_DIM[branch]
            for g in range(2):
                transposes((branch, l, part, t, g),
                           [k.head_rows[:, t, dim * u:dim * u + dim] for u in range(4 * g, 4 * g + 4)],
                           (k.heads_turned, branch, l, part, t, g), width=dim)

        def attention(branch):
            dim, vd = QK_DIM[branch], V_DIM[branch]
            todo = attention_units(l)

            def scores(n):
                t, u = todo[n]
                keys = 512 if t >= 2 else TOK
                bank = k.bank_of[branch, l, t, u] = use("S%d" % (n % 2), k.probs_ready, branch, l, t, u)
                biased = branch == "na" and t >= 2
                mm = nc.tensor.matmul(bank[:, 0:keys], k.qt[0:dim, u, P * t:P * t + P], k.kt[0:dim, u, 0:keys],
                                      start=True, stop=not biased)
                if biased:
                    if (t, u) == (2, 0):
                        wait(k.bias_ready, l)
                    mm = nc.tensor.matmul(bank[:, TOK:2 * TOK], k.reverse, k.bias[:, t - 2, u, :], start=False, stop=True)
                mm.then_inc(k.scores_done.sem, k.scores_done.step(branch, l, t, u))

            def turn(n):
                t, u = todo[n]
                wait(k.probs_ready, branch, l, t, u)
                transposes(("p", branch, l, t, u), [k.probs[:, n % 2, P * c:P * c + P] for c in range(4 if t >= 2 else 2)],
                           (k.probs_turned, branch, l, t, u))

            def values(n):
                t, u = todo[n]
                wait(k.probs_turned, branch, l, t, u)
                bank = k.bank_of["pv", branch, l, t, u] = use("O%d" % (n % 2), k.unit_out, branch, l, t, u)
                vc = vd * (u if branch != "diff" else u // 2)
                last = 3 if t >= 2 else 1
                for c in range(last + 1):
                    mm = nc.tensor.matmul(bank[:, 0:vd], k.probs_t[:, n % 2, P * c:P * c + P], k.v[:, c, vc:vc + vd],
                                          start=(c == 0), stop=(c == last))
                mm.then_inc(k.pv_done.sem, k.pv_done.step(branch, l, t, u))

            scores(0)
            for n in range(len(todo) + 1):
                if n + 1 < len(todo):
                    scores(n + 1)
                if n < len(todo):
                    turn(n)
                if n >= 1:
                    values(n - 1)

        for branch in BRANCHES:
            if branch == "mla":
                project("mla", "ckv", "kv", cols=288)
                project("mla", "cq", "q", cols=384)
                for part, kind, n in (("ckv", "kv", 2), ("cq", "q", 3)):
                    for t in tiles_of(l, kind):
                        wait(k.latent_normed, l, part, t)
                        src = k.ckv_rows if part == "ckv" else k.cq_rows
                        transposes((part, l, t), [src[:, t, P * c:P * c + P] for c in range(n)], (k.latent_turned, l, part, t))
                wait(k.latent_turned, l, "cq", 3)
                gemm_rows(("mla", l, "ukv"), 2, 1024, lambda c, t: k.ckvt[:, c, P * t:P * t + P],
                          [(("mla", l, "ukv", t, half), t, 512 * half, 512, (k.proj_read, "mla", l, "ukv", t, half))
                           for t in tiles_of(l, "kv") for half in range(2)])
            else:
                project(branch, "k", "kv")
                project(branch, "v", "kv")
            for t in tiles_of(l, "kv"):
                turn_heads(branch, "k", t)
            if branch == "mla":
                gemm_rows(("mla", l, "uq"), 3, 768, lambda c, t: k.cqt[:, c, P * t:P * t + P],
                          [(("mla", l, "uq", t, half), t, 384 * half, 384, (k.proj_read, "mla", l, "uq", t, half))
                           for t in tiles_of(l, "q") for half in range(2)])
            else:
                project(branch, "q", "q")
            for t in tiles_of(l, "q"):
                turn_heads(branch, "q", t)
            wait(k.heads_turned, branch, l, "q", 3, 1)
            attention(branch)
            b = BRANCHES.index(branch)
            gemm_rows(("z", l, b), KT_D, 512, tile_of_h,
                      [(("z", l, b, t), t, 0, 512, (k.z_read, l, b, t)) for t in tiles_of(l, "q")])
            for t in tiles_of(l, "q"):
                wait(k.branch_gated, l, b, t)
                transposes(("o", l, b, t), [k.o[:, t, P * c:P * c + P] for c in range(4)], (k.branch_turned, l, b, t))
            wait(k.branch_turned, l, b, 3)
            wbr = weights(("br", l, b), 4, 1024)
            for half in range(2):
                wgm = weights(("gm", l, b, half), KT_D, 512)
                for t in tiles_of(l, "q"):
                    bank = k.bank_of["gm", l, b, half, t] = gemm_bank(k.gm_read, l, b, half, t)
                    for c in range(KT_D):
                        mm = nc.tensor.matmul(bank, tile_of_h(c, t), wgm[:, c, :], start=(c == 0), stop=(c == KT_D - 1))
                    mm.then_inc(k.gemm_done.sem, k.gemm_done.step("gm", l, b, half, t))
                    bank = k.bank_of["br", l, b, half, t] = gemm_bank(k.merged, l, b, half, t)
                    for c in range(4):
                        mm = nc.tensor.matmul(bank, k.ogt[:, c, P * t:P * t + P], wbr[:, c, 512 * half:512 * half + 512],
                                              start=(c == 0), stop=(c == 3))
                    mm.then_inc(k.gemm_done.sem, k.gemm_done.step("br", l, b, half, t))
        for t in tiles_of(l, "q"):
            for half in range(2):
                wait(k.merged, l, 2, half, t)
                transposes(("y", l, t, half), [k.y[:, t, P * c:P * c + P] for c in range(4 * half, 4 * half + 4)],
                           (k.y_turned, l, t, half))
        wait(k.spread_c, l)
        for n in (4, 5):
            wt = weights(("ada", l, n), KT_D, 512)
            for who in (["ctx", "x"] if l == 0 else ["x"]):
                bank = k.bank_of["gate", l, n, who] = gemm_bank(k.gate_ready, l, n, who)
                for c in range(KT_D):
                    mm = nc.tensor.matmul(bank, k.sc_wide[:, 0 if who == "x" else 1, c, :], wt[:, c, :],
                                          start=(c == 0), stop=(c == KT_D - 1))
                mm.then_inc(k.gemm_done.sem, k.gemm_done.step("gate", l, n, who))
        wait(k.y_turned, l, 3, 1)
        for half in range(2):
            gemm_rows(("out", l, half), KT_D, 512, lambda c, t: k.yt[:, c, P * t:P * t + P],
                      [(("out", l, half, t), t, 0, 512, (k.layer_done, "x", l, t, half)) for t in tiles_of(l, "q")])



def scalar_program(act, k):
    nc = k.nc

    def wait(signal, *key):
        act.wait_ge(signal.sem, signal.at(*key))

    def activate(out, in_, func, **more):
        return nc.scalar.activation(out, in_, func, **more)

    wait(k.cols_ready)
    for n, name in enumerate(["c_2", "c_ctx_2"]):
        ins = activate(k.sc[:, :, n], k.cols[:, COLS[name]:COLS[name] + 8], ACT.Silu)
    ins.then_inc(k.silu_c.sem, k.silu_c.step())
    wait(k.lb_diff)
    activate(k.lb, k.lb_raw, ACT.Sigmoid).then_inc(k.lb_ready.sem, k.lb_ready.step())

    for pair in range(2):
        wait(k.gemm_done, "mix", 4, pair)
        at = slice(512 * pair, 512 * pair + 512)
        bank = k.bank_of["mix", 4, pair]
        activate(k.lf[:, at], bank, ACT.Sigmoid)
        activate(k.kk[:, at], bank, ACT.Sigmoid, scale=-1.0).then_inc(k.mix_read.sem, k.mix_read.step(4, pair))
    for pair in range(2):
        wait(k.gemm_done, "mix", 3, pair)
        activate(k.qq[:, 512 * pair:512 * pair + 512], k.bank_of["mix", 3, pair], ACT.Copy)\
            .then_inc(k.mix_read.sem, k.mix_read.step(3, pair))
    wait(k.f_ready)
    activate(k.lf, k.lf, ACT.Ln).then_inc(k.logf_ready.sem, k.logf_ready.step())
    for t in range(TT):
        wait(k.gemm_done, "mix", 5, t)
        activate(k.v[:, t, :], k.bank_of["mix", 5, t], ACT.Copy).then_inc(k.mix_read.sem, k.mix_read.step(5, t))

    def level_exp(n):
        wait(k.level_diff, n)
        if n >= 1:
            wait(k.level_ready, n - 1)
        activate(k.level_e, k.level_d, ACT.Exp).then_inc(k.level_exp.sem, k.level_exp.step(n))

    for part, dst, func in [(6, k.silu_g, ACT.Silu), (1, k.cc, ACT.Copy)]:
        first = 0 if part == 6 else 2
        level_exp(first)
        level_exp(first + 1)
        for pair in range(2):
            wait(k.gemm_done, "mix", part, pair)
            activate(dst[:, 512 * pair:512 * pair + 512], k.bank_of["mix", part, pair], func)\
                .then_inc(k.mix_read.sem, k.mix_read.step(part, pair))
    for n in range(4, len(LEVELS)):
        level_exp(n)

    for n in range(2):
        for pair in range(2):
            wait(k.gemm_done, "xk", n, pair)
            f = 4 * n + 2 * pair
            activate(k.cross_k[:, f:f + 2, :].rearrange("p f t -> p (f t)"), k.bank_of["xk", n, pair], ACT.Copy)\
                .then_inc(k.cross_read.sem, k.cross_read.step("xk", n, pair))
    for n in range(2):
        for t in range(TT):
            wait(k.gemm_done, "xv", n, t)
            activate(k.cross_v[:, t, 512 * n:512 * n + 512], k.bank_of["xv", n, t], ACT.Copy)\
                .then_inc(k.cross_read.sem, k.cross_read.step("xv", n, t))
    for n in range(2):
        for pair in range(2):
            wait(k.gemm_done, "xq", n, pair)
            f = 4 * n + 2 * pair
            activate(k.cross_q[:, f:f + 2, :].rearrange("p f t -> p (f t)"), k.bank_of["xq", n, pair], ACT.Copy,
                     scale=float(D // HEADS1) ** -0.5).then_inc(k.cross_read.sem, k.cross_read.step("xq", n, pair))
    units = [(t, h) for t in range(TT) for h in range(HEADS1)]

    def cross_exp(n):
        t, h = units[n]
        wait(k.max_ready, "x", t, h)
        if n >= 2:
            wait(k.turned, "xp", *units[n - 2])
        activate(k.probs[:, n % 2, 0:TOK], k.bank_of["x", t, h][:, 0:TOK], ACT.Exp, bias=k.nmax[:, n % 4:n % 4 + 1],
                 accum_out=k.psums[:, n % 4:n % 4 + 1]).then_inc(k.probs_ready.sem, k.probs_ready.step("x", t, h))

    cross_exp(0)
    for n, (t, h) in enumerate(units):
        if n + 1 < len(units):
            cross_exp(n + 1)
        wait(k.turned, "xp", t, h)
        if n >= 2:
            wait(k.pv_done, "x", *units[n - 2])
        activate(k.probs_t[:, n % 2, 0:TOK], k.bank_of["xp", t, h][:, 0:TOK], ACT.Copy)\
            .then_inc(k.probs_turned.sem, k.probs_turned.step("x", t, h))
        wait(k.pv_done, "x", t, h)
        activate(k.t_out[:, 2 * h:2 * h + 2, P * t:P * t + P],
                 k.bank_of["xo_bank", t, h][:, 0:TOK].rearrange("p (f t) -> p f t", f=2), ACT.Copy)\
            .then_inc(k.cross_out.sem, k.cross_out.step(t, h))

    wait(k.route_diff, "group")
    activate(k.route_ge, k.route_ge, ACT.Exp).then_inc(k.route_exp.sem, k.route_exp.step("group"))
    wait(k.route_diff, "expert")
    activate(k.route_ee, k.route_ee, ACT.Exp).then_inc(k.route_exp.sem, k.route_exp.step("expert"))

    def expert(e, first):
        for pair in range(2):
            act.wait_ge(k.moe_gate, 2 * e + pair + 1)
            if not first:
                act.wait_ge(k.moe_hidden, 2 * e + pair - 1)
            activate(k.moe_g[:, pair, :], k.all_banks[pair], ACT.Silu).then_inc(k.moe_silu, 1)

    def weights_out(p):
        act.wait_ge(k.pair_turned, p + 1)
        activate(k.weighted_t, k.all_banks[4][:, 0:TOK], ACT.Copy).then_inc(k.pair_weights, 1)

    def expert_pair(p, first, last):
        for j in range(2):
            act.wait_ge(k.pair_gate, 2 * p + j + 1)
            if not (first and j == 0):
                act.wait_ge(k.pair_hidden, 2 * p + j)
            activate(k.pair_g, k.all_banks[0][:, 0:4 * CAP], ACT.Silu).then_inc(k.pair_silu, 1)
        act.wait_ge(k.pair_down, 2 * p + 2)
        for half in range(2):
            activate(k.down_rows[:, 512 * half:512 * half + 512], k.all_banks[2 + half], ACT.Copy).then_inc(k.pair_rows, 1)
        if not last:
            weights_out(p + 1)

    crowded = read_crowded(act, k)
    with act.If(crowded == 0):
        weights_out(0)
        expert_pair(0, True, False)
        with act.Fori(1, N_EXPERTS // 2 - 1) as p:
            expert_pair(p, False, False)
        expert_pair(N_EXPERTS // 2 - 1, False, True)
    with act.Else():
        expert(0, True)
        expert(1, False)
        with act.Fori(1, N_EXPERTS // 2) as i:
            for j in range(2):
                expert(2 * i + j, False)

    for l in range(LAYERS):
        wait(k.lam_dots, l)
        activate(k.lam2, k.lam2, ACT.Exp).then_inc(k.lam_exp.sem, k.lam_exp.step(l))

        def read(branch, part, t, pairs):
            for n, (dst, src) in enumerate(pairs):
                ins = activate(dst, src, ACT.Copy)
            return ins

        def project(branch, part, kind):
            for t in tiles_of(l, kind):
                wait(k.gemm_done, branch, l, part, t)
                bank = k.bank_of[branch, l, part, t]
                if part == "v":
                    dst, src = k.v[:, t, :], bank
                elif part == "ckv":
                    dst, src = k.ckv_rows[:, t, :], bank[:, 0:288]
                elif part == "cq":
                    dst, src = k.cq_rows[:, t, :], bank[:, 0:384]
                else:
                    dst, src = k.head_rows[:, t, 0:512], bank
                    if part == "q" and t in tiles_of(l, "kv"):
                        wait(k.turned, branch, l, "k", t, 1)
                activate(dst, src, ACT.Copy).then_inc(k.proj_read.sem, k.proj_read.step(branch, l, part, t))

        def turn_heads(branch, part, t):
            dim = QK_DIM[branch]
            dst = k.qt if part == "q" else k.kt
            for g in range(2):
                wait(k.turned, branch, l, part, t, g)
                activate(dst[0:dim, 4 * g:4 * g + 4, P * t:P * t + P],
                         k.bank_of[branch, l, part, t, g][0:dim, :].rearrange("p (u t) -> p u t", u=4), ACT.Copy,
                         scale=float(dim) ** -0.5 if part == "q" else 1.0)\
                    .then_inc(k.heads_turned.sem, k.heads_turned.step(branch, l, part, t, g))

        for branch in BRANCHES:
            if branch == "mla":
                project("mla", "ckv", "kv")
                project("mla", "cq", "q")
                for t in tiles_of(l, "kv"):
                    for half in range(2):
                        wait(k.gemm_done, "mla", l, "ukv", t, half)
                        bank = k.bank_of["mla", l, "ukv", t, half].rearrange("p (h d) -> p h d", h=4)
                        activate(k.head_rows[:, t, 384 * half:384 * half + 384].rearrange("p (h d) -> p h d", h=4)[:, :, 0:64],
                                 bank[:, :, 0:64], ACT.Copy)
                        activate(k.v[:, t, 256 * half:256 * half + 256].rearrange("p (h d) -> p h d", h=4),
                                 bank[:, :, 64:128], ACT.Copy)\
                            .then_inc(k.proj_read.sem, k.proj_read.step("mla", l, "ukv", t, half))
            else:
                project(branch, "k", "kv")
                project(branch, "v", "kv")
            for t in tiles_of(l, "kv"):
                turn_heads(branch, "k", t)
            if branch == "mla":
                for t in tiles_of(l, "q"):
                    for half in range(2):
                        wait(k.gemm_done, "mla", l, "uq", t, half)
                        activate(k.head_rows[:, t, 384 * half:384 * half + 384],
                                 k.bank_of["mla", l, "uq", t, half][:, 0:384], ACT.Copy)\
                            .then_inc(k.proj_read.sem, k.proj_read.step("mla", l, "uq", t, half))
            else:
                project(branch, "q", "q")
            for t in tiles_of(l, "q"):
                turn_heads(branch, "q", t)

            todo = attention_units(l)

            def exp(n):
                t, u = todo[n]
                keys = 512 if t >= 2 else TOK
                wait(k.max_ready, branch, l, t, u)
                if n >= 2:
                    wait(k.turned, "p", branch, l, *todo[n - 2])
                activate(k.probs[:, n % 2, 0:keys], k.bank_of[branch, l, t, u][:, 0:keys], ACT.Exp,
                         bias=k.nmax[:, n % 4:n % 4 + 1], accum_out=k.psums[:, n % 4:n % 4 + 1])\
                    .then_inc(k.probs_ready.sem, k.probs_ready.step(branch, l, t, u))

            def turned_probs(n):
                t, u = todo[n]
                keys = 512 if t >= 2 else TOK
                wait(k.turned, "p", branch, l, t, u)
                if n >= 2:
                    wait(k.pv_done, branch, l, *todo[n - 2])
                activate(k.probs_t[:, n % 2, 0:keys], k.bank_of["p", branch, l, t, u][:, 0:keys], ACT.Copy)\
                    .then_inc(k.probs_turned.sem, k.probs_turned.step(branch, l, t, u))

            for n in range(len(todo) + 1):
                if n < len(todo):
                    exp(n)
                if n >= 1:
                    turned_probs(n - 1)

            b = BRANCHES.index(branch)
            for i, t in enumerate(tiles_of(l, "q")):
                wait(k.gemm_done, "z", l, b, t)
                if i >= 2:
                    wait(k.branch_gated, l, b, t - 2)
                activate(k.sz[:, t % 2, :], k.bank_of["z", l, b, t], ACT.Silu)\
                    .then_inc(k.z_read.sem, k.z_read.step(l, b, t))
            for t in tiles_of(l, "q"):
                wait(k.turned, "o", l, b, t)
                activate(k.ogt[:, :, P * t:P * t + P], k.bank_of["o", l, b, t].rearrange("p (c t) -> p c t", c=4), ACT.Copy)\
                    .then_inc(k.branch_turned.sem, k.branch_turned.step(l, b, t))
            steps = [(half, t) for half in range(2) for t in tiles_of(l, "q")]
            for n, (half, t) in enumerate(steps):
                wait(k.gemm_done, "gm", l, b, half, t)
                if n >= 2:
                    wait(k.merged, l, b, *steps[n - 2])
                activate(k.sg[:, n % 2, :], k.bank_of["gm", l, b, half, t], ACT.Sigmoid)\
                    .then_inc(k.gm_read.sem, k.gm_read.step(l, b, half, t))
        for t in tiles_of(l, "q"):
            for half in range(2):
                wait(k.turned, "y", l, t, half)
                activate(k.yt[:, 4 * half:4 * half + 4, P * t:P * t + P],
                         k.bank_of["y", l, t, half].rearrange("p (c t) -> p c t", c=4), ACT.Copy)\
                    .then_inc(k.y_turned.sem, k.y_turned.step(l, t, half))



def vector_program(dve, k):
    nc = k.nc
    v = nc.vector

    def wait(signal, *key):
        dve.wait_ge(signal.sem, signal.at(*key))

    def then(ins):
        ins.then_inc(k.vector_steps.sem, k.vector_steps.step(k.vector_steps.count))
        dve.wait_ge(k.vector_steps.sem, k.vector_steps.count)

    xn_reader = {}

    def rstd(sums, n, *key):
        v.tensor_scalar(sums, sums, 1.0 / n, EPS, ALU.mult, ALU.add).then_inc(k.mean_squares.sem, k.mean_squares.step(*key))
        wait(k.rstd_ready, *key)

    def norm(what, tile, src):
        slot = tile % 2
        if slot in xn_reader:
            wait(k.turned, *xn_reader[slot])
        xn_reader[slot] = (what, tile, 1)
        then(v.tensor_tensor_reduce(out=k.xn[:, slot, :], in0=src, in1=src, scale=1.0, scalar=0.0, op0=ALU.mult,
                                    op1=ALU.add, accum_out=k.ss[:, 0:1]))
        rstd(k.ss[:, 0:1], D, what, tile)
        v.tensor_scalar(k.xn[:, slot, :], src, k.ss[:, 0:1], None, ALU.mult)\
            .then_inc(k.norm_rows.sem, k.norm_rows.step(what, tile))
        wait(k.norm_rows, what, tile)

    def ht_out(what, tile, at, gain, shift=None):
        for half in range(2):
            wait(k.turned, what, tile, half)
            dst = k.ht[:, 4 * half:4 * half + 4, at:at + P]
            src = k.bank_of[what, tile, half].rearrange("p (c t) -> p c t", c=4)
            ins = v.tensor_tensor(dst, src, gain[:, 4 * half:4 * half + 4].unsqueeze(2).to_broadcast([P, 4, P]), ALU.mult)
            if shift is not None:
                then(ins)
                ins = v.tensor_tensor(dst, dst, shift[:, 4 * half:4 * half + 4].unsqueeze(2).to_broadcast([P, 4, P]), ALU.add)
            ins.then_inc(k.ht_ready.sem, k.ht_ready.step(what, tile, half))

    def col(name, at, n):
        return k.cols[:, COLS[name] + at:COLS[name] + at + n]

    def group_norm(x3, groups, dim, scratch, *key):
        sq = scratch[:, 0:groups * dim].rearrange("p (g d) -> p g d", g=groups)
        then(v.tensor_tensor(sq, x3, x3, ALU.mult))
        then(v.tensor_reduce(k.ss[:, 0:groups], sq, X_AXIS, ALU.add))
        rstd(k.ss[:, 0:groups], dim, *key)
        return v.tensor_tensor(x3, x3, k.ss[:, 0:groups].unsqueeze(2).to_broadcast([P, groups, dim]), ALU.mult)

    v.memset(k.ones, 1.0)
    v.memset(k.near_scores, 0.0)
    v.memset(k.conv_in[:, :, 0:2], 0.0)
    wait(k.turned, "cols")
    v.tensor_copy(k.cols, k.banks["T0"][:, 0:2 * P]).then_inc(k.cols_ready.sem, k.cols_ready.step())
    wait(k.cols_ready)
    v.tensor_tensor(k.lb_raw, col("hgrn_lb", 0, 4), col("hgrn_lb", 4, 4), ALU.subtract)\
        .then_inc(k.lb_diff.sem, k.lb_diff.step())

    dve.wait_ge(k.x_loaded, 16)
    for t in range(TT):
        norm("mixer", t, k.x_rows[:, t, :])
    wait(k.lb_ready)
    then(v.tensor_scalar(k.omlb, k.lb, -1.0, 1.0, ALU.mult, ALU.add))
    for t in range(TT):
        ht_out("mixer", t, TOK + P * t, col("mix_norm", 0, 8))
    dve.wait_ge(k.mem_loaded, 16)
    for t in range(TT):
        norm("mem", t, k.ctx_rows[:, t, :])

    for pair in range(2):
        wait(k.mix_read, 4, pair)
        for h in (2 * pair, 2 * pair + 1):
            at = slice(TOK * h, TOK * h + TOK)
            ins = v.tensor_scalar(k.lf[:, at], k.lf[:, at], k.omlb[:, h:h + 1], k.lb[:, h:h + 1], ALU.mult, ALU.add)
    ins.then_inc(k.f_ready.sem, k.f_ready.step())
    for h in range(HEADS1):
        at = slice(TOK * h, TOK * h + TOK)
        ins = v.tensor_scalar(k.kk[:, at], k.kk[:, at], k.omlb[:, h:h + 1], None, ALU.mult)
    ins.then_inc(k.kk_ready.sem, k.kk_ready.step())
    wait(k.logf_ready)
    for n in range(2 * HEADS1):
        at = slice(P * n, P * n + P)
        ins = v.tensor_tensor_scan(k.b[:, at], k.ones, k.lf[:, at], 0.0, ALU.mult, ALU.add)
    then(ins)

    def level_diff(n):
        size = LEVELS[n]
        if n >= 1:
            wait(k.level_exp, n - 1)
        b4 = k.b.rearrange("p (b two s) -> p b two s", two=2, s=size)
        d4 = k.level_d.rearrange("p (b two s) -> p b two s", two=2, s=size)
        middle = b4[:, :, 0, size - 1:size].to_broadcast([P, 2 * HEADS1 * P // (2 * size), size])
        v.tensor_tensor(d4[:, :, 0, :], middle, b4[:, :, 0, :], ALU.subtract)
        if size == P:
            ins = v.tensor_copy(d4[:, :, 1, :], b4[:, :, 1, :])
        else:
            ins = v.tensor_tensor(d4[:, :, 1, :], b4[:, :, 1, :], middle, ALU.subtract)
        ins.then_inc(k.level_diff.sem, k.level_diff.step(n))

    def take_scores(n):
        size = (LEVELS + [0])[n]
        if size == P:
            wait(k.scores_done, "level", n, 0)
            v.tensor_copy(k.far_scores, k.banks["S0"]).then_inc(k.scores_taken.sem, k.scores_taken.step(n, 0))
            return
        mask = k.masks[:, P * (n - 1):P * n].unsqueeze(1).to_broadcast([P, 4, P])
        for half in range(2):
            wait(k.scores_done, "level", n, half)
            dst = k.near_scores[:, 512 * half:512 * half + 512].rearrange("p (b t) -> p b t", b=4)
            src = k.banks["S%d" % half].rearrange("p (b t) -> p b t", b=4)
            v.copy_predicated(dst, mask.bitcast(U32), src).then_inc(k.scores_taken.sem, k.scores_taken.step(n, half))
            wait(k.scores_taken, n, half)

    def conv_input():
        for pair in range(2):
            wait(k.gemm_done, "mix", 2, pair)
            wait(k.mix_read, 1, pair)
            f = 2 * pair
            v.tensor_tensor(k.conv_in[:, f:f + 2, 2:2 + TOK], k.bank_of["mix", 2, pair].rearrange("p (f t) -> p f t", f=2),
                            k.cc[:, TOK * f:TOK * f + 2 * TOK].rearrange("p (f t) -> p f t", f=2), ALU.mult)\
                .then_inc(k.conv_read.sem, k.conv_read.step(2, pair))
        wait(k.conv_read, 2, 1)
        for f in range(4):
            tap = lambda j: col("conv_w", 4 * j + f, 1)
            then(v.tensor_scalar(k.conv[:, f, :], k.conv_in[:, f, 0:TOK], tap(0), None, ALU.mult))
            for j in (1, 2):
                then(v.scalar_tensor_tensor(out=k.conv[:, f, :], in0=k.conv_in[:, f, j:j + TOK], scalar=tap(j),
                                            in1=k.conv[:, f, :], op0=ALU.mult, op1=ALU.add))

    dve.wait_ge(k.masks_loaded, 16)
    level_diff(0)
    level_diff(1)
    for n in range(0, len(LEVELS), 2):
        take_scores(n)
        take_scores(n + 1)
        if n + 2 < len(LEVELS):
            level_diff(n + 2)
            level_diff(n + 3)
        if n == 4:
            conv_input()
    for pair in range(2):
        wait(k.gemm_done, "mix", 0, pair)
        v.tensor_tensor(k.t_out[:, 2 * pair:2 * pair + 2, :], k.bank_of["mix", 0, pair].rearrange("p (f t) -> p f t", f=2),
                        k.conv[:, 2 * pair:2 * pair + 2, :], ALU.mult).then_inc(k.conv_read.sem, k.conv_read.step(0, pair))
    take_scores(len(LEVELS))
    for t in range(TT):
        wait(k.pv_done, "hgrn", t)
        v.tensor_copy(k.o[:, t, :], k.banks["O%d" % t]).then_inc(k.hgrn_out.sem, k.hgrn_out.step(t))
        wait(k.hgrn_out, t)
        group_norm(k.o[:, t, :].rearrange("p (h d) -> p h d", h=HEADS1), HEADS1, P, k.level_d, "hgrn", t)\
            .then_inc(k.hgrn_normed.sem, k.hgrn_normed.step(t))
        wait(k.hgrn_normed, t)
    for t in range(TT):
        wait(k.turned, "hgrn", t)
        wait(k.mix_read, 6, 1)
        for h in range(HEADS1):
            ins = v.scalar_tensor_tensor(out=k.t_out[:, 4 + h, P * t:P * t + P], in0=k.bank_of["hgrn", t][:, P * h:P * h + P],
                                         scalar=col("hgrn_norm", h, 1), in1=k.silu_g[:, TOK * h + P * t:TOK * h + P * t + P],
                                         op0=ALU.mult, op1=ALU.mult)
        ins.then_inc(k.yt_ready.sem, k.yt_ready.step(t))

    def add_to_x(what):
        for half in range(2):
            for t in range(TT):
                wait(k.gemm_done, what, half, t)
                at = k.x_rows[:, t, 512 * half:512 * half + 512]
                v.tensor_tensor(at, at, k.bank_of[what, half, t], ALU.add)\
                    .then_inc(k.x_added.sem, k.x_added.step(what, half, t))
        wait(k.x_added, what, 1, TT - 1)

    add_to_x("mixout")
    for t in range(TT):
        ht_out("mem", t, P * t, col("mem_norm", 0, 8))
        norm("cross", t, k.x_rows[:, t, :])
    for t in range(TT):
        ht_out("cross", t, TOK + P * t, col("xattn_norm", 0, 8))

    units = [(t, h) for t in range(TT) for h in range(HEADS1)]

    def cross_max(n):
        t, h = units[n]
        wait(k.scores_done, "x", t, h)
        v.tensor_reduce(k.nmax[:, n % 4:n % 4 + 1], k.bank_of["x", t, h][:, 0:TOK], X_AXIS, ALU.max, negate=True)\
            .then_inc(k.max_ready.sem, k.max_ready.step("x", t, h))

    cross_max(0)
    for n, (t, h) in enumerate(units):
        if n + 1 < len(units):
            cross_max(n + 1)
        wait(k.probs_ready, "x", t, h)
        then(v.reciprocal(k.ss[:, 0:1], k.psums[:, n % 4:n % 4 + 1]))
        v.tensor_scalar(k.probs[:, n % 2, 0:TOK], k.probs[:, n % 2, 0:TOK], k.ss[:, 0:1], None, ALU.mult)\
            .then_inc(k.probs_scaled.sem, k.probs_scaled.step("x", t, h))
        wait(k.probs_scaled, "x", t, h)
    add_to_x("xo")
    for t in range(TT):
        norm("moe", t, k.x_rows[:, t, :])
    for t in range(TT):
        ht_out("moe", t, TOK + P * t, col("ffn_norm", 0, 8))

    def bc(ap, n):
        return ap.unsqueeze(2).to_broadcast([P, TT, n])

    rank = k.rank.unsqueeze(1).to_broadcast([P, TT, 4])
    r = k.route
    lg, gp, goh, el, ep, oh1, oh2, wts, eq, ep2 = (r[:, 64 * n:64 * n + 64] for n in range(10))
    three = lambda ap: ap[:, 0:8].rearrange("p (t e) -> p t e", t=TT)
    gp, goh, el, ep, oh1, oh2, wts, eq, ep2 = (three(a) for a in (gp, goh, el, ep, oh1, oh2, wts, eq, ep2))
    lg = lg[:, 0:40].rearrange("p (t n) -> p t n", t=TT)
    small = lambda n: k.route_small[:, 2 * n:2 * n + 2]
    gmax, gsum, gbest, rm, emax, m1, m2, den, gw, esum = (small(n) for n in range(10))

    def first_best(values, best, out):
        then(v.tensor_tensor(eq, values, bc(best, 4), ALU.is_equal))
        then(v.tensor_tensor(eq, eq, rank, ALU.mult))
        then(v.tensor_reduce(rm, eq, X_AXIS, ALU.max))
        then(v.tensor_tensor(out, eq, bc(rm, 4), ALU.is_equal))

    wait(k.gemm_done, "router")
    dve.wait_ge(k.router_loaded, 64)
    v.tensor_tensor(lg, k.bank_of["router",][:, 0:40].rearrange("p (t n) -> p t n", t=TT),
                    k.router_b.unsqueeze(1).to_broadcast([P, TT, 20]), ALU.add).then_inc(k.routed.sem, k.routed.step())
    wait(k.routed)
    ge = k.route_ge.rearrange("p (t e) -> p t e", t=TT)
    ee = k.route_ee.rearrange("p (t e) -> p t e", t=TT)
    then(v.tensor_reduce(gmax, lg[:, :, 0:4], X_AXIS, ALU.max))
    v.tensor_tensor(ge, lg[:, :, 0:4], bc(gmax, 4), ALU.subtract).then_inc(k.route_diff.sem, k.route_diff.step("group"))
    wait(k.route_exp, "group")
    then(v.tensor_reduce(gsum, ge, X_AXIS, ALU.add))
    then(v.reciprocal(gsum, gsum))
    then(v.tensor_tensor(gp, ge, bc(gsum, 4), ALU.mult))
    then(v.tensor_reduce(gbest, gp, X_AXIS, ALU.max))
    first_best(gp, gbest, goh)
    for t in range(TT):
        picked = k.route_pick[:, 16 * t:16 * t + 16].rearrange("p (g e) -> p g e", g=4)
        then(v.tensor_tensor(picked, lg[:, t, 4:20].rearrange("p (g e) -> p g e", g=4),
                             goh[:, t, :].unsqueeze(2).to_broadcast([P, 4, 4]), ALU.mult))
        then(v.tensor_reduce(el[:, t, :], picked.rearrange("p g e -> p e g"), X_AXIS, ALU.add))
    then(v.tensor_reduce(emax, el, X_AXIS, ALU.max))
    v.tensor_tensor(ee, el, bc(emax, 4), ALU.subtract).then_inc(k.route_diff.sem, k.route_diff.step("expert"))
    wait(k.route_exp, "expert")
    then(v.tensor_reduce(esum, ee, X_AXIS, ALU.add))
    then(v.reciprocal(esum, esum))
    then(v.tensor_tensor(ep, ee, bc(esum, 4), ALU.mult))
    then(v.tensor_reduce(m1, ep, X_AXIS, ALU.max))
    first_best(ep, m1, oh1)
    then(v.scalar_tensor_tensor(out=ep2, in0=oh1, scalar=-2.0, in1=ep, op0=ALU.mult, op1=ALU.add))
    then(v.tensor_reduce(m2, ep2, X_AXIS, ALU.max))
    first_best(ep2, m2, oh2)
    then(v.tensor_tensor(den, m1, m2, ALU.add))
    then(v.reciprocal(den, den))
    then(v.tensor_tensor(gw, gbest, den, ALU.mult))
    then(v.tensor_tensor(ep2, oh1, oh2, ALU.add))
    for t in range(TT):
        ins = v.tensor_tensor(k.selected[:, t, :].rearrange("p (g e) -> p g e", g=4),
                              goh[:, t, :].unsqueeze(2).to_broadcast([P, 4, 4]),
                              ep2[:, t, :].unsqueeze(1).to_broadcast([P, 4, 4]), ALU.mult)
    ins.then_inc(k.picked.sem, k.picked.step())
    then(v.tensor_tensor(oh1, oh1, bc(m1, 4), ALU.mult))
    then(v.tensor_tensor(oh2, oh2, bc(m2, 4), ALU.mult))
    then(v.tensor_tensor(wts, oh1, oh2, ALU.add))
    then(v.tensor_tensor(wts, wts, bc(gw, 4), ALU.mult))
    for t in range(TT):
        then(v.tensor_tensor(k.combine[:, t, :].rearrange("p (g e) -> p g e", g=4),
                             goh[:, t, :].unsqueeze(2).to_broadcast([P, 4, 4]),
                             wts[:, t, :].unsqueeze(1).to_broadcast([P, 4, 4]), ALU.mult))

    wait(k.gemm_done, "places")
    places = k.bank_of["places",]
    v.tensor_copy(k.places, places[:, 0:32])
    v.tensor_reduce(k.longest, places[:, 32:48], X_AXIS, ALU.max).then_inc(k.places_read.sem, k.places_read.step())
    wait(k.places_read)
    v.tensor_scalar(k.crowded, k.longest, float(CAP), None, ALU.is_gt).then_inc(k.crowded_ready.sem, k.crowded_ready.step())

    def lists(p, first):
        if not first:
            dve.wait_ge(k.pair_gathered, 2 * p)
            dve.wait_ge(k.pair_turned, p)
        for t in range(TT):
            for j in range(2):
                e = 2 * p + j
                place = k.places[:, bass.ds(16 * t + e, 1)]
                v.tensor_scalar(k.lists[:, t, j, :], k.iota, place, k.selected[:, t, bass.ds(e, 1)], ALU.is_equal, ALU.mult)
                ins = v.tensor_scalar(k.weighted[:, t, j, :], k.iota, place, k.combine[:, t, bass.ds(e, 1)], ALU.is_equal,
                                      ALU.mult)
        ins.then_inc(k.pair_lists, 1)

    def tokens_out(p):
        for j in range(2):
            dve.wait_ge(k.pair_gathered, 2 * p + j + 1)
            v.tensor_tensor(k.tokens[:, j, :, :], k.all_banks[4 + j].rearrange("p (c n) -> p c n", c=KT_D),
                            col("ffn_norm", 0, 8).unsqueeze(2).to_broadcast([P, KT_D, CAP]), ALU.mult).then_inc(k.pair_tokens, 1)

    def expert_pair(p, first, last):
        if not last:
            lists(p + 1, False)
        for j in range(2):
            dve.wait_ge(k.pair_up, 2 * p + j + 1)
            dve.wait_ge(k.pair_silu, 2 * p + j + 1)
            v.tensor_tensor(k.pair_h[:, j, :, :], k.pair_g.rearrange("p (c n) -> p c n", c=4),
                            k.all_banks[1][:, 0:4 * CAP].rearrange("p (c n) -> p c n", c=4), ALU.mult)\
                .then_inc(k.pair_hidden, 1)
        if not last:
            tokens_out(p + 1)
        for g in range(4):
            t, half = g // 2, g % 2
            dve.wait_ge(k.pair_spread, 4 * p + g + 1)
            if not first:
                dve.wait_ge(k.pair_summed, 4 * p + g - 3)
            at = k.x_rows[:, t, 512 * half:512 * half + 512]
            v.tensor_tensor(at, at, k.all_banks[6 + g % 2], ALU.add).then_inc(k.pair_summed, 1)

    def expert(e, first):
        for pair in range(2):
            dve.wait_ge(k.moe_up, 2 * e + pair + 1)
            dve.wait_ge(k.moe_silu, 2 * e + pair + 1)
            if not first and pair == 0:
                dve.wait_ge(k.moe_down, 4 * e)
            v.tensor_tensor(k.hidden[:, 2 * pair:2 * pair + 2, :], k.moe_g[:, pair, :].rearrange("p (f t) -> p f t", f=2),
                            k.all_banks[2 + pair].rearrange("p (f t) -> p f t", f=2), ALU.mult).then_inc(k.moe_hidden, 1)
        for t in range(TT):
            for half in range(2):
                g = 2 * t + half
                dve.wait_ge(k.moe_down, 4 * e + g + 1)
                if not first:
                    dve.wait_ge(k.moe_added, 4 * e + g - 3)
                at = k.x_rows[:, t, 512 * half:512 * half + 512]
                v.scalar_tensor_tensor(out=at, in0=k.all_banks[4 + g], scalar=k.combine[:, t, bass.ds(e, 1)], in1=at,
                                       op0=ALU.mult, op1=ALU.add).then_inc(k.moe_added, 1)

    crowded = read_crowded(dve, k)
    with dve.If(crowded == 0):
        lists(0, True)
        tokens_out(0)
        expert_pair(0, True, False)
        with dve.Fori(1, N_EXPERTS // 2 - 1) as p:
            expert_pair(p, False, False)
        expert_pair(N_EXPERTS // 2 - 1, False, True)
        dve.wait_ge(k.pair_summed, 2 * N_EXPERTS)
    with dve.Else():
        expert(0, True)
        expert(1, False)
        with dve.Fori(1, N_EXPERTS // 2) as i:
            for j in range(2):
                expert(2 * i + j, False)
        dve.wait_ge(k.moe_added, 4 * N_EXPERTS)

    dve.wait_ge(k.final_norm_loaded, 16)
    wait(k.turned, "moe", TT - 1, 1)
    for t in range(TT):
        xt = k.x_rows[:, t, :]
        then(v.tensor_tensor_reduce(out=k.xn[:, t, :], in0=xt, in1=xt, scale=1.0, scalar=0.0, op0=ALU.mult, op1=ALU.add,
                                    accum_out=k.ss[:, 0:1]))
        rstd(k.ss[:, 0:1], D, "final", t)
        then(v.scalar_tensor_tensor(out=xt, in0=xt, scalar=k.ss[:, 0:1], in1=k.v_flat[:, 0:D], op0=ALU.mult, op1=ALU.mult))

    dve.wait_ge(k.ctx_loaded, 16)
    all_rows = lambda t: k.ctx_rows[:, t, :] if t < 2 else k.x_rows[:, t - 2, :]
    for l in range(LAYERS):
        def row(name):
            at, n = ROWV[name]
            return k.rowv[:, at:at + n]

        dve.wait_ge(k.rowv_loaded, 16 * (l + 1))
        for n in range(2):
            then(v.tensor_tensor_reduce(out=k.lam_products, in0=row("diff_lq%d_2" % (n + 1)), in1=row("diff_lk%d_2" % (n + 1)),
                                        scale=1.0, scalar=0.0, op0=ALU.mult, op1=ALU.add, accum_out=k.lam2[:, n:n + 1]))
        lam_init = 0.8 - 0.6 * math.exp(-0.3 * l)
        v.tensor_scalar(row("diff_subln_g_2"), row("diff_subln_g_2"), 1.0 - lam_init, None, ALU.mult)\
            .then_inc(k.lam_dots.sem, k.lam_dots.step(l))
        wait(k.lam_exp, l)
        then(v.tensor_tensor(k.neg_lam, k.lam2[:, 1:2], k.lam2[:, 0:1], ALU.subtract))
        then(v.tensor_scalar(k.neg_lam, k.neg_lam, -lam_init, None, ALU.add))

        wait(k.gemm_done, "ada", l, 3)
        ada = k.bank_of["ada", l][:, 0:32].rearrange("p (f w) -> p f w", w=2)
        for who in range(2):
            then(v.tensor_tensor(k.shift[:, who, :], ada[:, 0:8, who], col("b_ada_2", 24 * l, 8), ALU.add))
            then(v.tensor_tensor(k.gain[:, who, :], ada[:, 8:16, who], col("b_ada_2", 24 * l + 8, 8), ALU.add))
            then(v.tensor_scalar(k.gain[:, who, :], k.gain[:, who, :], 1.0, None, ALU.add))
            ins = v.tensor_tensor(k.gain[:, who, :], k.gain[:, who, :], col("norm_g_2", 8 * l, 8), ALU.mult)
            if who == 0:
                then(ins)
        ins.then_inc(k.ada_ready.sem, k.ada_ready.step(l))
        wait(k.ada_ready, l)
        for t in range(4):
            norm(("h", l), t, all_rows(t))
            if t >= 1:
                who = 1 if t - 1 < 2 else 0
                ht_out(("h", l), t - 1, P * (t - 1), k.gain[:, who, :], k.shift[:, who, :])
        ht_out(("h", l), 3, P * 3, k.gain[:, 0, :], k.shift[:, 0, :])

        def head_norm(branch, part, t):
            dim = QK_DIM[branch]
            if branch == "mla":
                for half in range(2):
                    wait(k.proj_read, "mla", l, "ukv" if part == "k" else "uq", t, half)
                if part == "k":
                    rows = k.head_rows[:, t, :].rearrange("p (h d) -> p h d", h=8)
                    then(v.tensor_copy(rows[:, :, 64:96], k.ckv_rows[:, t, 256:288].unsqueeze(1).to_broadcast([P, 8, 32])))
            else:
                wait(k.proj_read, branch, l, part, t)
            group_norm(k.head_rows[:, t, 0:8 * dim].rearrange("p (h d) -> p h d", h=8), 8, dim, k.xn[:, 0, :],
                       branch, l, part, t)\
                .then_inc(k.heads_normed.sem, k.heads_normed.step(branch, l, part, t))
            wait(k.heads_normed, branch, l, part, t)

        for branch in BRANCHES:
            b = BRANCHES.index(branch)
            if branch == "mla":
                for part, kind, n, rows, dst, name in (("ckv", "kv", 256, k.ckv_rows, k.ckvt, "mla_ckv_g_2"),
                                                       ("cq", "q", 384, k.cq_rows, k.cqt, "mla_cq_g_2")):
                    for t in tiles_of(l, kind):
                        wait(k.proj_read, "mla", l, part, t)
                        xt = rows[:, t, 0:n]
                        then(v.tensor_tensor_reduce(out=k.xn[:, 0, 0:n], in0=xt, in1=xt, scale=1.0, scalar=0.0,
                                                    op0=ALU.mult, op1=ALU.add, accum_out=k.ss[:, 0:1]))
                        rstd(k.ss[:, 0:1], n, "latent", l, part, t)
                        v.tensor_scalar(xt, xt, k.ss[:, 0:1], None, ALU.mult)\
                            .then_inc(k.latent_normed.sem, k.latent_normed.step(l, part, t))
                        wait(k.latent_normed, l, part, t)
                for part, kind, n, rows, dst, name in (("ckv", "kv", 2, k.ckv_rows, k.ckvt, "mla_ckv_g_2"),
                                                       ("cq", "q", 3, k.cq_rows, k.cqt, "mla_cq_g_2")):
                    for t in tiles_of(l, kind):
                        wait(k.turned, part, l, t)
                        v.tensor_tensor(dst[:, :, P * t:P * t + P],
                                        k.bank_of[part, l, t][:, 0:P * n].rearrange("p (c t) -> p c t", c=n),
                                        col(name, n * l, n).unsqueeze(2).to_broadcast([P, n, P]), ALU.mult)\
                            .then_inc(k.latent_turned.sem, k.latent_turned.step(l, part, t))
            for t in tiles_of(l, "kv"):
                head_norm(branch, "k", t)
            for t in tiles_of(l, "q"):
                head_norm(branch, "q", t)

            todo = attention_units(l)
            vd = V_DIM[branch]

            def unit_max(n):
                t, u = todo[n]
                keys = 512 if t >= 2 else TOK
                bank = k.bank_of[branch, l, t, u]
                wait(k.scores_done, branch, l, t, u)
                v.tensor_reduce(k.nmax[:, n % 4:n % 4 + 1], bank[:, 0:keys], X_AXIS, ALU.max, negate=True)\
                    .then_inc(k.max_ready.sem, k.max_ready.step(branch, l, t, u))

            def unit_out(n):
                t, u = todo[n]
                wait(k.pv_done, branch, l, t, u)
                bank = k.bank_of["pv", branch, l, t, u][:, 0:vd]
                rs = k.rsum[:, n % 2:n % 2 + 1]
                then(v.reciprocal(rs, k.psums[:, n % 4:n % 4 + 1]))
                if branch == "diff":
                    at = k.o[:, t, vd * (u // 2):vd * (u // 2) + vd]
                    if u % 2:
                        then(v.tensor_tensor(rs, rs, k.neg_lam, ALU.mult))
                        ins = v.scalar_tensor_tensor(out=at, in0=bank, scalar=rs, in1=at, op0=ALU.mult, op1=ALU.add)
                    else:
                        ins = v.tensor_scalar(at, bank, rs, None, ALU.mult)
                else:
                    ins = v.tensor_scalar(k.o[:, t, vd * u:vd * u + vd], bank, rs, None, ALU.mult)
                ins.then_inc(k.unit_out.sem, k.unit_out.step(branch, l, t, u))
                wait(k.unit_out, branch, l, t, u)

            for n in range(len(todo) + 2):
                if n < len(todo):
                    unit_max(n)
                if n >= 2:
                    unit_out(n - 2)

            for t in tiles_of(l, "q"):
                o4 = k.o[:, t, :].rearrange("p (h d) -> p h d", h=4)
                if branch == "diff":
                    then(group_norm(o4, 4, P, k.xn[:, 0, :], "o", l, t))
                    then(v.tensor_tensor(o4, o4, row("diff_subln_g_2").unsqueeze(1).to_broadcast([P, 4, P]), ALU.mult))
                wait(k.z_read, l, b, t)
                v.tensor_tensor(k.o[:, t, :], k.o[:, t, :], k.sz[:, t % 2, :], ALU.mult)\
                    .then_inc(k.branch_gated.sem, k.branch_gated.step(l, b, t))
            for n, (half, t) in enumerate([(half, t) for half in range(2) for t in tiles_of(l, "q")]):
                at = k.y[:, t, 512 * half:512 * half + 512]
                wait(k.gm_read, l, b, half, t)
                wait(k.gemm_done, "br", l, b, half, t)
                bank = k.bank_of["br", l, b, half, t]
                if b == 0:
                    ins = v.tensor_tensor(at, bank, k.sg[:, n % 2, :], ALU.mult)
                else:
                    then(v.tensor_tensor(k.sg[:, n % 2, :], bank, k.sg[:, n % 2, :], ALU.mult))
                    ins = v.tensor_tensor(at, at, k.sg[:, n % 2, :], ALU.add)
                ins.then_inc(k.merged.sem, k.merged.step(l, b, half, t))

        wait(k.turned, "o", l, 2, 3)
        for who in range(2):
            ins = v.tensor_copy(k.sc_wide[:, who, :, :], k.sc[:, :, who].unsqueeze(2).to_broadcast([P, 8, P]))
        ins.then_inc(k.spread_c.sem, k.spread_c.step(l))
        dve.wait_ge(k.gate_bias_loaded, 32 if l == 0 else 48)
        for n in (4, 5):
            for who in (["ctx", "x"] if l == 0 else ["x"]):
                wait(k.gemm_done, "gate", l, n, who)
                at = k.gates[:, 0 if who == "x" else 1, 512 * (n - 4):512 * (n - 4) + 512]
                v.tensor_tensor(at, at, k.bank_of["gate", l, n, who], ALU.add)\
                    .then_inc(k.gate_ready.sem, k.gate_ready.step(l, n, who))
        wait(k.gate_ready, l, 5, "x")
        for half in range(2):
            for t in tiles_of(l, "q"):
                wait(k.gemm_done, "out", l, half, t)
                wait(k.turned, "y", l, t, half)
                tmp = k.y[:, t, 512 * half:512 * half + 512]
                at = all_rows(t)[:, 512 * half:512 * half + 512]
                then(v.tensor_tensor(tmp, k.bank_of["out", l, half, t],
                                     k.gates[:, 0 if t >= 2 else 1, 512 * half:512 * half + 512], ALU.mult))
                v.tensor_tensor(at, at, tmp, ALU.add).then_inc(k.layer_done.sem, k.layer_done.step("x", l, t, half))
        wait(k.layer_done, "x", l, 3, 1)



def gpsimd_program(pool, k):
    nc = k.nc
    g = nc.gpsimd

    def wait(signal, *key):
        pool.wait_ge(signal.sem, signal.at(*key))

    def then(ins):
        ins.then_inc(k.gpsimd_steps.sem, k.gpsimd_steps.step(k.gpsimd_steps.count))
        pool.wait_ge(k.gpsimd_steps.sem, k.gpsimd_steps.count)

    then(g.memset(k.minus_half, -0.5))

    def power(groups, *key):
        wait(k.mean_squares, *key)
        g.tensor_tensor(k.ss[:, 0:groups], k.ss[:, 0:groups], k.minus_half[:, 0:groups], ALU.pow)\
            .then_inc(k.rstd_ready.sem, k.rstd_ready.step(*key))

    for what in ("mixer", "mem"):
        for t in range(TT):
            power(1, what, t)
    wait(k.kk_ready)
    wait(k.mix_read, 3, 1)
    for n, size in enumerate(LEVELS):
        wait(k.level_exp, n)
        if n >= 2:
            wait(k.scores_done, "level", n - 2, 0 if n == 2 else 1)
        half = lambda ap, side: ap.rearrange("p (b two s) -> p b two s", two=2, s=size)[:, :, side, :]
        out = k.level[:, n % 2, :]
        g.tensor_tensor(half(out, 0), half(k.level_e, 0), half(k.kk, 0), ALU.mult)
        g.tensor_tensor(half(out, 1), half(k.level_e, 1), half(k.qq, 1), ALU.mult)\
            .then_inc(k.level_ready.sem, k.level_ready.step(n))
    for what in ("hgrn", "cross", "moe", "final"):
        for t in range(TT):
            power(HEADS1 if what == "hgrn" else 1, what, t)

    for l in range(LAYERS):
        for t in range(4):
            power(1, ("h", l), t)
        pool.wait_ge(k.bias_loaded, 16 * 32 * (l + 1))
        mask = k.colmask.unsqueeze(1).to_broadcast([P, 32, 64])
        for t in range(TT):
            rows = k.bias[:, t, :, :].rearrange("p h (a b) -> p (h a) b", b=64)
            ins = g.tensor_tensor(rows, rows, mask, ALU.add)
        ins.then_inc(k.bias_ready.sem, k.bias_ready.step(l))
        pool.wait_ge(k.rowv_loaded, 16 * (l + 1))

        def finish_heads(branch, part, t):
            dim = QK_DIM[branch]
            at, n = ROWV["%s_%s_g_2" % (branch, part)]
            power(8, branch, l, part, t)
            wait(k.heads_normed, branch, l, part, t)
            rows = k.head_rows[:, t, 0:8 * dim].rearrange("p (h d) -> p h d", h=8)
            ins = g.tensor_tensor(rows, rows, k.rowv[:, at:at + n].unsqueeze(1).to_broadcast([P, 8, dim]), ALU.mult)
            if branch != "na" and t >= 2:
                then(ins)
                half = ROPE[branch] // 2
                x1, x2 = rows[:, :, dim - 2 * half:dim - half], rows[:, :, dim - half:dim]
                cs, sn = (getter[:, (t - 2) * half:(t - 1) * half].unsqueeze(1).to_broadcast([P, 8, half])
                          for getter in ((k.cos_mla, k.sin_mla) if branch == "mla" else (k.cos_diff, k.sin_diff)))
                tmp = k.rope_tmp[:, 0:4 * 8 * half].rearrange("p (n h d) -> p n h d", n=4, h=8)
                for i, (a, f) in enumerate([(x1, cs), (x2, sn), (x2, cs), (x1, sn)]):
                    ins = g.tensor_tensor(tmp[:, i], a, f, ALU.mult)
                then(ins)
                g.tensor_tensor(x1, tmp[:, 0], tmp[:, 1], ALU.subtract)
                ins = g.tensor_tensor(x2, tmp[:, 2], tmp[:, 3], ALU.add)
            ins.then_inc(k.heads_ready.sem, k.heads_ready.step(branch, l, part, t))
            wait(k.heads_ready, branch, l, part, t)

        for branch in BRANCHES:
            if branch == "mla":
                for part, kind in (("ckv", "kv"), ("cq", "q")):
                    for t in tiles_of(l, kind):
                        power(1, "latent", l, part, t)
            for t in tiles_of(l, "kv"):
                finish_heads(branch, "k", t)
            for t in tiles_of(l, "q"):
                finish_heads(branch, "q", t)
        for t in tiles_of(l, "q"):
            power(4, "o", l, t)



def build_program(nc, w, book):
    with ExitStack() as stack:
        def sb(name, cols):
            return stack.enter_context(nc.sbuf_tensor(name, [P, cols], F32))[:, :]

        def sem(name):
            return stack.enter_context(nc.semaphore(name))

        def signal(name):
            return Signal(sem(name), name, book)

        split = lambda ap, a: ap.rearrange("p (a b) -> p a b", a=a)
        k = Program()
        k.nc, k.w, k.landed, k.loads, k.bank_of = nc, w, {}, [0] * MOE_RING, book["banks"]
        k.all_banks = [stack.enter_context(nc.psum_tensor("bank%d" % n, [P, 512], F32))[:, :] for n in range(8)]
        k.banks = dict(zip(["G0", "G1", "T0", "T1", "S0", "S1", "O0", "O1"], k.all_banks))

        k.pool6 = sb("weights_qt_kt", MOE_RING * SLOT)
        qt, kt = k.pool6[:, RING * SLOT:(RING + 1) * SLOT], k.pool6[:, (RING + 1) * SLOT:]
        k.x_rows = split(sb("x_rows", TT * D), TT)
        k.ctx_rows = split(sb("ctx_rows", TT * D), TT)
        k.ht = split(sb("ht", KT_D * 512), KT_D)
        k.v_flat = sb("v", 2048)
        o_flat = sb("o", 2048)
        head = sb("head_rows", 3072)
        y_flat = sb("y", 4096)
        aux = sb("aux", 4096)
        pp = sb("probs", 2048)
        k.const = sb("const", N_CONST)
        k.cols = sb("cols", 2 * P)
        k.rowv = sb("rowv", N_ROWV)
        k.router_w = split(sb("router_w", 8 * 20), 8)
        k.router_b = sb("router_b", 20)
        small = sb("small", 512)
        k.sc = split(small[:, 0:16], 8)
        k.ss, k.nmax, k.psums, k.rsum = small[:, 16:24], small[:, 24:28], small[:, 28:32], small[:, 32:34]
        k.lam2, k.neg_lam = small[:, 34:36], small[:, 36:37]
        k.lb, k.lb_raw, k.omlb = small[:, 40:44], small[:, 44:48], small[:, 48:52]
        k.gain, k.shift = split(small[:, 56:72], 2), split(small[:, 72:88], 2)
        k.combine = split(small[:, 88:120], 2)
        k.route_ge, k.route_ee = small[:, 120:128], small[:, 128:136]
        k.route_small, k.route_pick = small[:, 136:160], small[:, 160:192]
        k.lam_products, k.minus_half = small[:, 192:256], small[:, 256:264]
        k.selected, k.places, k.longest = split(small[:, 264:296], 2), small[:, 296:328], small[:, 328:329]
        constant = lambda name: k.const[:, CONST[name][0]:sum(CONST[name])]
        k.ident, k.reverse, k.colmask, k.rank = (constant(name) for name in ("ident", "reverse", "colmask", "rank"))
        k.before, k.iota = constant("before"), constant("iota")
        k.cos_diff, k.sin_diff, k.cos_mla, k.sin_mla = (constant(name) for name in ("cos_diff", "sin_diff", "cos_mla", "sin_mla"))
        k.qt, k.kt, k.yt = split(qt, 8), split(kt, 8), split(qt, 8)
        k.v, k.o, k.y = split(k.v_flat, 4), split(o_flat, 4), split(y_flat, 4)
        k.head_rows = split(head, 4)
        k.cq_rows, k.ckv_rows = split(k.v_flat[:, 0:1536], 4), split(o_flat[:, 0:1152], 4)
        k.probs, k.probs_t = split(pp[:, 0:1024], 2), split(pp[:, 1024:2048], 2)
        k.xn = split(pp, 2)
        k.rope_tmp = pp[:, 1024:2048]
        k.bias = aux.rearrange("p (t h n) -> p t h n", t=TT, h=8)
        k.ogt, k.sz, k.sg = split(aux[:, 0:2048], 4), split(aux[:, 2048:3072], 2), split(aux[:, 3072:4096], 2)
        k.cqt, k.ckvt = split(aux[:, 0:1536], 3), split(aux[:, 1536:2560], 2)
        k.gates = split(k.v_flat, 2)
        k.sc_wide = o_flat.rearrange("p (w c n) -> p w c n", w=2, c=8)
        k.qq, k.kk, k.b, k.lf = (qt[:, 1024 * n:1024 * n + 1024] for n in range(4))
        k.level = split(kt[:, 0:2048], 2)
        k.level_d, k.level_e = kt[:, 2048:3072], kt[:, 3072:4096]
        k.near_scores, k.far_scores = y_flat[:, 0:1024], y_flat[:, 1024:1536]
        k.conv_in = split(y_flat[:, 1536:1536 + 4 * (TOK + 2)], 4)
        k.ones = y_flat[:, 2688:2816]
        k.conv, k.silu_g, k.cc = split(head[:, 0:1024], 4), head[:, 1024:2048], head[:, 2048:3072]
        k.t_out, k.masks = split(aux[:, 0:2048], 8), aux[:, 2048:3072]
        k.col_rows = split(aux[:, 3072:3328], 2)
        k.cross_q, k.cross_k, k.cross_v = split(qt[:, 0:2048], 8), split(kt[:, 0:2048], 8), split(y_flat[:, 0:2048], 2)
        k.hidden, k.moe_g = split(aux[:, 0:1024], 4), split(aux[:, 1024:2048], 2)
        k.route = aux[:, 3328:3968]
        k.tokens = head[:, 0:1024].rearrange("p (j c n) -> p j c n", j=2, c=KT_D)
        k.down_rows = head[:, 1024:2048]
        k.lists = head[:, 2048:2304].rearrange("p (t j n) -> p t j n", t=TT, j=2)
        k.weighted = head[:, 2304:2560].rearrange("p (t j n) -> p t j n", t=TT, j=2)
        k.weighted_t, k.pair_g = head[:, 2560:2816], head[:, 2816:3072]
        k.pair_h = y_flat[:, 0:512].rearrange("p (j c n) -> p j c n", j=2, c=4)
        k.crowded = stack.enter_context(nc.sbuf_tensor("crowded", [P, 1], mybir.dt.int32))[:, :]

        k.x_loaded = sem("x_loaded")
        k.small_loaded = sem("small_loaded")
        k.masks_loaded = sem("masks_loaded")
        k.mem_loaded = sem("mem_loaded")
        k.router_loaded = sem("router_loaded")
        k.ctx_loaded = sem("ctx_loaded")
        k.rowv_loaded = sem("rowv_loaded")
        k.bias_loaded = sem("bias_loaded")
        k.gate_bias_loaded = sem("gate_bias_loaded")
        k.final_norm_loaded = sem("final_norm_loaded")
        k.stored = sem("stored")
        k.slot_loaded = [sem("slot_loaded%d" % n) for n in range(MOE_RING)]
        k.moe_gate = sem("moe_gate")
        k.moe_silu = sem("moe_silu")
        k.moe_up = sem("moe_up")
        k.moe_hidden = sem("moe_hidden")
        k.moe_down = sem("moe_down")
        k.moe_added = sem("moe_added")
        k.pair_lists = sem("pair_lists")
        k.pair_gathered = sem("pair_gathered")
        k.pair_tokens = sem("pair_tokens")
        k.pair_turned = sem("pair_turned")
        k.pair_weights = sem("pair_weights")
        k.pair_gate = sem("pair_gate")
        k.pair_silu = sem("pair_silu")
        k.pair_up = sem("pair_up")
        k.pair_hidden = sem("pair_hidden")
        k.pair_down = sem("pair_down")
        k.pair_rows = sem("pair_rows")
        k.pair_spread = sem("pair_spread")
        k.pair_summed = sem("pair_summed")
        k.gemm_done = signal("gemm_done")
        k.turned = signal("turned")
        k.scores_done = signal("scores_done")
        k.pv_done = signal("pv_done")
        k.silu_c = signal("silu_c")
        k.lb_ready = signal("lb_ready")
        k.mix_read = signal("mix_read")
        k.logf_ready = signal("logf_ready")
        k.level_exp = signal("level_exp")
        k.cross_read = signal("cross_read")
        k.probs_ready = signal("probs_ready")
        k.probs_turned = signal("probs_turned")
        k.cross_out = signal("cross_out")
        k.route_exp = signal("route_exp")
        k.lam_exp = signal("lam_exp")
        k.proj_read = signal("proj_read")
        k.heads_turned = signal("heads_turned")
        k.z_read = signal("z_read")
        k.branch_turned = signal("branch_turned")
        k.gm_read = signal("gm_read")
        k.y_turned = signal("y_turned")
        k.cols_ready = signal("cols_ready")
        k.lb_diff = signal("lb_diff")
        k.norm_rows = signal("norm_rows")
        k.ht_ready = signal("ht_ready")
        k.f_ready = signal("f_ready")
        k.kk_ready = signal("kk_ready")
        k.level_diff = signal("level_diff")
        k.scores_taken = signal("scores_taken")
        k.conv_read = signal("conv_read")
        k.mean_squares = signal("mean_squares")
        k.hgrn_out = signal("hgrn_out")
        k.hgrn_normed = signal("hgrn_normed")
        k.yt_ready = signal("yt_ready")
        k.x_added = signal("x_added")
        k.max_ready = signal("max_ready")
        k.probs_scaled = signal("probs_scaled")
        k.routed = signal("routed")
        k.picked = signal("picked")
        k.places_read = signal("places_read")
        k.crowded_ready = signal("crowded_ready")
        k.route_diff = signal("route_diff")
        k.lam_dots = signal("lam_dots")
        k.ada_ready = signal("ada_ready")
        k.heads_normed = signal("heads_normed")
        k.latent_normed = signal("latent_normed")
        k.latent_turned = signal("latent_turned")
        k.unit_out = signal("unit_out")
        k.branch_gated = signal("branch_gated")
        k.merged = signal("merged")
        k.spread_c = signal("spread_c")
        k.gate_ready = signal("gate_ready")
        k.layer_done = signal("layer_done")
        k.vector_steps = signal("vector_steps")
        k.level_ready = signal("level_ready")
        k.rstd_ready = signal("rstd_ready")
        k.bias_ready = signal("bias_ready")
        k.heads_ready = signal("heads_ready")
        k.gpsimd_steps = signal("gpsimd_steps")

        with nc.Block() as block:
            @block.sync
            def _(sp):
                load_program(sp, k)

            @block.tensor
            def _(pe):
                tensor_program(pe, k)

            @block.scalar
            def _(act):
                scalar_program(act, k)

            @block.vector
            def _(dve):
                vector_program(dve, k)

            @block.gpsimd
            def _(pool):
                gpsimd_program(pool, k)



INPUTS = ["x", "mem", "w_in", "w_out", "w_q", "w_kv", "w_o", "w_group", "w_expert", "b_group", "b_expert", "final_norm",
          "ctx_2", "w_ada_2", "b_ada_2", "w_in_2", "w_uq_2", "w_ukv_2", "w_br_2", "w_out_2"]
FLAT = {"w_gate": "w_gate_flat", "w_up": "w_up_flat", "w_down": "w_down_flat"}


def shape_constants():
    import numpy as np
    const = np.zeros((P, N_CONST), np.float32)

    def put(name, value):
        at, n = CONST[name]
        const[:, at:at + n] = value
    put("ident", np.eye(P))
    grid_w, win = 64, 16
    put("reverse", np.kron(np.eye(2), np.eye(grid_w)[::-1]))
    q = grid_w - 1 - np.arange(P) % grid_w
    start = np.clip(q - win // 2, 0, grid_w - win)
    key = np.arange(grid_w)
    inside = (key[None] >= start[:, None]) & (key[None] < start[:, None] + win)
    put("colmask", np.where(inside, 0.0, -1e30))
    token = np.arange(TOK)
    for name, rot in (("diff", ROPE["diff"]), ("mla", ROPE["mla"])):
        n = rot // 4
        inv = (np.float32(10000.0) ** (-np.arange(n, dtype=np.float32) / np.float32(n))).astype(np.float32)
        row, column = (token // grid_w).astype(np.float32), (token % grid_w).astype(np.float32)
        ang = np.concatenate([row[:, None] * inv, column[:, None] * inv], axis=-1).astype(np.float32)
        for what, f in (("cos", np.cos), ("sin", np.sin)):
            put(what + "_" + name, f(ang).astype(np.float32).reshape(TT, P, rot // 2).transpose(1, 0, 2).reshape(P, -1))
    put("rank", [4.0, 3.0, 2.0, 1.0])
    put("before", np.triu(np.ones((P, P)), 1))
    put("iota", np.arange(CAP))
    s, t = np.arange(P)[:, None], np.arange(P)[None]
    masks = [(s // (2 * n) == t // (2 * n)) & (s % (2 * n) < n) & (t % (2 * n) >= n) for n in LEVELS[1:]] + [s == t]
    return const, np.concatenate([m.astype(np.float32) for m in masks], axis=1)


def kernel(**inputs):
    import numpy as np
    import concourse.bacc as bacc
    from concourse.bass_utils import run_bass_kernel_spmd

    arrays = {name: np.ascontiguousarray(inputs[name]) for name in INPUTS}
    for name, flat in FLAT.items():
        a = np.ascontiguousarray(inputs[name])
        arrays[flat] = a.reshape(-1, a.shape[-1])
    col_vecs = np.zeros((2 * P, P), np.float32)
    for name, at in COLS.items():
        rows = np.asarray(inputs[name]).reshape(-1, P)
        col_vecs[at:at + rows.shape[0]] = rows
    arrays["col_vecs"] = col_vecs
    arrays["row_vecs"] = np.concatenate([np.asarray(inputs[name]).reshape(LAYERS, -1) for name in ROWV], axis=1)
    rpb = np.zeros((LAYERS, 8, 15, 127), np.float32)
    rpb[:, :, :, 48:79] = np.asarray(inputs["na_rpb_2"])
    arrays["rpb"] = rpb
    arrays["const"], arrays["masks"] = shape_constants()

    book = {"before": None, "now": {}, "banks": {}}
    for last in (False, True):
        nc = bacc.Bacc("TRN2", target_bir_lowering=False, num_devices=1)
        w = {}
        for name, a in arrays.items():
            w[name] = nc.dram_tensor("in_" + name, a.shape, F32, kind="ExternalInput").ap()
        w["out"] = nc.dram_tensor("out_0", (1, TOK, D), F32, kind="ExternalOutput").ap()
        build_program(nc, w, book)
        if not last:
            book = {"before": book["now"], "now": {}, "banks": {}}
    r = run_bass_kernel_spmd(nc, [{"in_" + name: a for name, a in arrays.items()}], core_ids=[0])
    return r.results[0]["out_0"]
```

```python
from contextlib import ExitStack
import math

import concourse.bass as bass
from concourse import mybir

F32 = mybir.dt.float32
F32R = mybir.dt.float32r
U32 = mybir.dt.uint32
ALU = mybir.AluOpType
ACT = mybir.ActivationFunctionType
X_AXIS = mybir.AxisListType.X

P = 128
D = 1024
KT_D = D // P
TOK = 256
TT = TOK // P
EPS = 1e-6
N_EXPERTS = 16
SLOT = KT_D * 512
RING = 4
RING2 = 3
HALF = SLOT // 2
KT_S = KT_D // 2
CAP = 64
MOE_RING = 6
HEADS1 = 4
LEVELS = [128, 64, 32, 16, 8, 4, 2, 1]
LAYERS = 2
UNITS = 8
CONDITIONING_AT = [3, 8, 13, 18]
C_NAQ, C_NAK, C_NAV, C_CQ, C_CKV = 0, 512, 1024, 1536, 1920
C_DQ, C_DK, C_DV, C_Z, C_GM = 2208, 2720, 3232, 3744, 5280
QK_DIM = {"na": 64, "mla": 96, "diff": 64}
V_DIM = {"na": 64, "mla": 64, "diff": 128}
BRANCHES = ["na", "mla", "diff"]
ROPE = {"mla": 32, "diff": 64}

COLS = {}
_at = 0
for _name, _n in [("mix_norm", 8), ("xattn_norm", 8), ("mem_norm", 8), ("ffn_norm", 8), ("conv_w", 12),
                  ("hgrn_lb", 8), ("hgrn_norm", 4), ("norm_g_2", 16), ("mla_cq_g_2", 6), ("mla_ckv_g_2", 4),
                  ("b_ada_2", 48), ("c_2", 8), ("c_ctx_2", 8)]:
    COLS[_name] = _at
    _at += _n
N_COLS = _at
ROWV = {}
_at = 0
for _name, _n in [("na_q_g_2", 64), ("na_k_g_2", 64), ("mla_q_g_2", 96), ("mla_k_g_2", 96), ("diff_q_g_2", 64),
                  ("diff_k_g_2", 64), ("diff_subln_g_2", 128), ("diff_lq1_2", 64), ("diff_lk1_2", 64),
                  ("diff_lq2_2", 64), ("diff_lk2_2", 64)]:
    ROWV[_name] = (_at, _n)
    _at += _n
N_ROWV = _at
CONST = {}
_at = 0
for _name, _n in [("ident", 128), ("reverse", 128), ("colmask", 64), ("cos_diff", 64), ("sin_diff", 64), ("cos_mla", 32),
                  ("sin_mla", 32), ("rank", 4), ("before", 128), ("iota", 64), ("pick_x", 128), ("pick_ctx", 128)]:
    CONST[_name] = (_at, _n)
    _at += _n
N_CONST = _at


class Program:
    pass


class Signal:

    def __init__(self, sem, name, book):
        self.sem, self.name, self.count, self.book = sem, name, 0, book

    def step(self, *key):
        self.count += 1
        self.book["now"][(self.name, key)] = self.count
        return 1

    def at(self, *key):
        return self.book["before"].get((self.name, key), 1) if self.book["before"] is not None else 1


def read_crowded(engine, k):
    engine.wait_ge(k.crowded_ready.sem, k.crowded_ready.at())
    return engine.value_load(k.crowded[0:1, 0:1], min_val=0, max_val=1)


def weight_chunks(w):
    def cols(ap, c0, n):
        return ap[:, c0:c0 + n].rearrange("(k p) n -> p k n", p=P)

    before, after = [], []
    for part in [4, 3, 5, 6, 1, 2, 0]:
        before.append((("mix", part), cols(w["w_in"][0], 512 * part, 512), ("mix", part, 1)))
    for half in range(2):
        before.append((("mixout", half), cols(w["w_out"][0], 512 * half, 512), ("mixout", half, TT - 1)))
    for n in range(2):
        before.append((("xk", n), cols(w["w_kv"][0], 512 * n, 512), ("xk", n, 1)))
    for n in range(2):
        before.append((("xv", n), cols(w["w_kv"][0], D + 512 * n, 512), ("xv", n, TT - 1)))
    for n in range(2):
        before.append((("xq", n), cols(w["w_q"][0], 512 * n, 512), ("xq", n, 1)))
    for n in range(2):
        before.append((("xo", n), cols(w["w_o"][0], 512 * n, 512), ("xo", n, TT - 1)))
    for l in range(LAYERS):
        win = w["w_in_2"][l]

        def add(key, src, *last):
            after.append((key, src, last))

        def add_split(key, c0, n, *last, of=win):
            src = cols(of, c0, n)
            after.append(((*key, "s0"), src[:, 0:KT_S, :], ("first", *key)))
            after.append(((*key, "s1"), src[:, KT_S:KT_D, :], last))

        def add_conditioning(l, numbers):
            for n in numbers:
                add(("ada", l, n), cols(w["w_ada_2"][l], 512 * n, 512), "ada", l, n)

        if l == 0:
            add_conditioning(l, range(4))
        for b, branch in enumerate(BRANCHES):
            if branch == "mla":
                add_split(("mla", l, "ckv"), C_CKV, 288, "mla", l, "ckv", 3)
                add_split(("mla", l, "cq"), C_CQ, 384, "mla", l, "cq", 3)
                add_split(("z", l, b), C_Z + 512 * b, 512, "z", l, b, 3)
                add(("mla", l, "ukv"), cols(w["w_ukv_2"][l], 0, 1024), "mla", l, "ukv", 3, 1)
                add(("mla", l, "uq"), cols(w["w_uq_2"][l], 0, 768), "mla", l, "uq", 3, 1)
            else:
                for part, c0 in zip("kvq", (C_NAK, C_NAV, C_NAQ) if branch == "na" else (C_DK, C_DV, C_DQ)):
                    add_split((branch, l, part), c0, 512, branch, l, part, 3)
                add_split(("z", l, b), C_Z + 512 * b, 512, "z", l, b, 3)
            if branch == "diff" and l + 1 < LAYERS:
                add_conditioning(l + 1, range(4))
            for half in range(2):
                add_split(("gm", l, b, half), C_GM + 1024 * b + 512 * half, 512, "gm", l, b, half, 3)
        add_conditioning(l, range(4, 6))
        for half in range(2):
            add_split(("out", l, half), 512 * half, 512, "out", l, half, 3, of=w["w_out_2"][l])
    return before, after


def tiles_of(l, what):
    return [0, 1, 2, 3] if l < LAYERS - 1 or what == "kv" else [2, 3]


def attention_units(l):
    return [(t, u) for t in tiles_of(l, "q") for u in range(UNITS)]



def load_program(sp, k):
    w = k.w
    before, after = weight_chunks(w)

    def load(n, chunks, ring):
        key, src, _ = chunks[n]
        slot = n % ring
        if n >= ring:
            sp.wait_ge(k.gemm_done.sem, k.gemm_done.at(*chunks[n - ring][2]))
        dst = k.pool6[:, slot * SLOT:slot * SLOT + src.shape[1] * src.shape[2]]
        k.loads[slot] += 1
        k.landed[key] = (slot, 16 * k.loads[slot])
        k.chunk_floats[key] = src.shape[1] * src.shape[2]
        sp.dma_start(dst.rearrange("p (k n) -> p k n", k=src.shape[1]), src).then_inc(k.slot_loaded[slot], 16)

    sp.dma_start(k.x_rows, w["x"][0].rearrange("(t p) d -> p t d", p=P)).then_inc(k.x_loaded, 16)
    sp.dma_start(k.const, w["const"]).then_inc(k.small_loaded, 16)
    sp.dma_start(k.col_rows, w["col_vecs"].rearrange("(t p) d -> p t d", p=P)).then_inc(k.small_loaded, 16)
    load(0, before, RING)
    sp.dma_start(k.masks, w["masks"]).then_inc(k.masks_loaded, 16)
    load(1, before, RING)
    sp.dma_start(k.ctx_rows, w["mem"][0].rearrange("(t p) d -> p t d", p=P)).then_inc(k.mem_loaded, 16)
    sp.dma_start(k.router_w[:, :, 0:4], w["w_group"][0].rearrange("(k p) n -> p k n", p=P)).then_inc(k.router_loaded, 16)
    sp.dma_start(k.router_w[:, :, 4:20], w["w_expert"][0].rearrange("(k p) n -> p k n", p=P)).then_inc(k.router_loaded, 16)
    sp.dma_start(k.router_b[:, 0:4], w["b_group"].partition_broadcast(P)[:, 0, :]).then_inc(k.router_loaded, 16)
    sp.dma_start(k.router_b[:, 4:20], w["b_expert"].partition_broadcast(P)[:, 0, :]).then_inc(k.router_loaded, 16)
    for n in range(2, len(before)):
        load(n, before, RING)

    def expert_src(e, part):
        if part == 2:
            return w["w_down_flat"][bass.ds(e * 512, 512), :].rearrange("(k p) n -> p k n", p=P)
        return [w["w_gate_flat"], w["w_up_flat"]][part][bass.ds(e * D, D), :].rearrange("(k p) n -> p k n", p=P)

    def load_expert(e, j, part):
        slot = 3 * j + part
        kt = 4 if part == 2 else KT_D
        dst = k.pool6[:, slot * SLOT:(slot + 1) * SLOT].rearrange("p (k n) -> p k n", k=kt)
        sp.dma_start(dst, expert_src(e, part)).then_inc(k.slot_loaded[slot], 16)

    for slot in range(MOE_RING):
        if slot < RING:
            held = [n for n in range(len(before)) if n % RING == slot][-1]
            sp.wait_ge(k.gemm_done.sem, k.gemm_done.at(*before[held][2]))
        else:
            sp.wait_ge(k.scores_done.sem, k.scores_done.at("x", TT - 1, HEADS1 - 1))
        load_expert(slot // 3, slot // 3, slot % 3)
    crowded = read_crowded(sp, k)
    with sp.If(crowded == 0):
        with sp.Fori(1, N_EXPERTS // 2) as p:
            sp.wait_ge(k.pair_gate, p)
            for j in range(2):
                load_expert(2 * p + j, j, 0)
            sp.wait_ge(k.pair_up, p)
            for j in range(2):
                load_expert(2 * p + j, j, 1)
            sp.wait_ge(k.pair_down, p)
            for j in range(2):
                load_expert(2 * p + j, j, 2)
        sp.wait_ge(k.pair_down, N_EXPERTS // 2)
    with sp.Else():
        with sp.Fori(1, N_EXPERTS // 2) as i:
            for j in range(2):
                sp.wait_ge(k.moe_gate, 4 * i + 2 * j - 2)
                load_expert(2 * i + j, j, 0)
                sp.wait_ge(k.moe_up, 4 * i + 2 * j - 2)
                load_expert(2 * i + j, j, 1)
                sp.wait_ge(k.moe_down, 8 * i + 4 * j - 4)
                load_expert(2 * i + j, j, 2)
        sp.wait_ge(k.moe_down, 4 * N_EXPERTS)
    k.moe_base = list(k.loads)
    for slot in range(MOE_RING):
        k.loads[slot] += N_EXPERTS // 2

    sp.wait_ge(k.norm_rows.sem, k.norm_rows.at("mem", 1))
    sp.dma_start(k.ctx_rows, w["ctx_2"][0].rearrange("(t p) d -> p t d", p=P)).then_inc(k.ctx_loaded, 16)

    def load_layer_vectors(l):
        sp.dma_start(k.rowv, w["row_vecs"][l].partition_broadcast(P)).then_inc(k.rowv_loaded, 16)

    def load_gate_bias(l):
        for who in range(2 if l == 0 else 1):
            sp.dma_start(k.gates[:, who, :], w["b_ada_2"][l, 2 * D:].partition_broadcast(P)).then_inc(k.gate_bias_loaded, 16)

    def load_bias(l):
        for t in range(TT):
            for r in range(2):
                for h in range(8):
                    at = w["rpb"][l, h, 7 - 2 * t - r, 0:1]
                    src = bass.AP(tensor=at.tensor, offset=at.offset, ap=[[1, 64], [127, 4], [1, 64]])
                    dst = k.bias[64 * r:64 * r + 64, t, h, :].rearrange("p (a b) -> p a b", a=4)
                    sp.dma_start(dst, src).then_inc(k.bias_loaded, 16)

    sp.dma_start(k.v_flat[:, 0:D], w["final_norm"].partition_broadcast(P)).then_inc(k.final_norm_loaded, 16)
    load_layer_vectors(0)
    load_bias(0)
    for n in range(len(after)):
        key = after[n][0]
        if key == ("out", 0, 1, "s0"):
            sp.wait_ge(k.merged.sem, k.merged.at(0, 2, 1, 3))
            load_layer_vectors(1)
            load_bias(1)
        if key[0] == "ada" and key[2] == 4:
            sp.wait_ge(k.pv_done.sem, k.pv_done.at("diff", key[1], 3, UNITS - 1))
            load_gate_bias(key[1])
        if key[0] == "gm" and key[3:] == (1, "s1"):
            _, l, b = key[:3]
            sp.wait_ge(k.scores_done.sem, k.scores_done.at(BRANCHES[b], l, 3, UNITS - 1))
            for half in range(2):
                src = w["w_br_2"][l, b][:, 512 * half:512 * half + 512].rearrange("(k p) n -> p k n", p=P)
                sp.dma_start(k.branch_w[:, half], src).then_inc(k.branch_w_loaded[half], 16)
        load(n, after, RING2)

    sp.wait_ge(k.layer_done.sem, k.layer_done.at("x", LAYERS - 1, 3, 1))
    sp.dma_start(w["out"][0].rearrange("(t p) d -> p t d", p=P), k.x_rows).then_inc(k.stored, 16)
    sp.wait_ge(k.stored, 16)



def tensor_program(pe, k):
    readers = {}

    def wait(signal, *key):
        pe.wait_ge(signal.sem, signal.at(*key))

    def use(bank, signal, *key):
        if bank in readers:
            wait(readers[bank][0], *readers[bank][1])
        readers[bank] = (signal, key)
        return k.banks[bank]

    def weights(key, kt, cols):
        slot, value = k.landed[key]
        pe.wait_ge(k.slot_loaded[slot], value)
        return k.pool6[:, slot * SLOT:slot * SLOT + kt * cols].rearrange("p (k n) -> p k n", k=kt)

    def split_weights(key, cols):
        if key[0] in ("na", "diff") and key[2:] in (("v", "s1"), ("q", "s0"), ("q", "s1")) or key[0] == "z" and key[2] != 1:
            wait(k.weights_split_dve, *key)
        else:
            wait(k.weights_split, *key)
        slot, _ = k.landed[key]
        parts = (k.split_ring[:, slot, HALF:HALF + KT_S * cols], k.split_ring[:, slot, 0:KT_S * cols])
        return [part.rearrange("p (k n) -> p k n", k=KT_S) for part in parts]

    wide = [0]

    def split_bank(signal, *key):
        wide[0] += 1
        return use(["G0", "G1", "O0", "O1"][wide[0] % 4], signal, *key)

    def gemm_split(key, cols, groups, middle=None, between=None, ready=None, lhs=None):
        left_hi, left_lo = lhs or (k.h_hi, k.h_lo)
        banks = {}
        for part in range(2):
            w_hi, w_lo = split_weights((*key, "s%d" % part), cols)
            for step, tile, reader in groups:
                if part == 0:
                    if ready is not None:
                        wait(*ready(tile))
                    banks[tile] = k.bank_of[step] = split_bank(*reader)
                for c in range(KT_S):
                    kt = KT_S * part + c
                    h_hi, h_lo = left_hi[:, kt, P * tile:P * tile + P], left_lo[:, kt, P * tile:P * tile + P]
                    out = banks[tile][:, 0:cols]
                    nc.tensor.matmul(out, h_hi, w_hi[:, c, :], start=(kt == 0), stop=False)
                    nc.tensor.matmul(out, h_hi, w_lo[:, c, :], start=False, stop=False)
                    mm = nc.tensor.matmul(out, h_lo, w_hi[:, c, :], start=False, stop=(kt == KT_D - 1))
                if part == 1:
                    mm.then_inc(k.gemm_done.sem, k.gemm_done.step(*step))
                    if between is not None:
                        between(tile)
            if part == 0:
                mm.then_inc(k.gemm_done.sem, k.gemm_done.step("first", *key))
                if middle is not None:
                    middle()

    turn = [0]

    def gemm_bank(signal, *key):
        turn[0] += 1
        return use("G%d" % (turn[0] % 2), signal, *key)

    def gemm_rows(key, kt, cols, lhs, groups, out_cols=None):
        wt = weights(key, kt, cols)
        for step, tile, c0, n, reader in groups:
            bank = gemm_bank(*reader)
            for c in range(kt):
                mm = nc.tensor.matmul(bank[:, 0:n], lhs(c, tile), wt[:, c, c0:c0 + n], start=(c == 0), stop=(c == kt - 1))
            k.bank_of[step] = bank
            mm.then_inc(k.gemm_done.sem, k.gemm_done.step(*step))

    def gemm_t(key, rhs, reader):
        wt = weights(key, KT_D, 512)
        for pair in range(2):
            bank = k.bank_of[(*key, pair)] = gemm_bank(*reader, pair)
            for g in range(2):
                f = 2 * pair + g
                for c in range(KT_D):
                    mm = nc.tensor.matmul(bank[:, 256 * g:256 * g + 256], wt[:, c, P * f:P * f + P], rhs(c),
                                          start=(c == 0), stop=(c == KT_D - 1))
            mm.then_inc(k.gemm_done.sem, k.gemm_done.step(*key, pair))

    flip = [0]

    def transposes(step, blocks, reader, width=P):
        flip[0] += 1
        bank = k.bank_of[step] = use("T%d" % (flip[0] % 2), *reader)
        for n, block in enumerate(blocks):
            mm = nc.tensor.transpose(bank[0:width, P * n:P * n + P], block, k.ident)
        mm.then_inc(k.turned.sem, k.turned.step(*step))

    def turn_normed(what, tile):
        wait(k.norm_rows, what, tile)
        for half in range(2):
            transposes((what, tile, half), [k.xn[:, tile % 2, P * c:P * c + P] for c in range(4 * half, 4 * half + 4)],
                       (k.ht_ready, what, tile, half))

    nc = k.nc
    xh = lambda c: k.ht[:, c, TOK:2 * TOK]
    mh = lambda c: k.ht[:, c, 0:TOK]
    tile_of_h = lambda c, t: k.ht[:, c, P * t:P * t + P]

    pe.wait_ge(k.small_loaded, 32)
    bank = use("T0", k.cols_ready)
    for n in range(2):
        mm = nc.tensor.transpose(bank[:, P * n:P * n + P], k.col_rows[:, n, :], k.ident)
    mm.then_inc(k.turned.sem, k.turned.step("cols"))

    for t in range(TT):
        turn_normed("mixer", t)
    wait(k.ht_ready, "mixer", 1, 1)

    def level_scores(n):
        size = (LEVELS + [0])[n]
        if size:
            wait(k.level_ready, n)
        else:
            wait(k.kk_ready)
        if size == 128:
            bank = use("S0", k.scores_taken, n, 0)
            for h in range(HEADS1):
                lv = k.level[:, n % 2, :].rearrange("p (h t) -> p h t", h=HEADS1)
                mm = nc.tensor.matmul(bank[:, P * h:P * h + P], lv[:, h, 0:P], lv[:, h, P:2 * P], start=True, stop=True)
            mm.then_inc(k.scores_done.sem, k.scores_done.step("level", n, 0))
            return
        for half in range(2):
            bank = use("S%d" % half, k.scores_taken, n, half)
            for b in range(4):
                at = slice(P * (4 * half + b), P * (4 * half + b) + P)
                left, right = (k.kk[:, at], k.qq[:, at]) if size == 0 else (k.level[:, n % 2, at],) * 2
                mm = nc.tensor.matmul(bank[:, P * b:P * b + P], left, right, start=True, stop=True)
            mm.then_inc(k.scores_done.sem, k.scores_done.step("level", n, half))

    gemm_t(("mix", 4), xh, (k.mix_read, 4))
    gemm_t(("mix", 3), xh, (k.mix_read, 3))
    gemm_rows(("mix", 5), KT_D, 512, lambda c, t: tile_of_h(c, 2 + t),
              [(("mix", 5, t), t, 0, 512, (k.mix_read, 5, t)) for t in range(TT)])
    for n, part in enumerate([6, 1, 2, 0]):
        level_scores(2 * n)
        level_scores(2 * n + 1)
        gemm_t(("mix", part), xh, (k.mix_read, part) if part not in (2, 0) else (k.conv_read, part))
    level_scores(len(LEVELS))
    wait(k.scores_taken, len(LEVELS), 1)
    wait(k.mix_read, 5, 1)
    for t in range(TT):
        bank = use("O%d" % t, k.hgrn_out, t)
        for h in range(HEADS1):
            out = bank[:, P * h:P * h + P]
            if t == 1:
                nc.tensor.matmul(out, k.far_scores[:, P * h:P * h + P], k.v[:, 0, P * h:P * h + P], start=True, stop=False)
            at = P * (2 * h + t)
            mm = nc.tensor.matmul(out, k.near_scores[:, at:at + P], k.v[:, t, P * h:P * h + P], start=(t == 0), stop=True)
        mm.then_inc(k.pv_done.sem, k.pv_done.step("hgrn", t))
    for t in range(TT):
        wait(k.hgrn_normed, t)
        transposes(("hgrn", t), [k.o[:, t, P * h:P * h + P] for h in range(HEADS1)], (k.yt_ready, t))
    wait(k.yt_ready, 1)
    wait(k.conv_read, 0, 1)
    for half in range(2):
        gemm_rows(("mixout", half), KT_D, 512, lambda c, t: k.t_out[:, c, P * t:P * t + P],
                  [(("mixout", half, t), t, 0, 512, (k.x_added, "mixout", half, t)) for t in range(TT)])

    for t in range(TT):
        turn_normed("mem", t)
    wait(k.ht_ready, "mem", 1, 1)
    for n in range(2):
        gemm_t(("xk", n), mh, (k.cross_read, "xk", n))
    for n in range(2):
        gemm_rows(("xv", n), KT_D, 512, tile_of_h,
                  [(("xv", n, t), t, 0, 512, (k.cross_read, "xv", n, t)) for t in range(TT)])
    for t in range(TT):
        turn_normed("cross", t)
    wait(k.ht_ready, "cross", 1, 1)
    for n in range(2):
        gemm_t(("xq", n), xh, (k.cross_read, "xq", n))
    wait(k.cross_read, "xq", 1, 1)
    units = [(t, h) for t in range(TT) for h in range(HEADS1)]

    def cross_scores(n):
        t, h = units[n]
        bank = k.bank_of["x", t, h] = use("S%d" % (n % 2), k.probs_ready, "x", t, h)
        for c in range(2):
            mm = nc.tensor.matmul(bank[:, 0:TOK], k.cross_q[:, 2 * h + c, P * t:P * t + P], k.cross_k[:, 2 * h + c, :],
                                  start=(c == 0), stop=(c == 1))
        mm.then_inc(k.scores_done.sem, k.scores_done.step("x", t, h))

    def cross_values(n):
        t, h = units[n]
        wait(k.probs_scaled, "x", t, h)
        transposes(("xp", t, h), [k.probs[:, n % 2, P * c:P * c + P] for c in range(TT)], (k.probs_turned, "x", t, h))
        wait(k.probs_turned, "x", t, h)
        bank = k.bank_of["xo_bank", t, h] = use("O%d" % (n % 2), k.cross_out, t, h)
        for f in range(2):
            for c in range(TT):
                at = 256 * h + P * f
                mm = nc.tensor.matmul(bank[:, P * f:P * f + P], k.cross_v[:, c, at:at + P],
                                      k.probs_t[:, n % 2, P * c:P * c + P], start=(c == 0), stop=(c == TT - 1))
        mm.then_inc(k.pv_done.sem, k.pv_done.step("x", t, h))

    cross_scores(0)
    for n in range(len(units)):
        if n + 1 < len(units):
            cross_scores(n + 1)
        cross_values(n)
    wait(k.cross_out, TT - 1, HEADS1 - 1)
    for n in range(2):
        gemm_rows(("xo", n), KT_D, 512, lambda c, t: k.t_out[:, c, P * t:P * t + P],
                  [(("xo", n, t), t, 0, 512, (k.x_added, "xo", n, t)) for t in range(TT)])

    for t in range(TT):
        turn_normed("moe", t)
    wait(k.ht_ready, "moe", 1, 1)
    pe.wait_ge(k.router_loaded, 64)
    bank = k.bank_of["router",] = gemm_bank(k.routed)
    for t in range(TT):
        for c in range(KT_D):
            mm = nc.tensor.matmul(bank[:, 20 * t:20 * t + 20], tile_of_h(c, 2 + t), k.router_w[:, c, :],
                                  start=(c == 0), stop=(c == KT_D - 1))
    mm.then_inc(k.gemm_done.sem, k.gemm_done.step("router"))
    wait(k.picked)
    bank = k.bank_of["places",] = gemm_bank(k.places_read)
    nc.tensor.matmul(bank[:, 0:16], k.before, k.selected[:, 0, :], start=True, stop=True)
    nc.tensor.matmul(bank[:, 16:32], k.before, k.selected[:, 1, :], start=True, stop=False)
    nc.tensor.matmul(bank[:, 16:32], k.ones, k.selected[:, 0, :], start=False, stop=True)
    nc.tensor.matmul(bank[:, 32:48], k.ones, k.selected[:, 0, :], start=True, stop=False)
    nc.tensor.matmul(bank[:, 32:48], k.ones, k.selected[:, 1, :], start=False, stop=True)\
        .then_inc(k.gemm_done.sem, k.gemm_done.step("places"))
    for bank in sorted(readers):
        wait(readers[bank][0], *readers[bank][1])
    readers.clear()
    gate_bank, up_bank, down_banks, list_banks, sum_banks = (k.all_banks[0], k.all_banks[1], k.all_banks[2:4],
                                                             k.all_banks[4:6], k.all_banks[6:8])

    def gather():
        for f in range(KT_D):
            for t in range(TT):
                mm = nc.tensor.matmul(list_banks[f // 4][:, P * (f % 4):P * (f % 4) + P], k.xn[:, t, P * f:P * f + P],
                                      k.lists[:, t, :, :].rearrange("p j n -> p (j n)"), start=(t == 0), stop=(t == TT - 1))
            if f % 4 == 3:
                mm.then_inc(k.pair_gathered, 1)

    def turn_lists(p):
        pe.wait_ge(k.pair_tokens, 2 * p + 1)
        for t in range(TT):
            mm = nc.tensor.transpose(list_banks[0][:, P * t:P * t + P], k.weighted[:, t, :, :].rearrange("p j n -> p (j n)"),
                                     k.ident)
        mm.then_inc(k.pair_turned, 1)

    def expert_pair(p, first, last):
        def w_slot(j, part, kt):
            pe.wait_ge(k.slot_loaded[3 * j + part], 16 * (p + 1 + k.moe_base[3 * j + part]))
            return k.pool6[:, (3 * j + part) * SLOT:(3 * j + part + 1) * SLOT].rearrange("p (k n) -> p k n", k=kt)

        pe.wait_ge(k.pair_tokens, 2 * p + 2)
        for part, bank, sem, freed in ((0, gate_bank, k.pair_gate, k.pair_silu), (1, up_bank, k.pair_up, k.pair_hidden)):
            wts = [w_slot(j, part, KT_D) for j in range(2)]
            if not first:
                pe.wait_ge(freed, p)
            for c in range(KT_D):
                for j in range(2):
                    mm = nc.tensor.matmul(bank[CAP * j:CAP * j + CAP, :], k.tokens[:, c, CAP * j:CAP * j + CAP], wts[j][:, c, :],
                                          start=(c == 0), stop=(c == KT_D - 1))
            mm.then_inc(sem, 1)
        if not last:
            pe.wait_ge(k.pair_lists, p + 2)
            pe.wait_ge(k.pair_weights, p + 1)
            gather()
        wts = [w_slot(j, 2, 4) for j in range(2)]
        pe.wait_ge(k.pair_hidden, p + 1)
        if not first:
            pe.wait_ge(k.pair_summed, 4 * p - 1)
        for c in range(4):
            mm = nc.tensor.transpose(sum_banks[0][:, P * c:P * c + P], k.pair_h[:, P * c:P * c + P], k.ident)
        mm.then_inc(k.pair_h_turned, 1)
        pe.wait_ge(k.pair_h_ready, p + 1)
        if not first:
            pe.wait_ge(k.pair_rows, 2 * p)
        for half in range(2):
            for c in range(4):
                for j in range(2):
                    mm = nc.tensor.matmul(down_banks[half][CAP * j:CAP * j + CAP, :], k.pair_ht[:, c, CAP * j:CAP * j + CAP],
                                          wts[j][:, c, 512 * half:512 * half + 512], start=(c == 0), stop=(c == 3))
        mm.then_inc(k.pair_down, 1)
        pe.wait_ge(k.pair_rows, 2 * p + 2)
        pe.wait_ge(k.pair_weights, p + 1)
        for g in range(4):
            half, t = g // 2, g % 2
            if g >= 2:
                pe.wait_ge(k.pair_summed, 4 * p + g - 1)
            elif not first:
                pe.wait_ge(k.pair_summed, 4 * p)
            nc.tensor.matmul(sum_banks[g % 2], k.weighted_t[:, P * t:P * t + P],
                             k.down_rows[:, 512 * half:512 * half + 512], start=True, stop=True).then_inc(k.pair_spread, 1)
        if not last:
            turn_lists(p + 1)

    def expert(e, i, j, first):
        def w_slot(part, kt):
            pe.wait_ge(k.slot_loaded[3 * j + part], 16 * (i + 1 + k.moe_base[3 * j + part]))
            return k.pool6[:, (3 * j + part) * SLOT:(3 * j + part + 1) * SLOT].rearrange("p (k n) -> p k n", k=kt)

        for part, (sem, freed) in enumerate([(k.moe_gate, k.moe_silu), (k.moe_up, k.moe_hidden)]):
            wt = w_slot(part, KT_D)
            for pair in range(2):
                if not first:
                    pe.wait_ge(freed, 2 * e + pair - 1)
                bank = k.all_banks[2 * part + pair]
                for g in range(2):
                    f = 2 * pair + g
                    for c in range(KT_D):
                        mm = nc.tensor.matmul(bank[:, TOK * g:TOK * g + TOK], wt[:, c, P * f:P * f + P], xh(c),
                                              start=(c == 0), stop=(c == KT_D - 1))
                mm.then_inc(sem, 1)
        wt = w_slot(2, 4)
        for t in range(TT):
            for half in range(2):
                g = 2 * t + half
                if not first:
                    pe.wait_ge(k.moe_added, 4 * e + g - 3)
                for c in range(4):
                    if g == 0 and c % 2 == 0:
                        pe.wait_ge(k.moe_hidden, 2 * e + c // 2 + 1)
                    mm = nc.tensor.matmul(k.all_banks[4 + g], k.hidden[:, c, P * t:P * t + P],
                                          wt[:, c, 512 * half:512 * half + 512], start=(c == 0), stop=(c == 3))
                mm.then_inc(k.moe_down, 1)

    crowded = read_crowded(pe, k)
    with pe.If(crowded == 0):
        pe.wait_ge(k.pair_lists, 1)
        gather()
        turn_lists(0)
        expert_pair(0, True, False)
        with pe.Fori(1, N_EXPERTS // 2 - 1) as p:
            expert_pair(p, False, False)
        expert_pair(N_EXPERTS // 2 - 1, False, True)
        pe.wait_ge(k.pair_summed, 2 * N_EXPERTS)
    with pe.Else():
        expert(0, 0, 0, True)
        expert(1, 0, 1, False)
        with pe.Fori(1, N_EXPERTS // 2) as i:
            for j in range(2):
                expert(2 * i + j, i, j, False)
        pe.wait_ge(k.moe_added, 4 * N_EXPERTS)

    wait(k.silu_c)
    def conditioning(l, n):
        wt = weights(("ada", l, n), KT_D, 512)
        bank = k.bank_of["ada", l, n] = gemm_bank(k.ada_rows_ready, l, n)
        for c in range(2):
            for g in range(4):
                mm = nc.tensor.matmul(bank[32 * g:32 * g + 32, :], k.sc[:, 2 * g + c, :], wt[:, 2 * g + c, :],
                                      start=(c == 0), stop=(c == 1), skip_group_check=True)
        mm.then_inc(k.gemm_done.sem, k.gemm_done.step("ada", l, n))

    def turn_conditioning(l, n):
        wait(k.ada_rows_ready, l, n)
        transposes(("ada t", l, n), [k.ada_rows[:, n % 2, P * f:P * f + P] for f in range(4)], (k.ada_taken, l, n))

    for n in range(5):
        if n < 4:
            conditioning(0, n)
        if n >= 1:
            turn_conditioning(0, n - 1)
    for l in range(LAYERS):
        for t in range(4):
            turn_normed(("h", l), t)

        def project(branch, part, kind, cols=512):
            gemm_split((branch, l, part), cols,
                       [((branch, l, part, t), t, (k.proj_read, branch, l, part, t)) for t in tiles_of(l, kind)],
                       ready=(lambda t: (k.h_split, l, t)) if (branch, part) == ("na", "k") else None)

        def turn_heads(branch, part, t):
            wait(k.heads_ready, branch, l, part, t)
            dim = QK_DIM[branch]
            for g in range(2):
                transposes((branch, l, part, t, g),
                           [k.head_rows[:, t, dim * u:dim * u + dim] for u in range(4 * g, 4 * g + 4)],
                           (k.heads_turned, branch, l, part, t, g), width=dim)

        def attention(branch):
            dim, vd = QK_DIM[branch], V_DIM[branch]
            todo = attention_units(l)

            def scores(n):
                t, u = todo[n]
                keys = 512 if t >= 2 else TOK
                bank = k.bank_of[branch, l, t, u] = use("S%d" % (n % 2), k.probs_ready, branch, l, t, u)
                biased = branch == "na" and t >= 2
                mm = nc.tensor.matmul(bank[:, 0:keys], k.qt[0:dim, u, P * t:P * t + P], k.kt[0:dim, u, 0:keys],
                                      start=True, stop=not biased)
                if biased:
                    if (t, u) == (2, 0):
                        wait(k.bias_ready, l)
                    mm = nc.tensor.matmul(bank[:, TOK:2 * TOK], k.reverse, k.bias[:, t - 2, u, :], start=False, stop=True)
                mm.then_inc(k.scores_done.sem, k.scores_done.step(branch, l, t, u))

            def turn(n):
                t, u = todo[n]
                wait(k.probs_ready, branch, l, t, u)
                transposes(("p", branch, l, t, u), [k.probs[:, n % 2, P * c:P * c + P] for c in range(4 if t >= 2 else 2)],
                           (k.probs_turned, branch, l, t, u))

            def values(n):
                t, u = todo[n]
                wait(k.probs_turned, branch, l, t, u)
                bank = k.bank_of["pv", branch, l, t, u] = use("O%d" % (n % 2), k.unit_out, branch, l, t, u)
                vc = P * (u // 2)
                last = 3 if t >= 2 else 1
                for c in range(last + 1):
                    mm = nc.tensor.matmul(bank[:, 0:P], k.probs_t[:, n % 2, P * c:P * c + P], k.v[:, c, vc:vc + P],
                                          start=(c == 0), stop=(c == last))
                mm.then_inc(k.pv_done.sem, k.pv_done.step(branch, l, t, u))

            scores(0)
            for n in range(len(todo) + 1):
                if n + 1 < len(todo):
                    scores(n + 1)
                if n < len(todo):
                    turn(n)
                if n >= 1:
                    values(n - 1)
                if branch == "diff" and l + 1 < LAYERS:
                    if n in CONDITIONING_AT:
                        conditioning(l + 1, CONDITIONING_AT.index(n))
                    if n - 1 in CONDITIONING_AT:
                        turn_conditioning(l + 1, CONDITIONING_AT.index(n - 1))

        for b, branch in enumerate(BRANCHES):
            def gate_product():
                gemm_split(("z", l, b), 512, [(("z", l, b, t), t, (k.z_read, l, b, t)) for t in tiles_of(l, "q")])

            if branch == "mla":
                project("mla", "ckv", "kv", cols=288)
                project("mla", "cq", "q", cols=384)
                gate_product()
                for part, kind, n in (("ckv", "kv", 2), ("cq", "q", 3)):
                    for t in tiles_of(l, kind):
                        wait(k.latent_normed, l, part, t)
                        src = k.ckv_rows if part == "ckv" else k.cq_rows
                        transposes((part, l, t), [src[:, t, P * c:P * c + P] for c in range(n)], (k.latent_turned, l, part, t))
                wait(k.latent_turned, l, "cq", 3)
                gemm_rows(("mla", l, "ukv"), 2, 1024, lambda c, t: k.ckvt[:, c, P * t:P * t + P],
                          [(("mla", l, "ukv", t, half), t, 512 * half, 512, (k.proj_read, "mla", l, "ukv", t, half))
                           for t in tiles_of(l, "kv") for half in range(2)])
            else:
                project(branch, "k", "kv")
                project(branch, "v", "kv")
            for t in tiles_of(l, "kv"):
                turn_heads(branch, "k", t)
            if branch == "mla":
                gemm_rows(("mla", l, "uq"), 3, 768, lambda c, t: k.cqt[:, c, P * t:P * t + P],
                          [(("mla", l, "uq", t, half), t, 384 * half, 384, (k.proj_read, "mla", l, "uq", t, half))
                           for t in tiles_of(l, "q") for half in range(2)])
            else:
                project(branch, "q", "q")
                gate_product()
            for t in tiles_of(l, "q"):
                turn_heads(branch, "q", t)
            wait(k.heads_turned, branch, l, "q", 3, 1)
            attention(branch)
            def turn_branch():
                for t in tiles_of(l, "q"):
                    wait(k.branch_gated, l, b, t)
                    transposes(("o", l, b, t), [k.o[:, t, P * c:P * c + P] for c in range(4)], (k.branch_turned, l, b, t))
                wait(k.branch_turned, l, b, 3)

            for half in range(2):
                def branch_product(t):
                    pe.wait_ge(k.branch_w_loaded[half], 16 * (len(BRANCHES) * l + b + 1))
                    bank = k.bank_of["br", l, b, half, t] = use("S%d" % (t % 2), k.merged, l, b, half, t)
                    for c in range(4):
                        mm = nc.tensor.matmul(bank, k.ogt[:, c, P * t:P * t + P], k.branch_w[:, half, c, :], start=(c == 0), stop=(c == 3))
                    mm.then_inc(k.gemm_done.sem, k.gemm_done.step("br", l, b, half, t))

                gemm_split(("gm", l, b, half), 512,
                           [(("gm", l, b, half, t), t, (k.gm_read, l, b, half, t)) for t in tiles_of(l, "q")],
                           middle=turn_branch if half == 0 else None, between=branch_product)
        for t in tiles_of(l, "q"):
            for half in range(2):
                wait(k.merged, l, 2, half, t)
                transposes(("y", l, t, half), [k.y[:, t, P * c:P * c + P] for c in range(4 * half, 4 * half + 4)],
                           (k.y_split, l, t, half))
        for n in (4, 5):
            conditioning(l, n)
            wait(k.ada_rows_ready, l, n)
            for who in (["ctx", "x"] if l == 0 else ["x"]):
                bank = k.bank_of["gate", l, n, who] = gemm_bank(k.gate_ready, l, n, who)
                nc.tensor.matmul(bank, k.pick_x if who == "x" else k.pick_ctx, k.ada_rows[:, n % 2, :], start=True, stop=True)\
                    .then_inc(k.gemm_done.sem, k.gemm_done.step("gate", l, n, who))
        for half in range(2):
            gemm_split(("out", l, half), 512,
                       [(("out", l, half, t), t, (k.layer_done, "x", l, t, half)) for t in tiles_of(l, "q")],
                       ready=(lambda t: (k.y_split, l, t, 1)) if half == 0 else None, lhs=(k.y_hi, k.y_lo))



def scalar_program(act, k):
    nc = k.nc

    def wait(signal, *key):
        act.wait_ge(signal.sem, signal.at(*key))

    def activate(out, in_, func, **more):
        return nc.scalar.activation(out, in_, func, **more)

    wait(k.cols_ready)
    for n, name in enumerate(["c_2", "c_ctx_2"]):
        ins = activate(k.sc[:, :, n], k.cols[:, COLS[name]:COLS[name] + 8], ACT.Silu)
    ins.then_inc(k.silu_c.sem, k.silu_c.step())
    wait(k.lb_diff)
    activate(k.lb, k.lb_raw, ACT.Sigmoid).then_inc(k.lb_ready.sem, k.lb_ready.step())

    for pair in range(2):
        wait(k.gemm_done, "mix", 4, pair)
        at = slice(512 * pair, 512 * pair + 512)
        bank = k.bank_of["mix", 4, pair]
        activate(k.lf[:, at], bank, ACT.Sigmoid)
        activate(k.kk[:, at], bank, ACT.Sigmoid, scale=-1.0).then_inc(k.mix_read.sem, k.mix_read.step(4, pair))
    for pair in range(2):
        wait(k.gemm_done, "mix", 3, pair)
        activate(k.qq[:, 512 * pair:512 * pair + 512], k.bank_of["mix", 3, pair], ACT.Copy)\
            .then_inc(k.mix_read.sem, k.mix_read.step(3, pair))
    wait(k.f_ready)
    activate(k.lf, k.lf, ACT.Ln).then_inc(k.logf_ready.sem, k.logf_ready.step())
    for t in range(TT):
        wait(k.gemm_done, "mix", 5, t)
        activate(k.v[:, t, :], k.bank_of["mix", 5, t], ACT.Copy).then_inc(k.mix_read.sem, k.mix_read.step(5, t))

    def level_exp(n):
        wait(k.level_diff, n)
        if n >= 1:
            wait(k.level_ready, n - 1)
        activate(k.level_e, k.level_d, ACT.Exp).then_inc(k.level_exp.sem, k.level_exp.step(n))

    for part, dst, func in [(6, k.silu_g, ACT.Silu), (1, k.cc, ACT.Copy)]:
        first = 0 if part == 6 else 2
        level_exp(first)
        level_exp(first + 1)
        for pair in range(2):
            wait(k.gemm_done, "mix", part, pair)
            activate(dst[:, 512 * pair:512 * pair + 512], k.bank_of["mix", part, pair], func)\
                .then_inc(k.mix_read.sem, k.mix_read.step(part, pair))
    for n in range(4, len(LEVELS)):
        level_exp(n)

    for n in range(2):
        for pair in range(2):
            wait(k.gemm_done, "xk", n, pair)
            f = 4 * n + 2 * pair
            activate(k.cross_k[:, f:f + 2, :].rearrange("p f t -> p (f t)"), k.bank_of["xk", n, pair], ACT.Copy)\
                .then_inc(k.cross_read.sem, k.cross_read.step("xk", n, pair))
    for n in range(2):
        for t in range(TT):
            wait(k.gemm_done, "xv", n, t)
            activate(k.cross_v[:, t, 512 * n:512 * n + 512], k.bank_of["xv", n, t], ACT.Copy)\
                .then_inc(k.cross_read.sem, k.cross_read.step("xv", n, t))
    for n in range(2):
        for pair in range(2):
            wait(k.gemm_done, "xq", n, pair)
            f = 4 * n + 2 * pair
            activate(k.cross_q[:, f:f + 2, :].rearrange("p f t -> p (f t)"), k.bank_of["xq", n, pair], ACT.Copy,
                     scale=float(D // HEADS1) ** -0.5).then_inc(k.cross_read.sem, k.cross_read.step("xq", n, pair))
    units = [(t, h) for t in range(TT) for h in range(HEADS1)]

    def cross_exp(n):
        t, h = units[n]
        wait(k.max_ready, "x", t, h)
        if n >= 2:
            wait(k.turned, "xp", *units[n - 2])
        activate(k.probs[:, n % 2, 0:TOK], k.bank_of["x", t, h][:, 0:TOK], ACT.Exp, bias=k.nmax[:, n % 4:n % 4 + 1],
                 accum_out=k.psums[:, n % 4:n % 4 + 1]).then_inc(k.probs_ready.sem, k.probs_ready.step("x", t, h))

    cross_exp(0)
    for n, (t, h) in enumerate(units):
        if n + 1 < len(units):
            cross_exp(n + 1)
        wait(k.turned, "xp", t, h)
        if n >= 2:
            wait(k.pv_done, "x", *units[n - 2])
        activate(k.probs_t[:, n % 2, 0:TOK], k.bank_of["xp", t, h][:, 0:TOK], ACT.Copy)\
            .then_inc(k.probs_turned.sem, k.probs_turned.step("x", t, h))
        wait(k.pv_done, "x", t, h)
        activate(k.t_out[:, 2 * h:2 * h + 2, P * t:P * t + P],
                 k.bank_of["xo_bank", t, h][:, 0:TOK].rearrange("p (f t) -> p f t", f=2), ACT.Copy)\
            .then_inc(k.cross_out.sem, k.cross_out.step(t, h))

    wait(k.route_diff, "group")
    activate(k.route_ge, k.route_ge, ACT.Exp).then_inc(k.route_exp.sem, k.route_exp.step("group"))
    wait(k.route_diff, "expert")
    activate(k.route_ee, k.route_ee, ACT.Exp).then_inc(k.route_exp.sem, k.route_exp.step("expert"))

    def expert(e, first):
        for pair in range(2):
            act.wait_ge(k.moe_gate, 2 * e + pair + 1)
            if not first:
                act.wait_ge(k.moe_hidden, 2 * e + pair - 1)
            activate(k.moe_g[:, pair, :], k.all_banks[pair], ACT.Silu).then_inc(k.moe_silu, 1)

    def weights_out(p):
        act.wait_ge(k.pair_turned, p + 1)
        activate(k.weighted_t, k.all_banks[4][:, 0:TOK], ACT.Copy).then_inc(k.pair_weights, 1)

    def expert_pair(p, first, last):
        act.wait_ge(k.pair_gate, p + 1)
        if not first:
            act.wait_ge(k.pair_hidden, p)
        activate(k.pair_g, k.all_banks[0], ACT.Silu).then_inc(k.pair_silu, 1)
        act.wait_ge(k.pair_h_turned, p + 1)
        activate(k.pair_ht, k.all_banks[6].rearrange("p (c n) -> p c n", c=4), ACT.Copy).then_inc(k.pair_h_ready, 1)
        act.wait_ge(k.pair_down, p + 1)
        for half in range(2):
            activate(k.down_rows[:, 512 * half:512 * half + 512], k.all_banks[2 + half], ACT.Copy).then_inc(k.pair_rows, 1)
        if not last:
            weights_out(p + 1)

    crowded = read_crowded(act, k)
    with act.If(crowded == 0):
        weights_out(0)
        expert_pair(0, True, False)
        with act.Fori(1, N_EXPERTS // 2 - 1) as p:
            expert_pair(p, False, False)
        expert_pair(N_EXPERTS // 2 - 1, False, True)
    with act.Else():
        expert(0, True)
        expert(1, False)
        with act.Fori(1, N_EXPERTS // 2) as i:
            for j in range(2):
                expert(2 * i + j, False)

    for l in range(LAYERS):

        def conditioning_rows(l, n):
            wait(k.gemm_done, "ada", l, n)
            if n >= 4:
                wait(k.turned, "ada t", min(l + 1, LAYERS - 1), n - 2)
            elif n >= 2:
                wait(k.turned, "ada t", l, n - 2)
            elif l > 0:
                wait(k.turned, "ada t", l - 1, n + 2)
            activate(k.ada_rows[:, n % 2, :], k.bank_of["ada", l, n], ACT.Copy)\
                .then_inc(k.ada_rows_ready.sem, k.ada_rows_ready.step(l, n))

        def high_parts(*keys):
            for key in keys:
                slot, value = k.landed[key]
                act.wait_ge(k.slot_loaded[slot], value)
                n = k.chunk_floats[key]
                activate(k.split_ring[:, slot, HALF:HALF + n], k.pool6[:, slot * SLOT:slot * SLOT + n], ACT.Copy)\
                    .then_inc(k.weights_high.sem, k.weights_high.step(*key))

        halves = lambda *key: [(*key, "s0"), (*key, "s1")]
        next_halves = {"na": [*halves("mla", l, "ckv"), ("mla", l, "cq", "s0")],
                       "mla": [*halves("diff", l, "k"), ("diff", l, "v", "s0")]}
        if l == 0:
            for n in range(4):
                conditioning_rows(l, n)
        high_parts(*halves("na", l, "k"))
        wait(k.lam_dots, l)
        activate(k.lam2, k.lam2, ACT.Exp).then_inc(k.lam_exp.sem, k.lam_exp.step(l))
        for t in range(4):
            wait(k.ht_ready, ("h", l), t, 1)
            activate(k.h_hi[:, :, P * t:P * t + P], k.h_new[:, t % 2], ACT.Copy)\
                .then_inc(k.h_high.sem, k.h_high.step(l, t))
        high_parts(("na", l, "v", "s0"))

        def middle_high(n, tiles, *keys):
            if n == len(tiles) // 2 - 1:
                high_parts(*keys)

        def project(branch, part, kind, *ahead):
            for n, t in enumerate(tiles_of(l, kind)):
                wait(k.gemm_done, branch, l, part, t)
                bank = k.bank_of[branch, l, part, t]
                if part == "v":
                    dst, src = k.v[:, t, :], bank
                elif part == "ckv":
                    dst, src = k.ckv_rows[:, t, :], bank[:, 0:288]
                elif part == "cq":
                    dst, src = k.cq_rows[:, t, :], bank[:, 0:384]
                else:
                    dst, src = k.head_rows[:, t, 0:512], bank
                    if part == "q" and t in tiles_of(l, "kv"):
                        wait(k.turned, branch, l, "k", t, 1)
                activate(dst, src, ACT.Copy).then_inc(k.proj_read.sem, k.proj_read.step(branch, l, part, t))
                middle_high(n, tiles_of(l, kind), *ahead)

        def gate(b):
            if b > 0:
                wait(k.merged, l, b - 1, 1, 3)
            for t in tiles_of(l, "q"):
                wait(k.gemm_done, "z", l, b, t)
                activate(k.sz[b][:, t, :], k.bank_of["z", l, b, t], ACT.Silu).then_inc(k.z_read.sem, k.z_read.step(l, b, t))

        def turn_heads(branch, part, t):
            dim = QK_DIM[branch]
            dst = k.qt if part == "q" else k.kt
            for g in range(2):
                wait(k.turned, branch, l, part, t, g)
                activate(dst[0:dim, 4 * g:4 * g + 4, P * t:P * t + P],
                         k.bank_of[branch, l, part, t, g][0:dim, :].rearrange("p (u t) -> p u t", u=4), ACT.Copy,
                         scale=float(dim) ** -0.5 if part == "q" else 1.0)\
                    .then_inc(k.heads_turned.sem, k.heads_turned.step(branch, l, part, t, g))

        for b, branch in enumerate(BRANCHES):
            if branch == "mla":
                project("mla", "ckv", "kv", ("mla", l, "cq", "s1"))
                high_parts(("z", l, b, "s0"))
                project("mla", "cq", "q", ("z", l, b, "s1"))
                gate(b)
                for t in tiles_of(l, "kv"):
                    for half in range(2):
                        wait(k.gemm_done, "mla", l, "ukv", t, half)
                        bank = k.bank_of["mla", l, "ukv", t, half].rearrange("p (h d) -> p h d", h=4)
                        activate(k.head_rows[:, t, 384 * half:384 * half + 384].rearrange("p (h d) -> p h d", h=4)[:, :, 0:64],
                                 bank[:, :, 0:64], ACT.Copy)
                        activate(k.v[:, t, 256 * half:256 * half + 256].rearrange("p (h d) -> p h d", h=4),
                                 bank[:, :, 64:128], ACT.Copy)\
                            .then_inc(k.proj_read.sem, k.proj_read.step("mla", l, "ukv", t, half))
            else:
                project(branch, "k", "kv", (branch, l, "v", "s1"))
                high_parts((branch, l, "q", "s0"))
                project(branch, "v", "kv", (branch, l, "q", "s1"))
            for t in tiles_of(l, "kv"):
                turn_heads(branch, "k", t)
            if branch == "mla":
                for t in tiles_of(l, "q"):
                    for half in range(2):
                        wait(k.gemm_done, "mla", l, "uq", t, half)
                        activate(k.head_rows[:, t, 384 * half:384 * half + 384],
                                 k.bank_of["mla", l, "uq", t, half][:, 0:384], ACT.Copy)\
                            .then_inc(k.proj_read.sem, k.proj_read.step("mla", l, "uq", t, half))
            else:
                high_parts(("z", l, b, "s0"))
                project(branch, "q", "q", ("z", l, b, "s1"))
                gate(b)
            for t in tiles_of(l, "q"):
                turn_heads(branch, "q", t)

            todo = attention_units(l)

            def exp(n):
                t, u = todo[n]
                keys = 512 if t >= 2 else TOK
                wait(k.max_ready, branch, l, t, u)
                if n >= 2:
                    wait(k.turned, "p", branch, l, *todo[n - 2])
                activate(k.probs[:, n % 2, 0:keys], k.bank_of[branch, l, t, u][:, 0:keys], ACT.Exp,
                         bias=k.nmax[:, n % 4:n % 4 + 1], accum_out=k.psums[:, n % 4:n % 4 + 1])\
                    .then_inc(k.probs_ready.sem, k.probs_ready.step(branch, l, t, u))

            def turned_probs(n):
                t, u = todo[n]
                keys = 512 if t >= 2 else TOK
                wait(k.turned, "p", branch, l, t, u)
                if n >= 2:
                    wait(k.pv_done, branch, l, *todo[n - 2])
                activate(k.probs_t[:, n % 2, 0:keys], k.bank_of["p", branch, l, t, u][:, 0:keys], ACT.Copy)\
                    .then_inc(k.probs_turned.sem, k.probs_turned.step(branch, l, t, u))

            ahead = [*halves("gm", l, b, 0), ("gm", l, b, 1, "s0")]
            last_unit = len(todo) - 1
            for n in range(len(todo) + 1):
                if n < len(todo):
                    exp(n)
                if n >= 1:
                    turned_probs(n - 1)
                if branch == "diff" and l + 1 < LAYERS:
                    if n in CONDITIONING_AT:
                        conditioning_rows(l + 1, CONDITIONING_AT.index(n))
                if n in (last_unit - 4, last_unit - 2, last_unit):
                    high_parts(ahead[(n - last_unit + 4) // 2])
            for t in tiles_of(l, "q"):
                wait(k.turned, "o", l, b, t)
                activate(k.ogt[:, :, P * t:P * t + P], k.bank_of["o", l, b, t].rearrange("p (c t) -> p c t", c=4), ACT.Copy)\
                    .then_inc(k.branch_turned.sem, k.branch_turned.step(l, b, t))
            steps = [(half, t) for half in range(2) for t in tiles_of(l, "q")]
            for n, (half, t) in enumerate(steps):
                wait(k.gemm_done, "gm", l, b, half, t)
                if n >= 2:
                    wait(k.merged, l, b, *steps[n - 2])
                activate(k.sg[:, n % 2, :], k.bank_of["gm", l, b, half, t], ACT.Sigmoid)\
                    .then_inc(k.gm_read.sem, k.gm_read.step(l, b, half, t))
                if half == 0:
                    middle_high(n, tiles_of(l, "q"), ("gm", l, b, 1, "s1"))
                elif branch != "diff":
                    middle_high(n - len(tiles_of(l, "q")), tiles_of(l, "q"), next_halves[branch][0])
            if branch != "diff":
                high_parts(*next_halves[branch][1:])
        for t in tiles_of(l, "q"):
            for half in range(2):
                wait(k.turned, "y", l, t, half)
                activate(k.y_hi[:, 4 * half:4 * half + 4, P * t:P * t + P],
                         k.bank_of["y", l, t, half].rearrange("p (c t) -> p c t", c=4), ACT.Copy)\
                    .then_inc(k.y_turned.sem, k.y_turned.step(l, t, half))
        for n in (4, 5):
            conditioning_rows(l, n)
        high_parts(*halves("out", l, 0), *halves("out", l, 1))



def vector_program(dve, k):
    nc = k.nc
    v = nc.vector

    def wait(signal, *key):
        dve.wait_ge(signal.sem, signal.at(*key))

    def then(ins):
        ins.then_inc(k.vector_steps.sem, k.vector_steps.step(k.vector_steps.count))
        dve.wait_ge(k.vector_steps.sem, k.vector_steps.count)

    xn_reader = {}

    def rstd(sums, n, *key):
        v.tensor_scalar(sums, sums, 1.0 / n, EPS, ALU.mult, ALU.add).then_inc(k.mean_squares.sem, k.mean_squares.step(*key))
        wait(k.rstd_ready, *key)

    def norm(what, tile, src):
        slot = tile % 2
        if slot in xn_reader:
            wait(k.turned, *xn_reader[slot])
        xn_reader[slot] = (what, tile, 1)
        then(v.tensor_tensor_reduce(out=k.xn[:, slot, :], in0=src, in1=src, scale=1.0, scalar=0.0, op0=ALU.mult,
                                    op1=ALU.add, accum_out=k.ss[:, 0:1]))
        rstd(k.ss[:, 0:1], D, what, tile)
        v.tensor_scalar(k.xn[:, slot, :], src, k.ss[:, 0:1], None, ALU.mult)\
            .then_inc(k.norm_rows.sem, k.norm_rows.step(what, tile))
        wait(k.norm_rows, what, tile)

    def ht_out(what, tile, at, gain, shift=None):
        for half in range(2):
            wait(k.turned, what, tile, half)
            dst = k.ht[:, 4 * half:4 * half + 4, at:at + P] if shift is None else k.h_new[:, tile % 2, 4 * half:4 * half + 4, :]
            if shift is not None and tile >= 2 and half == 0:
                wait(k.h_split, what[1], tile - 2)
            src = k.bank_of[what, tile, half].rearrange("p (c t) -> p c t", c=4)
            ins = v.tensor_tensor(dst, src, gain[:, 4 * half:4 * half + 4].unsqueeze(2).to_broadcast([P, 4, P]), ALU.mult)
            if shift is not None:
                then(ins)
                ins = v.tensor_tensor(dst, dst, shift[:, 4 * half:4 * half + 4].unsqueeze(2).to_broadcast([P, 4, P]), ALU.add)
            ins.then_inc(k.ht_ready.sem, k.ht_ready.step(what, tile, half))

    def col(name, at, n):
        return k.cols[:, COLS[name] + at:COLS[name] + at + n]

    def group_norm(x3, groups, dim, scratch, *key):
        sq = scratch[:, 0:groups * dim].rearrange("p (g d) -> p g d", g=groups)
        then(v.tensor_tensor(sq, x3, x3, ALU.mult))
        then(v.tensor_reduce(k.ss[:, 0:groups], sq, X_AXIS, ALU.add))
        rstd(k.ss[:, 0:groups], dim, *key)
        return v.tensor_tensor(x3, x3, k.ss[:, 0:groups].unsqueeze(2).to_broadcast([P, groups, dim]), ALU.mult)

    v.memset(k.ones, 1.0)
    v.memset(k.sc, 0.0)
    v.memset(k.near_scores, 0.0)
    v.memset(k.conv_in[:, :, 0:2], 0.0)
    wait(k.turned, "cols")
    v.tensor_copy(k.cols, k.banks["T0"][:, 0:2 * P]).then_inc(k.cols_ready.sem, k.cols_ready.step())
    wait(k.cols_ready)
    v.tensor_tensor(k.lb_raw, col("hgrn_lb", 0, 4), col("hgrn_lb", 4, 4), ALU.subtract)\
        .then_inc(k.lb_diff.sem, k.lb_diff.step())

    dve.wait_ge(k.x_loaded, 16)
    for t in range(TT):
        norm("mixer", t, k.x_rows[:, t, :])
    wait(k.lb_ready)
    then(v.tensor_scalar(k.omlb, k.lb, -1.0, 1.0, ALU.mult, ALU.add))
    for t in range(TT):
        ht_out("mixer", t, TOK + P * t, col("mix_norm", 0, 8))
    dve.wait_ge(k.mem_loaded, 16)
    for t in range(TT):
        norm("mem", t, k.ctx_rows[:, t, :])

    for pair in range(2):
        wait(k.mix_read, 4, pair)
        for h in (2 * pair, 2 * pair + 1):
            at = slice(TOK * h, TOK * h + TOK)
            ins = v.tensor_scalar(k.lf[:, at], k.lf[:, at], k.omlb[:, h:h + 1], k.lb[:, h:h + 1], ALU.mult, ALU.add)
    ins.then_inc(k.f_ready.sem, k.f_ready.step())
    for h in range(HEADS1):
        at = slice(TOK * h, TOK * h + TOK)
        ins = v.tensor_scalar(k.kk[:, at], k.kk[:, at], k.omlb[:, h:h + 1], None, ALU.mult)
    ins.then_inc(k.kk_ready.sem, k.kk_ready.step())
    wait(k.logf_ready)
    for n in range(2 * HEADS1):
        at = slice(P * n, P * n + P)
        ins = v.tensor_tensor_scan(k.b[:, at], k.ones, k.lf[:, at], 0.0, ALU.mult, ALU.add)
    then(ins)

    def level_diff(n):
        size = LEVELS[n]
        if n >= 1:
            wait(k.level_exp, n - 1)
        b4 = k.b.rearrange("p (b two s) -> p b two s", two=2, s=size)
        d4 = k.level_d.rearrange("p (b two s) -> p b two s", two=2, s=size)
        middle = b4[:, :, 0, size - 1:size].to_broadcast([P, 2 * HEADS1 * P // (2 * size), size])
        v.tensor_tensor(d4[:, :, 0, :], middle, b4[:, :, 0, :], ALU.subtract)
        if size == P:
            ins = v.tensor_copy(d4[:, :, 1, :], b4[:, :, 1, :])
        else:
            ins = v.tensor_tensor(d4[:, :, 1, :], b4[:, :, 1, :], middle, ALU.subtract)
        ins.then_inc(k.level_diff.sem, k.level_diff.step(n))

    def take_scores(n):
        size = (LEVELS + [0])[n]
        if size == P:
            wait(k.scores_done, "level", n, 0)
            v.tensor_copy(k.far_scores, k.banks["S0"]).then_inc(k.scores_taken.sem, k.scores_taken.step(n, 0))
            return
        mask = k.masks[:, P * (n - 1):P * n].unsqueeze(1).to_broadcast([P, 4, P])
        for half in range(2):
            wait(k.scores_done, "level", n, half)
            dst = k.near_scores[:, 512 * half:512 * half + 512].rearrange("p (b t) -> p b t", b=4)
            src = k.banks["S%d" % half].rearrange("p (b t) -> p b t", b=4)
            v.copy_predicated(dst, mask.bitcast(U32), src).then_inc(k.scores_taken.sem, k.scores_taken.step(n, half))
            wait(k.scores_taken, n, half)

    def conv_input():
        for pair in range(2):
            wait(k.gemm_done, "mix", 2, pair)
            wait(k.mix_read, 1, pair)
            f = 2 * pair
            v.tensor_tensor(k.conv_in[:, f:f + 2, 2:2 + TOK], k.bank_of["mix", 2, pair].rearrange("p (f t) -> p f t", f=2),
                            k.cc[:, TOK * f:TOK * f + 2 * TOK].rearrange("p (f t) -> p f t", f=2), ALU.mult)\
                .then_inc(k.conv_read.sem, k.conv_read.step(2, pair))
        wait(k.conv_read, 2, 1)
        for f in range(4):
            tap = lambda j: col("conv_w", 4 * j + f, 1)
            then(v.tensor_scalar(k.conv[:, f, :], k.conv_in[:, f, 0:TOK], tap(0), None, ALU.mult))
            for j in (1, 2):
                then(v.scalar_tensor_tensor(out=k.conv[:, f, :], in0=k.conv_in[:, f, j:j + TOK], scalar=tap(j),
                                            in1=k.conv[:, f, :], op0=ALU.mult, op1=ALU.add))

    dve.wait_ge(k.masks_loaded, 16)
    level_diff(0)
    level_diff(1)
    for n in range(0, len(LEVELS), 2):
        take_scores(n)
        take_scores(n + 1)
        if n + 2 < len(LEVELS):
            level_diff(n + 2)
            level_diff(n + 3)
        if n == 4:
            conv_input()
    for pair in range(2):
        wait(k.gemm_done, "mix", 0, pair)
        v.tensor_tensor(k.t_out[:, 2 * pair:2 * pair + 2, :], k.bank_of["mix", 0, pair].rearrange("p (f t) -> p f t", f=2),
                        k.conv[:, 2 * pair:2 * pair + 2, :], ALU.mult).then_inc(k.conv_read.sem, k.conv_read.step(0, pair))
    take_scores(len(LEVELS))
    for t in range(TT):
        wait(k.pv_done, "hgrn", t)
        v.tensor_copy(k.o[:, t, :], k.banks["O%d" % t]).then_inc(k.hgrn_out.sem, k.hgrn_out.step(t))
        wait(k.hgrn_out, t)
        group_norm(k.o[:, t, :].rearrange("p (h d) -> p h d", h=HEADS1), HEADS1, P, k.level_d, "hgrn", t)\
            .then_inc(k.hgrn_normed.sem, k.hgrn_normed.step(t))
        wait(k.hgrn_normed, t)
    for t in range(TT):
        wait(k.turned, "hgrn", t)
        wait(k.mix_read, 6, 1)
        for h in range(HEADS1):
            ins = v.scalar_tensor_tensor(out=k.t_out[:, 4 + h, P * t:P * t + P], in0=k.bank_of["hgrn", t][:, P * h:P * h + P],
                                         scalar=col("hgrn_norm", h, 1), in1=k.silu_g[:, TOK * h + P * t:TOK * h + P * t + P],
                                         op0=ALU.mult, op1=ALU.mult)
        ins.then_inc(k.yt_ready.sem, k.yt_ready.step(t))

    def add_to_x(what):
        for half in range(2):
            for t in range(TT):
                wait(k.gemm_done, what, half, t)
                at = k.x_rows[:, t, 512 * half:512 * half + 512]
                v.tensor_tensor(at, at, k.bank_of[what, half, t], ALU.add)\
                    .then_inc(k.x_added.sem, k.x_added.step(what, half, t))
        wait(k.x_added, what, 1, TT - 1)

    add_to_x("mixout")
    for t in range(TT):
        ht_out("mem", t, P * t, col("mem_norm", 0, 8))
        norm("cross", t, k.x_rows[:, t, :])
    for t in range(TT):
        ht_out("cross", t, TOK + P * t, col("xattn_norm", 0, 8))

    units = [(t, h) for t in range(TT) for h in range(HEADS1)]

    def cross_max(n):
        t, h = units[n]
        wait(k.scores_done, "x", t, h)
        v.tensor_reduce(k.nmax[:, n % 4:n % 4 + 1], k.bank_of["x", t, h][:, 0:TOK], X_AXIS, ALU.max, negate=True)\
            .then_inc(k.max_ready.sem, k.max_ready.step("x", t, h))

    cross_max(0)
    for n, (t, h) in enumerate(units):
        if n + 1 < len(units):
            cross_max(n + 1)
        wait(k.probs_ready, "x", t, h)
        then(v.reciprocal(k.ss[:, 0:1], k.psums[:, n % 4:n % 4 + 1]))
        v.tensor_scalar(k.probs[:, n % 2, 0:TOK], k.probs[:, n % 2, 0:TOK], k.ss[:, 0:1], None, ALU.mult)\
            .then_inc(k.probs_scaled.sem, k.probs_scaled.step("x", t, h))
        wait(k.probs_scaled, "x", t, h)
    add_to_x("xo")
    for t in range(TT):
        norm("moe", t, k.x_rows[:, t, :])
    for t in range(TT):
        ht_out("moe", t, TOK + P * t, col("ffn_norm", 0, 8))

    def bc(ap, n):
        return ap.unsqueeze(2).to_broadcast([P, TT, n])

    rank = k.rank.unsqueeze(1).to_broadcast([P, TT, 4])
    r = k.route
    lg, gp, goh, el, ep, oh1, oh2, wts, eq, ep2 = (r[:, 64 * n:64 * n + 64] for n in range(10))
    three = lambda ap: ap[:, 0:8].rearrange("p (t e) -> p t e", t=TT)
    gp, goh, el, ep, oh1, oh2, wts, eq, ep2 = (three(a) for a in (gp, goh, el, ep, oh1, oh2, wts, eq, ep2))
    lg = lg[:, 0:40].rearrange("p (t n) -> p t n", t=TT)
    small = lambda n: k.route_small[:, 2 * n:2 * n + 2]
    gmax, gsum, gbest, rm, emax, m1, m2, den, gw, esum = (small(n) for n in range(10))

    def first_best(values, best, out):
        then(v.tensor_tensor(eq, values, bc(best, 4), ALU.is_equal))
        then(v.tensor_tensor(eq, eq, rank, ALU.mult))
        then(v.tensor_reduce(rm, eq, X_AXIS, ALU.max))
        then(v.tensor_tensor(out, eq, bc(rm, 4), ALU.is_equal))

    wait(k.gemm_done, "router")
    dve.wait_ge(k.router_loaded, 64)
    v.tensor_tensor(lg, k.bank_of["router",][:, 0:40].rearrange("p (t n) -> p t n", t=TT),
                    k.router_b.unsqueeze(1).to_broadcast([P, TT, 20]), ALU.add).then_inc(k.routed.sem, k.routed.step())
    wait(k.routed)
    ge = k.route_ge.rearrange("p (t e) -> p t e", t=TT)
    ee = k.route_ee.rearrange("p (t e) -> p t e", t=TT)
    then(v.tensor_reduce(gmax, lg[:, :, 0:4], X_AXIS, ALU.max))
    v.tensor_tensor(ge, lg[:, :, 0:4], bc(gmax, 4), ALU.subtract).then_inc(k.route_diff.sem, k.route_diff.step("group"))
    wait(k.route_exp, "group")
    then(v.tensor_reduce(gsum, ge, X_AXIS, ALU.add))
    then(v.reciprocal(gsum, gsum))
    then(v.tensor_tensor(gp, ge, bc(gsum, 4), ALU.mult))
    then(v.tensor_reduce(gbest, gp, X_AXIS, ALU.max))
    first_best(gp, gbest, goh)
    for t in range(TT):
        picked = k.route_pick[:, 16 * t:16 * t + 16].rearrange("p (g e) -> p g e", g=4)
        then(v.tensor_tensor(picked, lg[:, t, 4:20].rearrange("p (g e) -> p g e", g=4),
                             goh[:, t, :].unsqueeze(2).to_broadcast([P, 4, 4]), ALU.mult))
        then(v.tensor_reduce(el[:, t, :], picked.rearrange("p g e -> p e g"), X_AXIS, ALU.add))
    then(v.tensor_reduce(emax, el, X_AXIS, ALU.max))
    v.tensor_tensor(ee, el, bc(emax, 4), ALU.subtract).then_inc(k.route_diff.sem, k.route_diff.step("expert"))
    wait(k.route_exp, "expert")
    then(v.tensor_reduce(esum, ee, X_AXIS, ALU.add))
    then(v.reciprocal(esum, esum))
    then(v.tensor_tensor(ep, ee, bc(esum, 4), ALU.mult))
    then(v.tensor_reduce(m1, ep, X_AXIS, ALU.max))
    first_best(ep, m1, oh1)
    then(v.scalar_tensor_tensor(out=ep2, in0=oh1, scalar=-2.0, in1=ep, op0=ALU.mult, op1=ALU.add))
    then(v.tensor_reduce(m2, ep2, X_AXIS, ALU.max))
    first_best(ep2, m2, oh2)
    then(v.tensor_tensor(den, m1, m2, ALU.add))
    then(v.reciprocal(den, den))
    then(v.tensor_tensor(gw, gbest, den, ALU.mult))
    then(v.tensor_tensor(ep2, oh1, oh2, ALU.add))
    for t in range(TT):
        ins = v.tensor_tensor(k.selected[:, t, :].rearrange("p (g e) -> p g e", g=4),
                              goh[:, t, :].unsqueeze(2).to_broadcast([P, 4, 4]),
                              ep2[:, t, :].unsqueeze(1).to_broadcast([P, 4, 4]), ALU.mult)
    ins.then_inc(k.picked.sem, k.picked.step())
    then(v.tensor_tensor(oh1, oh1, bc(m1, 4), ALU.mult))
    then(v.tensor_tensor(oh2, oh2, bc(m2, 4), ALU.mult))
    then(v.tensor_tensor(wts, oh1, oh2, ALU.add))
    then(v.tensor_tensor(wts, wts, bc(gw, 4), ALU.mult))
    for t in range(TT):
        then(v.tensor_tensor(k.combine[:, t, :].rearrange("p (g e) -> p g e", g=4),
                             goh[:, t, :].unsqueeze(2).to_broadcast([P, 4, 4]),
                             wts[:, t, :].unsqueeze(1).to_broadcast([P, 4, 4]), ALU.mult))

    wait(k.gemm_done, "places")
    places = k.bank_of["places",]
    v.tensor_copy(k.places, places[:, 0:32])
    v.tensor_reduce(k.longest, places[:, 32:48], X_AXIS, ALU.max).then_inc(k.places_read.sem, k.places_read.step())
    wait(k.places_read)
    v.tensor_scalar(k.crowded, k.longest, float(CAP), None, ALU.is_gt).then_inc(k.crowded_ready.sem, k.crowded_ready.step())

    def lists(p, first):
        if not first:
            dve.wait_ge(k.pair_gathered, 2 * p)
            dve.wait_ge(k.pair_turned, p)
        for t in range(TT):
            for j in range(2):
                e = 2 * p + j
                place = k.places[:, bass.ds(16 * t + e, 1)]
                v.tensor_scalar(k.lists[:, t, j, :], k.iota, place, k.selected[:, t, bass.ds(e, 1)], ALU.is_equal, ALU.mult)
                ins = v.tensor_scalar(k.weighted[:, t, j, :], k.iota, place, k.combine[:, t, bass.ds(e, 1)], ALU.is_equal,
                                      ALU.mult)
        ins.then_inc(k.pair_lists, 1)

    def tokens_out(p):
        for part in range(2):
            dve.wait_ge(k.pair_gathered, 2 * p + part + 1)
            v.tensor_tensor(k.tokens[:, 4 * part:4 * part + 4, :], k.all_banks[4 + part].rearrange("p (c n) -> p c n", c=4),
                            col("ffn_norm", 4 * part, 4).unsqueeze(2).to_broadcast([P, 4, P]), ALU.mult)\
                .then_inc(k.pair_tokens, 1)

    def expert_pair(p, first, last):
        if not last:
            lists(p + 1, False)
        dve.wait_ge(k.pair_up, p + 1)
        dve.wait_ge(k.pair_silu, p + 1)
        v.tensor_tensor(k.pair_h, k.pair_g, k.all_banks[1], ALU.mult).then_inc(k.pair_hidden, 1)
        if not last:
            tokens_out(p + 1)
        for g in range(4):
            half, t = g // 2, g % 2
            dve.wait_ge(k.pair_spread, 4 * p + g + 1)
            if not first:
                dve.wait_ge(k.pair_summed, 4 * p + g - 3)
            at = k.x_rows[:, t, 512 * half:512 * half + 512]
            v.tensor_tensor(at, at, k.all_banks[6 + g % 2], ALU.add).then_inc(k.pair_summed, 1)

    def expert(e, first):
        for pair in range(2):
            dve.wait_ge(k.moe_up, 2 * e + pair + 1)
            dve.wait_ge(k.moe_silu, 2 * e + pair + 1)
            if not first and pair == 0:
                dve.wait_ge(k.moe_down, 4 * e)
            v.tensor_tensor(k.hidden[:, 2 * pair:2 * pair + 2, :], k.moe_g[:, pair, :].rearrange("p (f t) -> p f t", f=2),
                            k.all_banks[2 + pair].rearrange("p (f t) -> p f t", f=2), ALU.mult).then_inc(k.moe_hidden, 1)
        for t in range(TT):
            for half in range(2):
                g = 2 * t + half
                dve.wait_ge(k.moe_down, 4 * e + g + 1)
                if not first:
                    dve.wait_ge(k.moe_added, 4 * e + g - 3)
                at = k.x_rows[:, t, 512 * half:512 * half + 512]
                v.scalar_tensor_tensor(out=at, in0=k.all_banks[4 + g], scalar=k.combine[:, t, bass.ds(e, 1)], in1=at,
                                       op0=ALU.mult, op1=ALU.add).then_inc(k.moe_added, 1)

    crowded = read_crowded(dve, k)
    with dve.If(crowded == 0):
        lists(0, True)
        tokens_out(0)
        expert_pair(0, True, False)
        with dve.Fori(1, N_EXPERTS // 2 - 1) as p:
            expert_pair(p, False, False)
        expert_pair(N_EXPERTS // 2 - 1, False, True)
        dve.wait_ge(k.pair_summed, 2 * N_EXPERTS)
    with dve.Else():
        expert(0, True)
        expert(1, False)
        with dve.Fori(1, N_EXPERTS // 2) as i:
            for j in range(2):
                expert(2 * i + j, False)
        dve.wait_ge(k.moe_added, 4 * N_EXPERTS)

    dve.wait_ge(k.final_norm_loaded, 16)
    wait(k.turned, "moe", TT - 1, 1)
    for t in range(TT):
        xt = k.x_rows[:, t, :]
        then(v.tensor_tensor_reduce(out=k.xn[:, t, :], in0=xt, in1=xt, scale=1.0, scalar=0.0, op0=ALU.mult, op1=ALU.add,
                                    accum_out=k.ss[:, 0:1]))
        rstd(k.ss[:, 0:1], D, "final", t)
        then(v.scalar_tensor_tensor(out=xt, in0=xt, scalar=k.ss[:, 0:1], in1=k.v_flat[:, 0:D], op0=ALU.mult, op1=ALU.mult))

    dve.wait_ge(k.ctx_loaded, 16)
    all_rows = lambda t: k.ctx_rows[:, t, :] if t < 2 else k.x_rows[:, t - 2, :]

    def take_conditioning(l, n):
        wait(k.turned, "ada t", l, n)
        groups = k.bank_of["ada t", l, n].rearrange("p (f g m) -> p f m g", f=4, g=4)[:, :, 0:2, :]
        dst = (k.shift if n < 2 else k.gain)[:, :, 4 * (n % 2):4 * (n % 2) + 4].rearrange("p w f -> p f w")
        v.tensor_reduce(dst, groups, X_AXIS, ALU.add).then_inc(k.ada_taken.sem, k.ada_taken.step(l, n))

    def finish_conditioning(l):
        wait(k.ada_taken, l, 3)
        for who in range(2):
            then(v.tensor_tensor(k.shift[:, who, :], k.shift[:, who, :], col("b_ada_2", 24 * l, 8), ALU.add))
            then(v.tensor_tensor(k.gain[:, who, :], k.gain[:, who, :], col("b_ada_2", 24 * l + 8, 8), ALU.add))
            then(v.tensor_scalar(k.gain[:, who, :], k.gain[:, who, :], 1.0, None, ALU.add))
            ins = v.tensor_tensor(k.gain[:, who, :], k.gain[:, who, :], col("norm_g_2", 8 * l, 8), ALU.mult)
            if who == 0:
                then(ins)
        ins.then_inc(k.ada_ready.sem, k.ada_ready.step(l))

    for l in range(LAYERS):
        def row(name):
            at, n = ROWV[name]
            return k.rowv[:, at:at + n]

        dve.wait_ge(k.rowv_loaded, 16 * (l + 1))
        for n in range(2):
            then(v.tensor_tensor_reduce(out=k.lam_products, in0=row("diff_lq%d_2" % (n + 1)), in1=row("diff_lk%d_2" % (n + 1)),
                                        scale=1.0, scalar=0.0, op0=ALU.mult, op1=ALU.add, accum_out=k.lam2[:, n:n + 1]))
        lam_init = 0.8 - 0.6 * math.exp(-0.3 * l)
        v.tensor_scalar(row("diff_subln_g_2"), row("diff_subln_g_2"), 1.0 - lam_init, None, ALU.mult)\
            .then_inc(k.lam_dots.sem, k.lam_dots.step(l))
        wait(k.lam_exp, l)
        then(v.tensor_tensor(k.neg_lam, k.lam2[:, 1:2], k.lam2[:, 0:1], ALU.subtract))
        then(v.tensor_scalar(k.neg_lam, k.neg_lam, -lam_init, None, ALU.add))

        if l == 0:
            for n in range(4):
                take_conditioning(l, n)
            finish_conditioning(l)
        wait(k.ada_ready, l)
        for t in range(4):
            if l == 0 or t >= 2:
                norm(("h", l), t, all_rows(t))
            if t >= 1:
                who = 1 if t - 1 < 2 else 0
                ht_out(("h", l), t - 1, P * (t - 1), k.gain[:, who, :], k.shift[:, who, :])
        ht_out(("h", l), 3, P * 3, k.gain[:, 0, :], k.shift[:, 0, :])

        def head_norm(branch, part, t):
            dim = QK_DIM[branch]
            if branch == "mla":
                for half in range(2):
                    wait(k.proj_read, "mla", l, "ukv" if part == "k" else "uq", t, half)
                if part == "k":
                    rows = k.head_rows[:, t, :].rearrange("p (h d) -> p h d", h=8)
                    then(v.tensor_copy(rows[:, :, 64:96], k.ckv_rows[:, t, 256:288].unsqueeze(1).to_broadcast([P, 8, 32])))
            else:
                wait(k.proj_read, branch, l, part, t)
            group_norm(k.head_rows[:, t, 0:8 * dim].rearrange("p (h d) -> p h d", h=8), 8, dim, k.xn[:, 0, :],
                       branch, l, part, t)\
                .then_inc(k.heads_normed.sem, k.heads_normed.step(branch, l, part, t))
            wait(k.heads_normed, branch, l, part, t)

        def low_parts(*keys):
            for key in keys:
                slot, _ = k.landed[key]
                n = k.chunk_floats[key]
                wait(k.weights_high, *key)
                v.tensor_tensor(k.split_ring[:, slot, 0:n], k.pool6[:, slot * SLOT:slot * SLOT + n],
                                k.split_ring[:, slot, HALF:HALF + n].bitcast(F32), ALU.subtract)\
                    .then_inc(k.weights_split_dve.sem, k.weights_split_dve.step(*key))

        for branch in BRANCHES:
            b = BRANCHES.index(branch)
            if branch == "mla":
                for part, kind, n, rows, dst, name in (("ckv", "kv", 256, k.ckv_rows, k.ckvt, "mla_ckv_g_2"),
                                                       ("cq", "q", 384, k.cq_rows, k.cqt, "mla_cq_g_2")):
                    for t in tiles_of(l, kind):
                        wait(k.proj_read, "mla", l, part, t)
                        xt = rows[:, t, 0:n]
                        then(v.tensor_tensor_reduce(out=k.xn[:, 0, 0:n], in0=xt, in1=xt, scale=1.0, scalar=0.0,
                                                    op0=ALU.mult, op1=ALU.add, accum_out=k.ss[:, 0:1]))
                        rstd(k.ss[:, 0:1], n, "latent", l, part, t)
                        v.tensor_scalar(xt, xt, k.ss[:, 0:1], None, ALU.mult)\
                            .then_inc(k.latent_normed.sem, k.latent_normed.step(l, part, t))
                        wait(k.latent_normed, l, part, t)
                for part, kind, n, rows, dst, name in (("ckv", "kv", 2, k.ckv_rows, k.ckvt, "mla_ckv_g_2"),
                                                       ("cq", "q", 3, k.cq_rows, k.cqt, "mla_cq_g_2")):
                    for t in tiles_of(l, kind):
                        wait(k.turned, part, l, t)
                        v.tensor_tensor(dst[:, :, P * t:P * t + P],
                                        k.bank_of[part, l, t][:, 0:P * n].rearrange("p (c t) -> p c t", c=n),
                                        col(name, n * l, n).unsqueeze(2).to_broadcast([P, n, P]), ALU.mult)\
                            .then_inc(k.latent_turned.sem, k.latent_turned.step(l, part, t))
            for n, t in enumerate(tiles_of(l, "kv")):
                head_norm(branch, "k", t)
                if branch != "mla" and n == 1:
                    low_parts((branch, l, "v", "s1"))
            if branch != "mla":
                low_parts((branch, l, "q", "s0"), (branch, l, "q", "s1"), ("z", l, b, "s0"))
            for n, t in enumerate(tiles_of(l, "q")):
                head_norm(branch, "q", t)
                if branch != "mla" and n == 0:
                    low_parts(("z", l, b, "s1"))

            todo = attention_units(l)
            vd = V_DIM[branch]

            def unit_max(n):
                t, u = todo[n]
                keys = 512 if t >= 2 else TOK
                bank = k.bank_of[branch, l, t, u]
                wait(k.scores_done, branch, l, t, u)
                v.tensor_reduce(k.nmax[:, n % 4:n % 4 + 1], bank[:, 0:keys], X_AXIS, ALU.max, negate=True)\
                    .then_inc(k.max_ready.sem, k.max_ready.step(branch, l, t, u))

            def unit_out(n):
                t, u = todo[n]
                wait(k.pv_done, branch, l, t, u)
                side = 0 if branch == "diff" else u % 2
                bank = k.bank_of["pv", branch, l, t, u][:, vd * side:vd * side + vd]
                rs = k.rsum[:, n % 2:n % 2 + 1]
                then(v.reciprocal(rs, k.psums[:, n % 4:n % 4 + 1]))
                if branch == "diff":
                    at = k.o[:, t, vd * (u // 2):vd * (u // 2) + vd]
                    if u % 2:
                        then(v.tensor_tensor(rs, rs, k.neg_lam, ALU.mult))
                        ins = v.scalar_tensor_tensor(out=at, in0=bank, scalar=rs, in1=at, op0=ALU.mult, op1=ALU.add)
                    else:
                        ins = v.tensor_scalar(at, bank, rs, None, ALU.mult)
                else:
                    ins = v.tensor_scalar(k.o[:, t, vd * u:vd * u + vd], bank, rs, None, ALU.mult)
                ins.then_inc(k.unit_out.sem, k.unit_out.step(branch, l, t, u))
                wait(k.unit_out, branch, l, t, u)

            for n in range(len(todo) + 2):
                if n < len(todo):
                    unit_max(n)
                if n >= 2:
                    unit_out(n - 2)
                if branch == "diff" and l + 1 < LAYERS and n - 2 in CONDITIONING_AT:
                    take_conditioning(l + 1, CONDITIONING_AT.index(n - 2))
            if branch == "diff" and l + 1 < LAYERS:
                finish_conditioning(l + 1)

            for t in tiles_of(l, "q"):
                o4 = k.o[:, t, :].rearrange("p (h d) -> p h d", h=4)
                if branch == "diff":
                    then(group_norm(o4, 4, P, k.xn[:, 0, :], "o", l, t))
                    then(v.tensor_tensor(o4, o4, row("diff_subln_g_2").unsqueeze(1).to_broadcast([P, 4, P]), ALU.mult))
                wait(k.z_read, l, b, t)
                v.tensor_tensor(k.o[:, t, :], k.o[:, t, :], k.sz[b][:, t, :], ALU.mult)\
                    .then_inc(k.branch_gated.sem, k.branch_gated.step(l, b, t))
            for n, (half, t) in enumerate([(half, t) for half in range(2) for t in tiles_of(l, "q")]):
                at = k.y[:, t, 512 * half:512 * half + 512]
                wait(k.gm_read, l, b, half, t)
                wait(k.gemm_done, "br", l, b, half, t)
                bank = k.bank_of["br", l, b, half, t]
                if b == 0:
                    ins = v.tensor_tensor(at, bank, k.sg[:, n % 2, :], ALU.mult)
                else:
                    then(v.tensor_tensor(k.sg[:, n % 2, :], bank, k.sg[:, n % 2, :], ALU.mult))
                    ins = v.tensor_tensor(at, at, k.sg[:, n % 2, :], ALU.add)
                ins.then_inc(k.merged.sem, k.merged.step(l, b, half, t))

        for t in tiles_of(l, "q"):
            for half in range(2):
                wait(k.y_turned, l, t, half)
                at = (slice(None), slice(4 * half, 4 * half + 4), slice(P * t, P * t + P))
                v.tensor_tensor(k.y_lo[at], k.bank_of["y", l, t, half].rearrange("p (c t) -> p c t", c=4),
                                k.y_hi[at].bitcast(F32), ALU.subtract).then_inc(k.y_split.sem, k.y_split.step(l, t, half))

        dve.wait_ge(k.gate_bias_loaded, 32 if l == 0 else 48)
        for n in (4, 5):
            for who in (["ctx", "x"] if l == 0 else ["x"]):
                wait(k.gemm_done, "gate", l, n, who)
                at = k.gates[:, 0 if who == "x" else 1, 512 * (n - 4):512 * (n - 4) + 512]
                v.tensor_tensor(at, at, k.bank_of["gate", l, n, who], ALU.add)\
                    .then_inc(k.gate_ready.sem, k.gate_ready.step(l, n, who))
        wait(k.gate_ready, l, 5, "x")
        for half in range(2):
            for t in tiles_of(l, "q"):
                wait(k.gemm_done, "out", l, half, t)
                wait(k.turned, "y", l, t, half)
                tmp = k.y[:, t, 512 * half:512 * half + 512]
                at = all_rows(t)[:, 512 * half:512 * half + 512]
                then(v.tensor_tensor(tmp, k.bank_of["out", l, half, t],
                                     k.gates[:, 0 if t >= 2 else 1, 512 * half:512 * half + 512], ALU.mult))
                v.tensor_tensor(at, at, tmp, ALU.add).then_inc(k.layer_done.sem, k.layer_done.step("x", l, t, half))
                if l + 1 < LAYERS and half == 1 and t < 2:
                    wait(k.layer_done, "x", l, t, half)
                    norm(("h", l + 1), t, all_rows(t))
        wait(k.layer_done, "x", l, 3, 1)



def gpsimd_program(pool, k):
    nc = k.nc
    g = nc.gpsimd

    def wait(signal, *key):
        pool.wait_ge(signal.sem, signal.at(*key))

    def then(ins):
        ins.then_inc(k.gpsimd_steps.sem, k.gpsimd_steps.step(k.gpsimd_steps.count))
        pool.wait_ge(k.gpsimd_steps.sem, k.gpsimd_steps.count)

    then(g.memset(k.minus_half, -0.5))

    def power(groups, *key):
        wait(k.mean_squares, *key)
        g.tensor_tensor(k.ss[:, 0:groups], k.ss[:, 0:groups], k.minus_half[:, 0:groups], ALU.pow)\
            .then_inc(k.rstd_ready.sem, k.rstd_ready.step(*key))

    for what in ("mixer", "mem"):
        for t in range(TT):
            power(1, what, t)
    wait(k.kk_ready)
    wait(k.mix_read, 3, 1)
    for n, size in enumerate(LEVELS):
        wait(k.level_exp, n)
        if n >= 2:
            wait(k.scores_done, "level", n - 2, 0 if n == 2 else 1)
        half = lambda ap, side: ap.rearrange("p (b two s) -> p b two s", two=2, s=size)[:, :, side, :]
        out = k.level[:, n % 2, :]
        g.tensor_tensor(half(out, 0), half(k.level_e, 0), half(k.kk, 0), ALU.mult)
        g.tensor_tensor(half(out, 1), half(k.level_e, 1), half(k.qq, 1), ALU.mult)\
            .then_inc(k.level_ready.sem, k.level_ready.step(n))
    for what in ("hgrn", "cross", "moe", "final"):
        for t in range(TT):
            power(HEADS1 if what == "hgrn" else 1, what, t)

    for l in range(LAYERS):
        def low_parts(*keys):
            for key in keys:
                slot, _ = k.landed[key]
                n = k.chunk_floats[key]
                wait(k.weights_high, *key)
                g.tensor_tensor(k.split_ring[:, slot, 0:n], k.pool6[:, slot * SLOT:slot * SLOT + n],
                                k.split_ring[:, slot, HALF:HALF + n].bitcast(F32), ALU.subtract)\
                    .then_inc(k.weights_split.sem, k.weights_split.step(*key))

        def split_tokens(t):
            wait(k.h_high, l, t)
            g.tensor_tensor(k.h_lo[:, :, P * t:P * t + P], k.h_new[:, t % 2], k.h_hi[:, :, P * t:P * t + P].bitcast(F32),
                            ALU.subtract).then_inc(k.h_split.sem, k.h_split.step(l, t))

        halves = lambda *key: [(*key, "s0"), (*key, "s1")]
        low_parts(("na", l, "k", "s0"))
        for t in range(3):
            power(1, ("h", l), t)
        low_parts(("na", l, "k", "s1"))
        split_tokens(0)
        power(1, ("h", l), 3)
        for t in range(1, 4):
            split_tokens(t)
        low_parts(("na", l, "v", "s0"))
        pool.wait_ge(k.bias_loaded, 16 * 32 * (l + 1))
        mask = k.colmask.unsqueeze(1).to_broadcast([P, 32, 64])
        for t in range(TT):
            rows = k.bias[:, t, :, :].rearrange("p h (a b) -> p (h a) b", b=64)
            ins = g.tensor_tensor(rows, rows, mask, ALU.add)
        ins.then_inc(k.bias_ready.sem, k.bias_ready.step(l))
        pool.wait_ge(k.rowv_loaded, 16 * (l + 1))

        def finish_heads(branch, part, t):
            dim = QK_DIM[branch]
            at, n = ROWV["%s_%s_g_2" % (branch, part)]
            power(8, branch, l, part, t)
            wait(k.heads_normed, branch, l, part, t)
            rows = k.head_rows[:, t, 0:8 * dim].rearrange("p (h d) -> p h d", h=8)
            ins = g.tensor_tensor(rows, rows, k.rowv[:, at:at + n].unsqueeze(1).to_broadcast([P, 8, dim]), ALU.mult)
            if branch != "na" and t >= 2:
                then(ins)
                half = ROPE[branch] // 2
                x1, x2 = rows[:, :, dim - 2 * half:dim - half], rows[:, :, dim - half:dim]
                cs, sn = (getter[:, (t - 2) * half:(t - 1) * half].unsqueeze(1).to_broadcast([P, 8, half])
                          for getter in ((k.cos_mla, k.sin_mla) if branch == "mla" else (k.cos_diff, k.sin_diff)))
                tmp = k.rope_tmp[:, 0:4 * 8 * half].rearrange("p (n h d) -> p n h d", n=4, h=8)
                for i, (a, f) in enumerate([(x1, cs), (x2, sn), (x2, cs), (x1, sn)]):
                    ins = g.tensor_tensor(tmp[:, i], a, f, ALU.mult)
                then(ins)
                g.tensor_tensor(x1, tmp[:, 0], tmp[:, 1], ALU.subtract)
                ins = g.tensor_tensor(x2, tmp[:, 2], tmp[:, 3], ALU.add)
            ins.then_inc(k.heads_ready.sem, k.heads_ready.step(branch, l, part, t))
            wait(k.heads_ready, branch, l, part, t)

        for b, branch in enumerate(BRANCHES):
            if branch == "mla":
                low_parts(("mla", l, "cq", "s1"), ("z", l, b, "s0"))
                for part, kind in (("ckv", "kv"), ("cq", "q")):
                    for t in tiles_of(l, kind):
                        power(1, "latent", l, part, t)
                    if part == "ckv":
                        low_parts(("z", l, b, "s1"))
            for t in tiles_of(l, "kv"):
                finish_heads(branch, "k", t)
            for t in tiles_of(l, "q"):
                finish_heads(branch, "q", t)
            low_parts(*halves("gm", l, b, 0), ("gm", l, b, 1, "s0"))
            if branch == "diff":
                for t in tiles_of(l, "q"):
                    power(4, "o", l, t)
            low_parts(("gm", l, b, 1, "s1"))
            if branch == "na":
                low_parts(*halves("mla", l, "ckv"), ("mla", l, "cq", "s0"))
            elif branch == "mla":
                low_parts(*halves("diff", l, "k"), ("diff", l, "v", "s0"))
        low_parts(*halves("out", l, 0), *halves("out", l, 1))



def build_program(nc, w, book):
    with ExitStack() as stack:
        def sb(name, cols):
            return stack.enter_context(nc.sbuf_tensor(name, [P, cols], F32))[:, :]

        def sem(name):
            return stack.enter_context(nc.semaphore(name))

        def signal(name):
            return Signal(sem(name), name, book)

        split = lambda ap, a: ap.rearrange("p (a b) -> p a b", a=a)
        k = Program()
        k.nc, k.w, k.landed, k.loads, k.bank_of = nc, w, {}, [0] * MOE_RING, book["banks"]
        k.chunk_floats = {}
        k.all_banks = [stack.enter_context(nc.psum_tensor("bank%d" % n, [P, 512], F32))[:, :] for n in range(8)]
        k.banks = dict(zip(["G0", "G1", "T0", "T1", "S0", "S1", "O0", "O1"], k.all_banks))

        aligned_base = lambda: (int(nc.sbuf_base) + 31) // 32 * 32
        ring_at = aligned_base()
        k.pool6 = sb("weights_qt_kt", MOE_RING * SLOT)
        qt, kt = k.pool6[:, RING * SLOT:(RING + 1) * SLOT], k.pool6[:, (RING + 1) * SLOT:]
        k.x_rows = split(sb("x_rows", TT * D), TT)
        k.ctx_rows = split(sb("ctx_rows", TT * D), TT)
        ht_at = aligned_base()
        k.ht = split(sb("ht", KT_D * 512), KT_D)
        k.split_ring = nc.alloc_sbuf_tensor_at("split_ring", [P, RING2 * SLOT], F32R, offset=ring_at)[:, :]
        k.split_ring = split(k.split_ring, RING2)
        k.h_lo = split(nc.alloc_sbuf_tensor_at("h_lo", [P, SLOT], F32R, offset=ring_at + 4 * RING2 * SLOT)[:, :], KT_D)
        k.y_hi = split(nc.alloc_sbuf_tensor_at("y_hi", [P, SLOT], F32R, offset=ring_at + 4 * RING * SLOT)[:, :], KT_D)
        k.y_lo = split(nc.alloc_sbuf_tensor_at("y_lo", [P, SLOT], F32R, offset=ring_at + 4 * (RING + 1) * SLOT)[:, :], KT_D)
        k.h_hi = split(nc.alloc_sbuf_tensor_at("h_hi", [P, KT_D * 512], F32R, offset=ht_at)[:, :], KT_D)
        k.v_flat = sb("v", 2048)
        o_flat = sb("o", 2048)
        head = sb("head_rows", 3072)
        y_flat = sb("y", 4096)
        aux = sb("aux", 4096)
        pp = sb("probs", 2048)
        k.const = sb("const", N_CONST)
        k.cols = sb("cols", 2 * P)
        k.rowv = sb("rowv", N_ROWV)
        k.router_w = split(sb("router_w", 8 * 20), 8)
        k.router_b = sb("router_b", 20)
        small = sb("small", 336)
        k.sc = split(sb("sc", 8 * 32), 8)
        k.ss, k.nmax, k.psums, k.rsum = small[:, 16:24], small[:, 24:28], small[:, 28:32], small[:, 32:34]
        k.lam2, k.neg_lam = small[:, 34:36], small[:, 36:37]
        k.lb, k.lb_raw, k.omlb = small[:, 40:44], small[:, 44:48], small[:, 48:52]
        k.gain, k.shift = split(small[:, 56:72], 2), split(small[:, 72:88], 2)
        k.combine = split(small[:, 88:120], 2)
        k.route_ge, k.route_ee = small[:, 120:128], small[:, 128:136]
        k.route_small, k.route_pick = small[:, 136:160], small[:, 160:192]
        k.lam_products, k.minus_half = small[:, 192:256], small[:, 256:264]
        k.selected, k.places, k.longest = split(small[:, 264:296], 2), small[:, 296:328], small[:, 328:329]
        constant = lambda name: k.const[:, CONST[name][0]:sum(CONST[name])]
        k.ident, k.reverse, k.colmask, k.rank = (constant(name) for name in ("ident", "reverse", "colmask", "rank"))
        k.before, k.iota, k.pick_x, k.pick_ctx = (constant(name) for name in ("before", "iota", "pick_x", "pick_ctx"))
        k.cos_diff, k.sin_diff, k.cos_mla, k.sin_mla = (constant(name) for name in ("cos_diff", "sin_diff", "cos_mla", "sin_mla"))
        k.qt, k.kt = split(qt, 8), split(kt, 8)
        k.branch_w = qt.rearrange("p (h k n) -> p h k n", h=2, k=4)
        k.v, k.o, k.y = split(k.v_flat, 4), split(o_flat, 4), split(y_flat, 4)
        k.head_rows = split(head, 4)
        k.h_new = y_flat[:, 0:2048].rearrange("p (t c n) -> p t c n", t=2, c=KT_D)
        k.cq_rows, k.ckv_rows = split(k.v_flat[:, 0:1536], 4), split(o_flat[:, 0:1152], 4)
        k.probs, k.probs_t = split(pp[:, 0:1024], 2), split(pp[:, 1024:2048], 2)
        k.xn = split(pp, 2)
        k.rope_tmp = pp[:, 1024:2048]
        k.bias = aux.rearrange("p (t h n) -> p t h n", t=TT, h=8)
        k.ogt, k.sg = split(aux[:, 0:2048], 4), split(aux[:, 3072:4096], 2)
        k.sz = [split(y_flat[:, 0:2048], 4), split(aux[:, 2048:4096], 4), split(aux[:, 2048:4096], 4)]
        k.cqt, k.ckvt = split(aux[:, 0:1536], 3), split(qt[:, 0:1024], 2)
        k.gates = split(k.v_flat, 2)
        k.ada_rows = split(head[:, 0:1024], 2)
        k.qq, k.kk, k.b, k.lf = (qt[:, 1024 * n:1024 * n + 1024] for n in range(4))
        k.level = split(kt[:, 0:2048], 2)
        k.level_d, k.level_e = kt[:, 2048:3072], kt[:, 3072:4096]
        k.near_scores, k.far_scores = y_flat[:, 0:1024], y_flat[:, 1024:1536]
        k.conv_in = split(y_flat[:, 1536:1536 + 4 * (TOK + 2)], 4)
        k.ones = y_flat[:, 2688:2816]
        k.conv, k.silu_g, k.cc = split(head[:, 0:1024], 4), head[:, 1024:2048], head[:, 2048:3072]
        k.t_out, k.masks = split(aux[:, 0:2048], 8), aux[:, 2048:3072]
        k.col_rows = split(aux[:, 3072:3328], 2)
        k.cross_q, k.cross_k, k.cross_v = split(qt[:, 0:2048], 8), split(kt[:, 0:2048], 8), split(y_flat[:, 0:2048], 2)
        k.hidden, k.moe_g = split(aux[:, 0:1024], 4), split(aux[:, 1024:2048], 2)
        k.route = aux[:, 3328:3968]
        k.tokens = split(head[:, 0:1024], KT_D)
        k.down_rows = head[:, 1024:2048]
        k.lists = head[:, 2048:2304].rearrange("p (t j n) -> p t j n", t=TT, j=2)
        k.weighted = head[:, 2304:2560].rearrange("p (t j n) -> p t j n", t=TT, j=2)
        k.weighted_t, k.pair_g = head[:, 2560:2816], y_flat[:, 1024:1536]
        k.pair_h, k.pair_ht = y_flat[:, 0:512], split(y_flat[:, 512:1024], 4)
        k.crowded = stack.enter_context(nc.sbuf_tensor("crowded", [P, 1], mybir.dt.int32))[:, :]

        k.x_loaded = sem("x_loaded")
        k.small_loaded = sem("small_loaded")
        k.masks_loaded = sem("masks_loaded")
        k.mem_loaded = sem("mem_loaded")
        k.router_loaded = sem("router_loaded")
        k.ctx_loaded = sem("ctx_loaded")
        k.rowv_loaded = sem("rowv_loaded")
        k.bias_loaded = sem("bias_loaded")
        k.gate_bias_loaded = sem("gate_bias_loaded")
        k.branch_w_loaded = [sem("branch_w_loaded%d" % half) for half in range(2)]
        k.final_norm_loaded = sem("final_norm_loaded")
        k.stored = sem("stored")
        k.slot_loaded = [sem("slot_loaded%d" % n) for n in range(MOE_RING)]
        k.moe_gate = sem("moe_gate")
        k.moe_silu = sem("moe_silu")
        k.moe_up = sem("moe_up")
        k.moe_hidden = sem("moe_hidden")
        k.moe_down = sem("moe_down")
        k.moe_added = sem("moe_added")
        k.pair_lists = sem("pair_lists")
        k.pair_gathered = sem("pair_gathered")
        k.pair_tokens = sem("pair_tokens")
        k.pair_turned = sem("pair_turned")
        k.pair_weights = sem("pair_weights")
        k.pair_gate = sem("pair_gate")
        k.pair_silu = sem("pair_silu")
        k.pair_up = sem("pair_up")
        k.pair_hidden = sem("pair_hidden")
        k.pair_h_turned = sem("pair_h_turned")
        k.pair_h_ready = sem("pair_h_ready")
        k.pair_down = sem("pair_down")
        k.pair_rows = sem("pair_rows")
        k.pair_spread = sem("pair_spread")
        k.pair_summed = sem("pair_summed")
        k.gemm_done = signal("gemm_done")
        k.turned = signal("turned")
        k.scores_done = signal("scores_done")
        k.pv_done = signal("pv_done")
        k.silu_c = signal("silu_c")
        k.weights_high = signal("weights_high")
        k.h_high = signal("h_high")
        k.ada_rows_ready = signal("ada_rows_ready")
        k.lb_ready = signal("lb_ready")
        k.mix_read = signal("mix_read")
        k.logf_ready = signal("logf_ready")
        k.level_exp = signal("level_exp")
        k.cross_read = signal("cross_read")
        k.probs_ready = signal("probs_ready")
        k.probs_turned = signal("probs_turned")
        k.cross_out = signal("cross_out")
        k.route_exp = signal("route_exp")
        k.lam_exp = signal("lam_exp")
        k.proj_read = signal("proj_read")
        k.heads_turned = signal("heads_turned")
        k.z_read = signal("z_read")
        k.branch_turned = signal("branch_turned")
        k.gm_read = signal("gm_read")
        k.y_turned = signal("y_turned")
        k.cols_ready = signal("cols_ready")
        k.lb_diff = signal("lb_diff")
        k.norm_rows = signal("norm_rows")
        k.ht_ready = signal("ht_ready")
        k.f_ready = signal("f_ready")
        k.kk_ready = signal("kk_ready")
        k.level_diff = signal("level_diff")
        k.scores_taken = signal("scores_taken")
        k.conv_read = signal("conv_read")
        k.mean_squares = signal("mean_squares")
        k.hgrn_out = signal("hgrn_out")
        k.hgrn_normed = signal("hgrn_normed")
        k.yt_ready = signal("yt_ready")
        k.x_added = signal("x_added")
        k.max_ready = signal("max_ready")
        k.probs_scaled = signal("probs_scaled")
        k.routed = signal("routed")
        k.picked = signal("picked")
        k.places_read = signal("places_read")
        k.crowded_ready = signal("crowded_ready")
        k.route_diff = signal("route_diff")
        k.lam_dots = signal("lam_dots")
        k.ada_ready = signal("ada_ready")
        k.heads_normed = signal("heads_normed")
        k.weights_split_dve = signal("weights_split_dve")
        k.latent_normed = signal("latent_normed")
        k.latent_turned = signal("latent_turned")
        k.unit_out = signal("unit_out")
        k.branch_gated = signal("branch_gated")
        k.merged = signal("merged")
        k.y_split = signal("y_split")
        k.ada_taken = signal("ada_taken")
        k.gate_ready = signal("gate_ready")
        k.layer_done = signal("layer_done")
        k.vector_steps = signal("vector_steps")
        k.weights_split = signal("weights_split")
        k.h_split = signal("h_split")
        k.level_ready = signal("level_ready")
        k.rstd_ready = signal("rstd_ready")
        k.bias_ready = signal("bias_ready")
        k.heads_ready = signal("heads_ready")
        k.gpsimd_steps = signal("gpsimd_steps")

        with nc.Block() as block:
            @block.sync
            def _(sp):
                load_program(sp, k)

            @block.tensor
            def _(pe):
                tensor_program(pe, k)

            @block.scalar
            def _(act):
                scalar_program(act, k)

            @block.vector
            def _(dve):
                vector_program(dve, k)

            @block.gpsimd
            def _(pool):
                gpsimd_program(pool, k)



INPUTS = ["x", "mem", "w_in", "w_out", "w_q", "w_kv", "w_o", "w_group", "w_expert", "b_group", "b_expert", "final_norm",
          "ctx_2", "w_ada_2", "b_ada_2", "w_in_2", "w_uq_2", "w_ukv_2", "w_br_2", "w_out_2"]
FLAT = {"w_gate": "w_gate_flat", "w_up": "w_up_flat", "w_down": "w_down_flat"}


def shape_constants():
    import numpy as np
    const = np.zeros((P, N_CONST), np.float32)

    def put(name, value):
        at, n = CONST[name]
        const[:, at:at + n] = value
    put("ident", np.eye(P))
    grid_w, win = 64, 16
    put("reverse", np.kron(np.eye(2), np.eye(grid_w)[::-1]))
    q = grid_w - 1 - np.arange(P) % grid_w
    start = np.clip(q - win // 2, 0, grid_w - win)
    key = np.arange(grid_w)
    inside = (key[None] >= start[:, None]) & (key[None] < start[:, None] + win)
    put("colmask", np.where(inside, 0.0, -1e30))
    token = np.arange(TOK)
    for name, rot in (("diff", ROPE["diff"]), ("mla", ROPE["mla"])):
        n = rot // 4
        inv = (np.float32(10000.0) ** (-np.arange(n, dtype=np.float32) / np.float32(n))).astype(np.float32)
        row, column = (token // grid_w).astype(np.float32), (token % grid_w).astype(np.float32)
        ang = np.concatenate([row[:, None] * inv, column[:, None] * inv], axis=-1).astype(np.float32)
        for what, f in (("cos", np.cos), ("sin", np.sin)):
            put(what + "_" + name, f(ang).astype(np.float32).reshape(TT, P, rot // 2).transpose(1, 0, 2).reshape(P, -1))
    put("rank", [4.0, 3.0, 2.0, 1.0])
    put("before", np.triu(np.ones((P, P)), 1))
    put("iota", np.arange(CAP))
    put("pick_x", np.arange(P)[:, None] % 32 == 0)
    put("pick_ctx", np.arange(P)[:, None] % 32 == 1)
    s, t = np.arange(P)[:, None], np.arange(P)[None]
    masks = [(s // (2 * n) == t // (2 * n)) & (s % (2 * n) < n) & (t % (2 * n) >= n) for n in LEVELS[1:]] + [s == t]
    return const, np.concatenate([m.astype(np.float32) for m in masks], axis=1)


def kernel(**inputs):
    import numpy as np
    import concourse.bacc as bacc
    from concourse.bass_utils import run_bass_kernel_spmd

    arrays = {name: np.ascontiguousarray(inputs[name]) for name in INPUTS}
    for name, flat in FLAT.items():
        a = np.ascontiguousarray(inputs[name])
        arrays[flat] = a.reshape(-1, a.shape[-1])
    col_vecs = np.zeros((2 * P, P), np.float32)
    for name, at in COLS.items():
        rows = np.asarray(inputs[name]).reshape(-1, P)
        col_vecs[at:at + rows.shape[0]] = rows
    arrays["col_vecs"] = col_vecs
    arrays["row_vecs"] = np.concatenate([np.asarray(inputs[name]).reshape(LAYERS, -1) for name in ROWV], axis=1)
    rpb = np.zeros((LAYERS, 8, 15, 127), np.float32)
    rpb[:, :, :, 48:79] = np.asarray(inputs["na_rpb_2"])
    arrays["rpb"] = rpb
    arrays["const"], arrays["masks"] = shape_constants()

    book = {"before": None, "now": {}, "banks": {}}
    for last in (False, True):
        nc = bacc.Bacc("TRN2", target_bir_lowering=False, num_devices=1)
        w = {}
        for name, a in arrays.items():
            w[name] = nc.dram_tensor("in_" + name, a.shape, F32, kind="ExternalInput").ap()
        w["out"] = nc.dram_tensor("out_0", (1, TOK, D), F32, kind="ExternalOutput").ap()
        build_program(nc, w, book)
        if not last:
            book = {"before": book["now"], "now": {}, "banks": {}}
    r = run_bass_kernel_spmd(nc, [{"in_" + name: a for name, a in arrays.items()}], core_ids=[0])
    return r.results[0]["out_0"]
```
